# Optimizing a Trainium2 kernel written in Bass

```python
import jax
import jax.numpy as jnp
from jax import lax
import numpy as np
import jax, jax.numpy as jnp

D_MODEL = 1024
BATCH = 1
SEQ = 512
DEPTH = 2

NORM_EPS = 1e-6
ROPE_BASE = 10000.0

RW_HEADS = 4
RW_HEAD_DIM = 64
RW_DIM = RW_HEADS * RW_HEAD_DIM
RW_DECAY_RANK = 32
RW_A_RANK = 32
RW_V_RANK = 32
RW_GATE_RANK = 64
RW_GN_EPS = 64e-5
RW_IN = 3 * RW_DIM + RW_DECAY_RANK + RW_A_RANK + RW_GATE_RANK

RET_HEADS = 4
RET_HEAD_DIM = 64
RET_DIM = RET_HEADS * RET_HEAD_DIM
RET_CHUNK = 128
RET_IN = 4 * RET_DIM

MLA_HEADS = 8
MLA_NOPE = 64
MLA_ROPE = 32
MLA_V = 64
MLA_Q_RANK = 384
MLA_KV_RANK = 256
MLA_DIM = MLA_HEADS * MLA_V
MLA_IN = MLA_Q_RANK + MLA_KV_RANK + MLA_ROPE
ATTN_BLOCK = 128

IN_DIM = RW_IN + RET_IN + MLA_IN
MIX_DIM = RW_DIM + RET_DIM + MLA_DIM
D_FF = -(-(8 * D_MODEL) // (3 * 256)) * 256


def rms_norm(x, g):
    xf = x.astype(jnp.float32)
    y = xf * lax.rsqrt(jnp.mean(xf * xf, axis=-1, keepdims=True) + NORM_EPS)
    return (y * g.astype(jnp.float32)).astype(x.dtype)

def rope(x, positions):
    d = x.shape[-1]
    inv = ROPE_BASE ** (-jnp.arange(0, d, 2, dtype=jnp.float32) / d)
    ang = positions.astype(jnp.float32)[..., None] * inv
    ang = ang.reshape(ang.shape[:2] + (1,) * (x.ndim - 3) + ang.shape[-1:])
    cos, sin = jnp.cos(ang), jnp.sin(ang)
    xf = x.astype(jnp.float32)
    x1, x2 = xf[..., : d // 2], xf[..., d // 2:]
    return jnp.concatenate([x1 * cos - x2 * sin, x2 * cos + x1 * sin], axis=-1).astype(x.dtype)

def token_shift(p):
    return jnp.pad(p, ((0, 0), (1, 0), (0, 0)))[:, :-1]

def rwkv7_mixer(p, mu, w0, w2, a0, a2, g2, k_k, k_a, r_k, gn_w, gn_b, v_first, v_res):
    B, S, _ = p.shape
    p = p.astype(jnp.float32)
    ps = p + (token_shift(p) - p) * mu
    o1, o2, o3 = RW_DIM, 2 * RW_DIM, 3 * RW_DIM
    o4, o5 = o3 + RW_DECAY_RANK, o3 + RW_DECAY_RANK + RW_A_RANK
    r, k, v = ps[..., :o1], ps[..., o1:o2], ps[..., o2:o3]
    wd, ad, gd = ps[..., o3:o4], ps[..., o4:o5], ps[..., o5:]
    w = -jax.nn.softplus(-(w0 + jnp.tanh(wd) @ w2)) - 0.5
    decay = jnp.exp(-jnp.exp(w))
    a = jax.nn.sigmoid(a0 + ad @ a2)
    g = jax.nn.sigmoid(gd) @ g2
    if v_res is None:
        v_first = v
    else:
        v0, v1, v2 = v_res
        v = v + (v_first - v) * jax.nn.sigmoid(v0 + (v @ v1) @ v2)
    heads = lambda t: t.reshape(B, S, RW_HEADS, RW_HEAD_DIM)
    kk = heads(k * k_k)
    kk = kk * lax.rsqrt(jnp.maximum(jnp.sum(kk * kk, axis=-1, keepdims=True), 1e-24))
    k = k * (1.0 + (a - 1.0) * k_a)
    r_h, k_h, v_h, w_h, a_h = heads(r), heads(k), heads(v), heads(decay), heads(a)

    def step(state, inp):
        rt, kt, vt, wt, kkt, at = inp
        sa = jnp.einsum('bhvk,bhk->bhv', state, -kkt)
        state = (state * wt[:, :, None, :] + sa[..., None] * (kkt * at)[:, :, None, :]
                 + vt[..., None] * kt[:, :, None, :])
        return state, jnp.einsum('bhvk,bhk->bhv', state, rt)

    xs = tuple(jnp.moveaxis(t, 1, 0) for t in (r_h, k_h, v_h, w_h, kk, a_h))
    s0 = jnp.zeros((B, RW_HEADS, RW_HEAD_DIM, RW_HEAD_DIM), jnp.float32)
    _, y = lax.scan(step, s0, xs)
    y = jnp.moveaxis(y, 0, 1)
    mean = jnp.mean(y, axis=-1, keepdims=True)
    var = jnp.mean(jnp.square(y - mean), axis=-1, keepdims=True)
    y = ((y - mean) * lax.rsqrt(var + RW_GN_EPS)).reshape(B, S, RW_DIM) * gn_w + gn_b
    bonus = jnp.sum(r_h * k_h * r_k, axis=-1, keepdims=True) * v_h
    y = (y + bonus.reshape(B, S, RW_DIM)) * g
    return y, v_first

def retention_mixer(p, positions):
    B, S, _ = p.shape
    p = p.astype(jnp.float32)
    q, k, v, g = jnp.split(p, 4, axis=-1)
    heads = lambda t: t.reshape(B, S, RET_HEADS, RET_HEAD_DIM)
    q = rope(heads(q), positions)
    k = rope(heads(k), positions) * (RET_HEAD_DIM ** -0.5)
    v = heads(v)
    log_gamma = jnp.log(1.0 - 2.0 ** (-5.0 - jnp.arange(RET_HEADS, dtype=jnp.float32)))
    n_chunks = S // RET_CHUNK
    chunk = lambda t: t.reshape(B, n_chunks, RET_CHUNK, RET_HEADS, RET_HEAD_DIM).transpose(0, 3, 1, 2, 4)
    qc, kc, vc = chunk(q), chunk(k), chunk(v)
    idx = jnp.arange(RET_CHUNK, dtype=jnp.float32)
    diff = idx[:, None] - idx[None, :]
    dmask = jnp.where(diff >= 0, jnp.exp(log_gamma[:, None, None] * jnp.maximum(diff, 0.0)), 0.0)
    inner = jnp.einsum('bhnqd,bhnkd->bhnqk', qc, kc) * dmask[:, None]
    inner = jnp.einsum('bhnqk,bhnkd->bhnqd', inner, vc)
    q_dec = jnp.exp(log_gamma[:, None] * (idx + 1.0))
    k_dec = jnp.exp(log_gamma[:, None] * (RET_CHUNK - 1.0 - idx))
    chunk_dec = jnp.exp(log_gamma * RET_CHUNK)
    kv_chunk = jnp.einsum('bhnkd,bhnke->nbhde', kc * k_dec[:, None, :, None], vc)

    def step(R, kv_i):
        return R * chunk_dec[None, :, None, None] + kv_i, R

    R0 = jnp.zeros((B, RET_HEADS, RET_HEAD_DIM, RET_HEAD_DIM), jnp.float32)
    _, R_prev = lax.scan(step, R0, kv_chunk)
    cross = jnp.einsum('bhnqd,nbhde->bhnqe', qc * q_dec[:, None, :, None], R_prev)
    y = (inner + cross).transpose(0, 2, 3, 1, 4).reshape(B, S, RET_HEADS, RET_HEAD_DIM)
    y = y * lax.rsqrt(jnp.mean(y * y, axis=-1, keepdims=True) + NORM_EPS)
    return jax.nn.silu(g) * y.reshape(B, S, RET_DIM)

def mla_mixer(p, positions, q_norm, kv_norm, w_q_up, w_kv_up):
    B, S, _ = p.shape
    q_lat = p[..., :MLA_Q_RANK]
    kv_lat = p[..., MLA_Q_RANK:MLA_Q_RANK + MLA_KV_RANK]
    k_rope = rope(p[..., MLA_Q_RANK + MLA_KV_RANK:], positions)
    q = (rms_norm(q_lat, q_norm) @ w_q_up).reshape(B, S, MLA_HEADS, MLA_NOPE + MLA_ROPE)
    q_nope, q_rope = q[..., :MLA_NOPE], rope(q[..., MLA_NOPE:], positions)
    kv = (rms_norm(kv_lat, kv_norm) @ w_kv_up).reshape(B, S, MLA_HEADS, MLA_NOPE + MLA_V)
    k_nope, v = kv[..., :MLA_NOPE], kv[..., MLA_NOPE:]
    scale = (MLA_NOPE + MLA_ROPE) ** -0.5
    n_blocks = S // ATTN_BLOCK
    blk = lambda t: t.reshape(B, n_blocks, ATTN_BLOCK, MLA_HEADS, t.shape[-1]).transpose(1, 0, 3, 2, 4)
    qn_b, qr_b = blk(q_nope), blk(q_rope)
    key_idx = jnp.arange(S)

    def attend(args):
        qn, qr, i = args
        s = (jnp.einsum('bhqd,bkhd->bhqk', qn, k_nope)
             + jnp.einsum('bhqr,bkr->bhqk', qr, k_rope)).astype(jnp.float32) * scale
        q_idx = i * ATTN_BLOCK + jnp.arange(ATTN_BLOCK)
        s = jnp.where(key_idx[None, :] <= q_idx[:, None], s, -jnp.inf)
        pr = jax.nn.softmax(s, axis=-1).astype(v.dtype)
        return jnp.einsum('bhqk,bkhd->bqhd', pr, v)

    o = lax.map(attend, (qn_b, qr_b, jnp.arange(n_blocks)))
    return o.transpose(1, 0, 2, 3, 4).reshape(B, S, MLA_DIM)

def first_inputs(seed: int = 0) -> dict:
    key = jax.random.key(seed)
    keys = jax.random.split(key, 32)
    nrm = lambda i, shape, scale: scale * jax.random.normal(keys[i], shape, jnp.float32)
    L = DEPTH
    ch = jnp.linspace(0.0, 1.0, RW_DIM, dtype=jnp.float32)
    return {
        'x': nrm(0, (BATCH, SEQ, D_MODEL), 1.0),
        'positions': jnp.broadcast_to(jnp.arange(SEQ, dtype=jnp.int32), (BATCH, SEQ)),
        'attn_norm': 1.0 + nrm(1, (L, D_MODEL), 0.05),
        'w_in': nrm(2, (L, D_MODEL, IN_DIM), D_MODEL ** -0.5),
        'w_out': nrm(3, (L, MIX_DIM, D_MODEL), MIX_DIM ** -0.5),
        'rw_mu': jax.random.uniform(keys[4], (L, RW_IN), jnp.float32),
        'rw_w0': -6.0 + 5.0 * ch ** 0.85 + nrm(5, (L, RW_DIM), 0.1),
        'rw_w2': nrm(6, (L, RW_DECAY_RANK, RW_DIM), 0.5 * RW_DECAY_RANK ** -0.5),
        'rw_a0': nrm(7, (L, RW_DIM), 0.1),
        'rw_a2': nrm(8, (L, RW_A_RANK, RW_DIM), RW_A_RANK ** -0.5),
        'rw_g2': nrm(9, (L, RW_GATE_RANK, RW_DIM), RW_GATE_RANK ** -0.5),
        'rw_k_k': 0.85 + nrm(10, (L, RW_DIM), 0.05),
        'rw_k_a': 1.0 + nrm(11, (L, RW_DIM), 0.05),
        'rw_r_k': nrm(12, (L, RW_HEADS, RW_HEAD_DIM), 0.1),
        'rw_gn_w': 1.0 + nrm(13, (L, RW_DIM), 0.05),
        'rw_gn_b': nrm(14, (L, RW_DIM), 0.01),
        'rw_v0': 1.0 + nrm(15, (L - 1, RW_DIM), 0.1),
        'rw_v1': nrm(16, (L - 1, RW_DIM, RW_V_RANK), RW_DIM ** -0.5),
        'rw_v2': nrm(17, (L - 1, RW_V_RANK, RW_DIM), 0.5 * RW_V_RANK ** -0.5),
        'mla_q_norm': 1.0 + nrm(18, (L, MLA_Q_RANK), 0.05),
        'mla_kv_norm': 1.0 + nrm(19, (L, MLA_KV_RANK), 0.05),
        'mla_w_q_up': nrm(20, (L, MLA_Q_RANK, MLA_HEADS * (MLA_NOPE + MLA_ROPE)), MLA_Q_RANK ** -0.5),
        'mla_w_kv_up': nrm(21, (L, MLA_KV_RANK, MLA_HEADS * (MLA_NOPE + MLA_V)), MLA_KV_RANK ** -0.5),
        'ffn_norm': 1.0 + nrm(22, (L, D_MODEL), 0.05),
        'w_gate_up': nrm(23, (L, D_MODEL, 2 * D_FF), D_MODEL ** -0.5),
        'w_down': nrm(24, (L, D_FF, D_MODEL), D_FF ** -0.5),
        'final_norm': 1.0 + nrm(25, (D_MODEL,), 0.05),
    }

def first_block(x, positions, attn_norm, w_in, w_out, rw_mu, rw_w0, rw_w2, rw_a0, rw_a2, rw_g2,
              rw_k_k, rw_k_a, rw_r_k, rw_gn_w, rw_gn_b, rw_v0, rw_v1, rw_v2, mla_q_norm, mla_kv_norm,
              mla_w_q_up, mla_w_kv_up, ffn_norm, w_gate_up, w_down, final_norm):
    h = x
    v_first = None
    for l in range(DEPTH):
        hn = rms_norm(h, attn_norm[l])
        proj = hn @ w_in[l]
        p_a = proj[..., :RW_IN]
        p_b = proj[..., RW_IN:RW_IN + RET_IN]
        p_c = proj[..., RW_IN + RET_IN:]
        v_res = None if l == 0 else (rw_v0[l - 1], rw_v1[l - 1], rw_v2[l - 1])
        y_a, v_first = rwkv7_mixer(p_a, rw_mu[l], rw_w0[l], rw_w2[l], rw_a0[l], rw_a2[l], rw_g2[l],
                                   rw_k_k[l], rw_k_a[l], rw_r_k[l], rw_gn_w[l], rw_gn_b[l], v_first, v_res)
        y_b = retention_mixer(p_b, positions)
        y_c = mla_mixer(p_c, positions, mla_q_norm[l], mla_kv_norm[l], mla_w_q_up[l], mla_w_kv_up[l])
        mix = jnp.concatenate([y_a.astype(h.dtype), y_b.astype(h.dtype), y_c.astype(h.dtype)], axis=-1)
        h = h + mix @ w_out[l]
        hn = rms_norm(h, ffn_norm[l])
        gu = hn @ w_gate_up[l]
        h = h + (jax.nn.silu(gu[..., :D_FF]) * gu[..., D_FF:]) @ w_down[l]
    return rms_norm(h, final_norm)


N_EVEN = (DEPTH + 1) // 2
N_ODD = DEPTH // 2

RG_WIDTH = D_MODEL
RG_HEADS = 8
RG_HEAD_DIM = RG_WIDTH // RG_HEADS
RG_CONV = 4
RG_C = 8.0
RG_CONV_LEFT = 2
SC_WIDTH = D_MODEL
SC_CONV = 3
SC_CONV_LEFT = 1
EVEN_IN = 2 * RG_WIDTH + 4 * SC_WIDTH
EVEN_MIX = RG_WIDTH + SC_WIDTH
GLA_HEADS = 4
GLA_KEY = D_MODEL // 2
GLA_VAL = D_MODEL
GLA_DK = GLA_KEY // GLA_HEADS
GLA_DV = GLA_VAL // GLA_HEADS
GLA_RANK = 16
GLA_NORMALIZER = 16.0
GLA_CHUNK = 64
ODD_IN = 2 * GLA_KEY + 2 * GLA_VAL + 2 * GLA_RANK


def rmsnorm(x, g):
    xf = x.astype(jnp.float32)
    y = xf * lax.rsqrt(jnp.mean(xf * xf, axis=-1, keepdims=True) + NORM_EPS)
    return (y * g.astype(jnp.float32)).astype(x.dtype)

def centred_dwconv(u, w, left):
    seq = u.shape[1]
    width = w.shape[0]
    up = jnp.pad(u, ((0, 0), (left, width - 1 - left), (0, 0)))
    out = up[:, 0:seq] * w[0]
    for k in range(1, width):
        out = out + up[:, k:k + seq] * w[k]
    return out

def rg_lru(u, gate_w, gate_b, lam, reverse):
    bsz, seq, width = u.shape
    uf = u.astype(jnp.float32)
    uh = uf.reshape(bsz, seq, RG_HEADS, RG_HEAD_DIM)
    gates = jax.nn.sigmoid(
        jnp.einsum('bshi,ghij->gbshj', uh, gate_w.astype(jnp.float32))
        + gate_b[:, None, None].astype(jnp.float32))
    r = gates[0].reshape(bsz, seq, width)
    i = gates[1].reshape(bsz, seq, width)
    log_a = -RG_C * r * jax.nn.softplus(-lam.astype(jnp.float32))
    a = jnp.exp(log_a)
    b = jnp.sqrt(-jnp.expm1(2.0 * log_a)) * (i * uf)

    def combine(left, right):
        a_l, b_l = left
        a_r, b_r = right
        return (a_l * a_r, a_r * b_l + b_r)

    _, h = lax.associative_scan(combine, (a, b), reverse=reverse, axis=1)
    return h

def gla_chunked(q, k, v, g):
    bsz, nh, seq, dk = q.shape
    dv = v.shape[-1]
    nc = seq // GLA_CHUNK
    qc = q.astype(jnp.float32).reshape(bsz, nh, nc, GLA_CHUNK, dk) * (dk ** -0.5)
    kc = k.astype(jnp.float32).reshape(bsz, nh, nc, GLA_CHUNK, dk)
    vc = v.astype(jnp.float32).reshape(bsz, nh, nc, GLA_CHUNK, dv)
    gc = g.reshape(bsz, nh, nc, GLA_CHUNK, dk)
    bcum = jnp.cumsum(gc, axis=3)
    btot = bcum[..., -1:, :]
    q_in = qc * jnp.exp(bcum)
    k_in = kc * jnp.exp(-bcum)
    k_st = kc * jnp.exp(btot - bcum)
    mask = jnp.tril(jnp.ones((GLA_CHUNK, GLA_CHUNK), dtype=bool))
    scores = jnp.einsum('bhnid,bhnjd->bhnij', q_in, k_in)
    scores = jnp.where(mask, scores, 0.0)
    o_intra = jnp.einsum('bhnij,bhnje->bhnie', scores, vc)
    decay = jnp.exp(btot[..., 0, :])

    def step(state, xs):
        q_n, k_n, v_n, dec_n = xs
        o_n = jnp.einsum('bhcd,bhde->bhce', q_n, state)
        state = dec_n[..., None] * state + jnp.einsum('bhcd,bhce->bhde', k_n, v_n)
        return state, o_n

    xs = (jnp.moveaxis(q_in, 2, 0), jnp.moveaxis(k_st, 2, 0),
          jnp.moveaxis(vc, 2, 0), jnp.moveaxis(decay, 2, 0))
    state0 = jnp.zeros((bsz, nh, dk, dv), jnp.float32)
    _, o_inter = lax.scan(step, state0, xs)
    o_inter = jnp.moveaxis(o_inter, 0, 2)
    return (o_intra + o_inter).reshape(bsz, nh, seq, dv)

def even_layer(x, norm_pre, norm_post, w_in, conv_w, conv_b, gate_w, gate_b, lam, sc_w, w_out):
    h = rmsnorm(x, norm_pre)
    proj = h @ w_in
    xa, za, xb, gb, gc, zb = jnp.split(
        proj, [RG_WIDTH, 2 * RG_WIDTH, 2 * RG_WIDTH + SC_WIDTH,
               2 * RG_WIDTH + 2 * SC_WIDTH, 2 * RG_WIDTH + 3 * SC_WIDTH], axis=-1)
    ua = centred_dwconv(xa, conv_w, RG_CONV_LEFT) + conv_b
    ya = rg_lru(ua, gate_w[0], gate_b[0], lam[0], False) + rg_lru(ua, gate_w[1], gate_b[1], lam[1], True)
    ya = ya * jax.nn.silu(za.astype(jnp.float32))
    yb = gb * centred_dwconv(gc * xb, sc_w, SC_CONV_LEFT)
    yb = yb * jax.nn.silu(zb)
    y = jnp.concatenate([ya, yb.astype(jnp.float32)], axis=-1) @ w_out
    return (x + rmsnorm(y, norm_post)).astype(x.dtype)

def odd_layer(x, norm_pre, norm_post, w_in, w_gate_lr, b_gate, head_norm_g, w_out):
    bsz, seq, _ = x.shape
    h = rmsnorm(x, norm_pre)
    proj = h @ w_in
    q, k, v, r, lr = jnp.split(
        proj, [GLA_KEY, 2 * GLA_KEY, 2 * GLA_KEY + GLA_VAL, 2 * GLA_KEY + 2 * GLA_VAL], axis=-1)
    lr = lr.reshape(bsz, seq, 2, GLA_RANK).astype(jnp.float32)
    z = jnp.einsum('bsdr,drk->dbsk', lr, w_gate_lr.astype(jnp.float32)) + b_gate[:, None, None].astype(jnp.float32)
    log_alpha = jax.nn.log_sigmoid(z) / GLA_NORMALIZER

    def heads(t, dh):
        return jnp.transpose(t.reshape(bsz, seq, GLA_HEADS, dh), (0, 2, 1, 3))

    qh, kh, vh = heads(q, GLA_DK), heads(k, GLA_DK), heads(v, GLA_DV)
    g_f, g_b = heads(log_alpha[0], GLA_DK), heads(log_alpha[1], GLA_DK)
    o_f = gla_chunked(qh, kh, vh, g_f)
    o_b = jnp.flip(gla_chunked(jnp.flip(qh, 2), jnp.flip(kh, 2), jnp.flip(vh, 2), jnp.flip(g_b, 2)), 2)
    o = rmsnorm(o_f + o_b, head_norm_g)
    o = jnp.transpose(o, (0, 2, 1, 3)).reshape(bsz, seq, GLA_VAL)
    y = (o * jax.nn.silu(r.astype(jnp.float32))) @ w_out
    return (x + rmsnorm(y, norm_post)).astype(x.dtype)

def second_inputs(seed: int = 0) -> dict:
    key = jax.random.key(seed)
    ks = jax.random.split(key, 20)
    nrm = jax.random.normal
    f32 = jnp.float32
    lam_a = jax.random.uniform(ks[8], (N_EVEN, 2, RG_WIDTH), f32, minval=0.9, maxval=0.999)
    lam_s = lam_a ** (1.0 / RG_C)
    rg_lambda = jnp.log(lam_s) - jnp.log1p(-lam_s)
    return {
        'x': nrm(ks[0], (BATCH, SEQ, D_MODEL), f32),
        'even_norm_pre': 1.0 + 0.05 * nrm(ks[1], (N_EVEN, D_MODEL), f32),
        'even_norm_post': 1.0 + 0.05 * nrm(ks[2], (N_EVEN, D_MODEL), f32),
        'even_w_in': nrm(ks[3], (N_EVEN, D_MODEL, EVEN_IN), f32) * D_MODEL ** -0.5,
        'rg_conv_w': nrm(ks[4], (N_EVEN, RG_CONV, RG_WIDTH), f32) * RG_CONV ** -0.5,
        'rg_conv_b': 0.01 * nrm(ks[5], (N_EVEN, RG_WIDTH), f32),
        'rg_gate_w': nrm(ks[6], (N_EVEN, 2, 2, RG_HEADS, RG_HEAD_DIM, RG_HEAD_DIM), f32) * RG_HEAD_DIM ** -0.5,
        'rg_gate_b': 0.01 * nrm(ks[7], (N_EVEN, 2, 2, RG_HEADS, RG_HEAD_DIM), f32),
        'rg_lambda': rg_lambda,
        'sc_conv_w': nrm(ks[9], (N_EVEN, SC_CONV, SC_WIDTH), f32) * SC_CONV ** -0.5,
        'even_w_out': nrm(ks[10], (N_EVEN, EVEN_MIX, D_MODEL), f32) * EVEN_MIX ** -0.5,
        'odd_norm_pre': 1.0 + 0.05 * nrm(ks[11], (N_ODD, D_MODEL), f32),
        'odd_norm_post': 1.0 + 0.05 * nrm(ks[12], (N_ODD, D_MODEL), f32),
        'odd_w_in': nrm(ks[13], (N_ODD, D_MODEL, ODD_IN), f32) * D_MODEL ** -0.5,
        'gla_w_gate_lr': nrm(ks[14], (N_ODD, 2, GLA_RANK, GLA_KEY), f32) * GLA_RANK ** -0.5,
        'gla_b_gate': 1.0 + 0.3 * nrm(ks[15], (N_ODD, 2, GLA_KEY), f32),
        'gla_norm_g': 1.0 + 0.05 * nrm(ks[16], (N_ODD, GLA_DV), f32),
        'odd_w_out': nrm(ks[17], (N_ODD, GLA_VAL, D_MODEL), f32) * GLA_VAL ** -0.5,
    }

def second_block(x, even_norm_pre, even_norm_post, even_w_in, rg_conv_w, rg_conv_b, rg_gate_w,
              rg_gate_b, rg_lambda, sc_conv_w, even_w_out, odd_norm_pre, odd_norm_post,
              odd_w_in, gla_w_gate_lr, gla_b_gate, gla_norm_g, odd_w_out):
    for layer in range(DEPTH):
        j = layer // 2
        if layer % 2 == 0:
            x = even_layer(x, even_norm_pre[j], even_norm_post[j], even_w_in[j], rg_conv_w[j],
                           rg_conv_b[j], rg_gate_w[j], rg_gate_b[j], rg_lambda[j],
                           sc_conv_w[j], even_w_out[j])
        else:
            x = odd_layer(x, odd_norm_pre[j], odd_norm_post[j], odd_w_in[j], gla_w_gate_lr[j],
                          gla_b_gate[j], gla_norm_g[j], odd_w_out[j])
    return x


def setup_inputs(seed=0):
    out = dict(first_inputs(seed))
    for name, value in second_inputs(seed + 1).items():
        if name != "x":
            out[name + "_2"] = value
    return out


def reference(
    x, positions, attn_norm, w_in, w_out, rw_mu, rw_w0, rw_w2, rw_a0, rw_a2, rw_g2, rw_k_k,
    rw_k_a, rw_r_k, rw_gn_w, rw_gn_b, rw_v0, rw_v1, rw_v2, mla_q_norm, mla_kv_norm, mla_w_q_up,
    mla_w_kv_up, ffn_norm, w_gate_up, w_down, final_norm, even_norm_pre_2, even_norm_post_2,
    even_w_in_2, rg_conv_w_2, rg_conv_b_2, rg_gate_w_2, rg_gate_b_2, rg_lambda_2, sc_conv_w_2,
    even_w_out_2, odd_norm_pre_2, odd_norm_post_2, odd_w_in_2, gla_w_gate_lr_2, gla_b_gate_2,
    gla_norm_g_2, odd_w_out_2,
):
    x = first_block(
        x, positions, attn_norm, w_in, w_out, rw_mu, rw_w0, rw_w2, rw_a0, rw_a2, rw_g2, rw_k_k,
        rw_k_a, rw_r_k, rw_gn_w, rw_gn_b, rw_v0, rw_v1, rw_v2, mla_q_norm, mla_kv_norm,
        mla_w_q_up, mla_w_kv_up, ffn_norm, w_gate_up, w_down, final_norm,
    )
    return second_block(
        x, even_norm_pre_2, even_norm_post_2, even_w_in_2, rg_conv_w_2, rg_conv_b_2,
        rg_gate_w_2, rg_gate_b_2, rg_lambda_2, sc_conv_w_2, even_w_out_2, odd_norm_pre_2,
        odd_norm_post_2, odd_w_in_2, gla_w_gate_lr_2, gla_b_gate_2, gla_norm_g_2, odd_w_out_2,
    )


_drawn_inputs = setup_inputs


def setup_inputs(seed=0):
    import zlib

    import numpy as np

    out = dict(_drawn_inputs(seed))
    spreads = {}
    factors = {'rw_gn_b': 3.125,
     'rw_v0': 28.192,
     'mla_q_norm': 3.71,
     'rg_gate_b_2': 8.0,
     'rw_v1': 6.404,
     'rw_v2': 6.641}
    for name, (base, spread) in spreads.items():
        noise = np.random.default_rng([zlib.crc32(name.encode()), seed]).standard_normal(out[name].shape)
        drawn = base * np.exp(spread * noise) if base else spread * noise
        out[name] = jnp.asarray(drawn.astype(out[name].dtype))
    for name, factor in factors.items():
        out[name] = (out[name] * factor).astype(out[name].dtype)
    return out
```

```python
from contextlib import ExitStack

import numpy as np
import concourse.bass as bass
from concourse import mybir

ALU = mybir.AluOpType
ACT = mybir.ActivationFunctionType
F32 = mybir.dt.float32
F32R = mybir.dt.float32r
I32 = mybir.dt.int32
AX_X = mybir.AxisListType.X

P = 128
D = 1024
T = 512
NT = T // P
DT = D // P
DEPTH = 2
EPS = 1e-6

RW_H, RW_HD = 4, 64
RW_DIM = RW_H * RW_HD
RW_HP = RW_DIM // P
RW_PA = 7
RW_GN_EPS = 64e-5
RW_CHUNK = 64
NC = T // RW_CHUNK
HALF_E = float(np.exp(-0.5))

RET_H = 4
MLA_H, MLA_NOPE, MLA_ROPE, MLA_V = 8, 64, 32, 64
MLA_QK = MLA_NOPE + MLA_ROPE
QT, KVT = 3, 2
Q_RANK, KV_RANK = QT * P, KVT * P
MLA_SCALE = MLA_QK ** -0.5
D_FF = 2816
FT = D_FF // P
FH = FT // 2
GLA_H, GLA_DV = 4, 256
GLA_CHUNK = 64

BANKS = 8
SLOTS = 2
SLOT = 2048
NEG = -3.0e38
LEVELS = (2, 4, 8, 16, 32)
GLA_PARTS = ((0, 2), (1, 3), (5,), (4, 6))

PAR = {}


def _par(name, n):
    PAR[name] = (sum(c for _, c in PAR.values()), n)


for _l in range(DEPTH):
    for _name, _n in (("attn_norm", DT), ("mu", RW_PA), ("w0", 2), ("a0", 2), ("k_k", 2), ("k_a", 2),
                      ("r_k", 2), ("gn_w", 2), ("gn_b", 2), ("v0", 2), ("q_norm", QT), ("kv_norm", KVT),
                      ("ffn_norm", DT)):
        _par(f"{_name}{_l}", _n)
_par("final_norm", DT)
for _name, _n in (("even_pre", DT), ("even_post", DT), ("conv_w", 4 * DT), ("conv_b", DT), ("gate_b", 4 * DT),
                  ("lam", 2 * DT), ("sc_w", 3 * DT), ("odd_pre", DT), ("odd_post", DT), ("b_gate", 2 * GLA_H),
                  ("gla_norm", 2)):
    _par(_name, _n)
NPAR = sum(c for _, c in PAR.values())

CON = {}


def _con(name, n):
    CON[name] = (sum(c for _, c in CON.values()), n)


for _name in ("ident", "ones", "ones64", "rot_ret", "upper", "upper_strict", "lower", "lower_strict",
              "upper_pair", "lower_pair", "causal"):
    _con(_name, P)
for _b in LEVELS:
    _con(f"lower_off{_b}", P)
_con("rot_mla", MLA_ROPE)
_con("inv_freq", 2)
_con("decay", RET_H * T)
_con("carry", T)
NCON = sum(c for _, c in CON.values())


def constants():
    c = np.zeros((P, NCON), np.float32)

    def put(name, a):
        o, n = CON[name]
        c[:, o:o + n] = a

    i = np.arange(P)
    row, col = i[:, None], i[None, :]
    same = row // RW_CHUNK == col // RW_CHUNK
    put("ident", np.eye(P))
    put("ones", 1.0)
    put("ones64", same)
    rot = np.zeros((P, P))
    for m in range(P):
        if m % 64 < 32:
            rot[m + 32, m] = -1.0
        else:
            rot[m - 32, m] = 1.0
    put("rot_ret", rot)
    rot = np.zeros((P, MLA_ROPE))
    for m in range(MLA_ROPE):
        if m < 16:
            rot[MLA_NOPE + m + 16, m] = -1.0
        else:
            rot[MLA_NOPE + m - 16, m] = 1.0
    put("rot_mla", rot)
    put("upper", same & (row <= col))
    put("upper_strict", same & (row < col))
    put("lower", same & (row >= col))
    put("lower_strict", same & (row > col))
    put("upper_pair", (row // 2 == col // 2) & (row < col))
    put("lower_pair", (row // 2 == col // 2) & (row > col))
    for b in LEVELS:
        put(f"lower_off{b}", (row // (2 * b) == col // (2 * b)) & (row // b > col // b))
    put("causal", np.where(col <= row, 0.0, NEG))
    inv = np.stack([
        np.float32(10000.0) ** (-(np.float32(2) * (i % 32).astype(np.float32)) / np.float32(64)),
        np.float32(10000.0) ** (-(np.float32(2) * (i % 16).astype(np.float32)) / np.float32(32)),
    ], axis=1)
    put("inv_freq", inv)
    gap = np.arange(T)[None, :] - i[:, None]
    for h in range(RET_H):
        o, _ = CON["decay"]
        gamma = 1.0 - 2.0 ** (-5.0 - h)
        c[:, o + h * T:o + (h + 1) * T] = np.where(gap >= 0, gamma ** np.maximum(gap, 0), 0.0) * 64 ** -0.5
    put("carry", (np.arange(T) % GLA_CHUNK != 0)[None, :])
    return c


def slab_plan():
    plan = []
    tile2 = 2 * DT * P
    for l in range(DEPTH):
        for n in ("r", "k", "v", "lo_rq0", "rq1_rk0", "rk1_rg0", "rg1_mq0", "mq12", "mkv"):
            plan.append((f"in{l}_{n}", tile2))
        plan.append((f"in{l}_krope", DT * P))
        plan.append((f"in{l}_rv", DT * RW_DIM))
        for n in range(2):
            plan.append((f"q_up{l}_{n}", 4 * QT * MLA_QK))
        plan.append((f"kv_up{l}", KVT * MLA_H * (MLA_NOPE + MLA_V)))
        for n in range(DT // 2):
            plan.append((f"out{l}_{n}", tile2))
        for half in range(2):
            for j in range(half * FH, (half + 1) * FH):
                plan.append((f"gu{l}_{j}", tile2))
            for m in range(DT):
                plan.append((f"down{l}_{m}_{half}", FH * P))
    for m in range(DT):
        for n in ("xa_za", "xb_gc", "gb_zb"):
            plan.append((f"even_{n}{m}", tile2))
        if m:
            plan.append((f"gates{m - 1}", 4 * P))
    plan.append((f"gates{DT - 1}", 4 * P))
    for m in range(DT):
        plan.append((f"even_out{m}", 2 * DT * P))
    for n in range(4):
        plan.append((f"odd_qk{n}", tile2))
    for n in range(4):
        plan.append((f"odd_v{n}", DT * 256))
    plan.append(("odd_lr", DT * P))
    for n in range(4):
        plan.append((f"odd_r{n}", tile2))
    for n in range(4):
        plan.append((f"odd_out{n}", tile2))
    return plan


def is_split(name):
    return not name.startswith(("q_up", "kv_up", "gates"))


def pack_slabs(x):

    def cols(w, start, n):
        k = w.shape[0] // P
        return np.transpose(w[:, start:start + n].reshape(k, P, n), (1, 0, 2)).reshape(P, k * n)

    def padded(w, start, n, at):
        z = np.zeros((P, w.shape[0] // P, P), np.float32)
        z[:, :, at:at + n] = cols(w, start, n).reshape(P, -1, n)
        return z.reshape(P, -1)

    def tiles(w, *starts):
        return np.concatenate([cols(w, s, P) for s in starts], axis=1)

    out = {}
    for l in range(DEPTH):
        w = x["w_in"][l]
        ret, mla = 896, 896 + 1024
        rq, rk, rv, rg = ret, ret + 256, ret + 512, ret + 768
        out[f"in{l}_r"] = tiles(w, 0, 128)
        out[f"in{l}_k"] = tiles(w, 256, 384)
        out[f"in{l}_v"] = tiles(w, 512, 640)
        out[f"in{l}_lo_rq0"] = tiles(w, 768, rq)
        out[f"in{l}_rq1_rk0"] = tiles(w, rq + P, rk)
        out[f"in{l}_rk1_rg0"] = tiles(w, rk + P, rg)
        out[f"in{l}_rg1_mq0"] = tiles(w, rg + P, mla)
        out[f"in{l}_mq12"] = tiles(w, mla + P, mla + 2 * P)
        out[f"in{l}_mkv"] = tiles(w, mla + Q_RANK, mla + Q_RANK + P)
        out[f"in{l}_krope"] = padded(w, mla + Q_RANK + KV_RANK, MLA_ROPE, 64)
        out[f"in{l}_rv"] = cols(w, rv, RW_DIM)
        q = x["mla_w_q_up"][l]
        for n in range(2):
            out[f"q_up{l}_{n}"] = np.concatenate([cols(q, h * MLA_QK, MLA_QK) for h in range(4 * n, 4 * n + 4)], 1)
        kv = x["mla_w_kv_up"][l].reshape(KV_RANK, MLA_H, MLA_NOPE + MLA_V)
        v = kv[:, :, MLA_NOPE:].reshape(KV_RANK, MLA_H * MLA_V)
        out[f"kv_up{l}"] = np.concatenate([cols(kv[:, h], 0, MLA_NOPE) for h in range(MLA_H)]
                                          + [cols(v, 0, MLA_H * MLA_V)], axis=1)
        for n in range(DT // 2):
            out[f"out{l}_{n}"] = tiles(x["w_out"][l], 2 * n * P, (2 * n + 1) * P)
        for j in range(FT):
            out[f"gu{l}_{j}"] = tiles(x["w_gate_up"][l], j * P, D_FF + j * P)
        for m in range(DT):
            for half in range(2):
                wd = x["w_down"][l][half * FH * P:(half + 1) * FH * P]
                out[f"down{l}_{m}_{half}"] = cols(wd, m * P, P)
    w = x["even_w_in_2"][0]
    for m in range(DT):
        xa, za, xb, gb, gc, zb = (n * D + m * P for n in range(6))
        out[f"even_xa_za{m}"] = tiles(w, xa, za)
        out[f"even_xb_gc{m}"] = tiles(w, xb, gc)
        out[f"even_gb_zb{m}"] = tiles(w, gb, zb)
        out[f"even_out{m}"] = cols(x["even_w_out_2"][0], m * P, P)
        g = x["rg_gate_w_2"][0].reshape(4, DT, P, P)
        out[f"gates{m}"] = np.concatenate([g[n, m] for n in range(4)], axis=1)
    w = x["odd_w_in_2"][0]
    for n in range(4):
        out[f"odd_qk{n}"] = tiles(w, 2 * n * P, (2 * n + 1) * P)
        out[f"odd_v{n}"] = cols(w, 1024 + n * 256, 256)
        out[f"odd_r{n}"] = tiles(w, 2048 + 2 * n * P, 2048 + (2 * n + 1) * P)
        out[f"odd_out{n}"] = tiles(x["odd_w_out_2"][0], 2 * n * P, (2 * n + 1) * P)
    out["odd_lr"] = padded(w, 3072, 32, 0)
    return np.concatenate([out[name].ravel() for name, _ in slab_plan()])


def pack_params(x):
    a = np.zeros((P, NPAR), np.float32)

    def put(name, v):
        o, n = PAR[name]
        a[:, o:o + n] = v.reshape(n, P).T

    for l in range(DEPTH):
        for name, src in (("attn_norm", "attn_norm"), ("mu", "rw_mu"), ("w0", "rw_w0"), ("a0", "rw_a0"),
                          ("k_k", "rw_k_k"), ("k_a", "rw_k_a"), ("r_k", "rw_r_k"), ("gn_w", "rw_gn_w"),
                          ("gn_b", "rw_gn_b"), ("q_norm", "mla_q_norm"), ("kv_norm", "mla_kv_norm"),
                          ("ffn_norm", "ffn_norm")):
            put(f"{name}{l}", x[src][l])
        if l:
            put(f"v0{l}", x["rw_v0"][l - 1])
    put("final_norm", x["final_norm"])
    put("even_pre", x["even_norm_pre_2"][0])
    put("even_post", x["even_norm_post_2"][0])
    put("conv_w", x["rg_conv_w_2"][0])
    put("conv_b", x["rg_conv_b_2"][0])
    put("gate_b", x["rg_gate_b_2"][0])
    put("lam", x["rg_lambda_2"][0])
    put("sc_w", x["sc_conv_w_2"][0])
    put("odd_pre", x["odd_norm_pre_2"][0])
    put("odd_post", x["odd_norm_post_2"][0])
    put("b_gate", x["gla_b_gate_2"][0])
    put("gla_norm", x["gla_norm_g_2"][0])
    return a


LORA, V1, V2, GLR = 0, 2 * RW_DIM, 2 * RW_DIM + 64, 2 * RW_DIM + 64 + RW_DIM
NSMALL = GLR + 2 * T


def pack_small(x):
    a = np.zeros((P, NSMALL), np.float32)
    for l in range(DEPTH):
        o = LORA + l * RW_DIM
        a[0:32, o:o + RW_DIM] = x["rw_w2"][l]
        a[32:64, o:o + RW_DIM] = x["rw_a2"][l]
        a[64:128, o:o + RW_DIM] = x["rw_g2"][l]
    a[:, V1:V1 + 64] = np.transpose(x["rw_v1"][0].reshape(2, P, 32), (1, 0, 2)).reshape(P, 64)
    a[0:32, V2:V2 + RW_DIM] = x["rw_v2"][0]
    for d in range(2):
        a[16 * d:16 * d + 16, GLR + d * T:GLR + (d + 1) * T] = x["gla_w_gate_lr_2"][0, d]
    return a


class Count:

    def __init__(self):
        self.given, self.seen = {}, {}
        self.sem, self.value = None, 0

    def up(self, sem):
        self.given[id(sem)] = self.given.get(id(sem), 0) + 1
        self.sem, self.value = sem, self.given[id(sem)]
        return sem

    def next(self, sem, n=1):
        self.seen[id(sem)] = self.seen.get(id(sem), 0) + n
        return self.seen[id(sem)]


def two_blocks(nc, x_in, pos_in, slabs_in, par_in, small_in, con_in, out):
    with ExitStack() as ctx:
        def sb(name, shape, dt=F32):
            return ctx.enter_context(nc.sbuf_tensor(name, shape, dt))

        def sem(name):
            return ctx.enter_context(nc.semaphore(name))

        h = sb("h", [P, DT, T])
        ring = sb("ring", [P, SLOTS, SLOT])
        ring_high = sb("ring_high", [P, SLOTS, SLOT], F32R)
        ring_low = sb("ring_low", [P, SLOTS, SLOT], F32R)
        arena_at = nc.sbuf_base
        arena = sb("arena", [P, 53, T])
        arena_split = nc.alloc_sbuf_tensor_at("arena_split", [P, 53, T], F32R, offset=arena_at)
        con = sb("con", [P, NCON])
        par = sb("par", [P, NPAR])
        small = sb("small", [P, NSMALL])
        trig = sb("trig", [P, 4, T])
        omu = sb("omu", [P, DEPTH, RW_PA])
        oka = sb("oka", [P, DEPTH, 2])
        splus = sb("splus", [P, 2 * DT])
        sp_t = sb("sp_t", [P, 2, 2 * DT])
        stat = sb("stat", [P, 4, MLA_H * NT])
        decay_end = sb("decay_end", [P, 2, NC])
        gla_dec = sb("gla_dec", [P, 2, 2, NC])
        banks = [ctx.enter_context(nc.psum_tensor(f"bank{i}", [P, T], F32)) for i in range(BANKS)]

        def A(t, n=1):
            return arena[:, t:t + n, :]

        def R(t):
            return arena_split[:, t, :]

        def flat(t, n):
            return arena[:, t:t + n, :].rearrange("p a b -> p (a b)")

        def cst(name):
            o, n = CON[name]
            return con[:, o:o + n]

        def pr(name, m=0):
            o, _ = PAR[name]
            return par[:, o + m:o + m + 1]

        x_loaded, pos_loaded, con_loaded, par_loaded, small_loaded = (
            sem(n) for n in ("x_loaded", "pos_loaded", "con_loaded", "par_loaded", "small_loaded"))
        slab_high_ready, slab_split = sem("slab_high_ready"), sem("slab_split")
        high_ready, parts_ready = sem("high_ready"), sem("parts_ready")
        slab_loaded = [sem(f"slab_loaded{i}") for i in range(SLOTS)]
        psum_ready, act_released, dve_released = sem("psum_ready"), sem("act_released"), sem("dve_released")
        act_done, dve_done, pool_done = sem("act_done"), sem("dve_done"), sem("pool_done")
        released = {"act": act_released, "dve": dve_released}
        square_ready = sem("square_ready")
        square_used = sem("square_used")
        squares_summed = sem("squares_summed")
        deviation_ready = sem("deviation_ready")
        value_ready = sem("value_ready")
        residual_ready = sem("residual_ready")
        output_ready = sem("output_ready")
        angle_ready = sem("angle_ready")
        sine_ready = sem("sine_ready")
        praw_used = sem("praw_used")
        shifted_ready = sem("shifted_ready")
        lora_ready = sem("lora_ready")
        latent_squares_ready = sem("latent_squares_ready")
        latent_ready = sem("latent_ready")
        krope_ready = sem("krope_ready")
        krope_spread = sem("krope_spread")
        qrope_ready = sem("qrope_ready")
        bias_ready = sem("bias_ready")
        attn_done = sem("attn_done")
        ret_rope_ready = sem("ret_rope_ready")
        mix_ret_ready = sem("mix_ret_ready")
        kk_square_ready = sem("kk_square_ready")
        decay_summed = sem("decay_summed")
        decays_ready = sem("decays_ready")
        scan_inputs_ready = sem("scan_inputs_ready")
        bonus_product_ready = sem("bonus_product_ready")
        lower_off_ready = sem("lower_off_ready")
        inverse_ready = sem("inverse_ready")
        state_input_ready = sem("state_input_ready")
        state_ready = sem("state_ready")
        centred_ready = sem("centred_ready")
        y_squares_ready = sem("y_squares_ready")
        mix_rw_ready = sem("mix_rw_ready")
        silu_used = sem("silu_used")
        conv_padded = sem("conv_padded")
        conv_ready = sem("conv_ready")
        sqrt_ready = sem("sqrt_ready")
        gated_ready = sem("gated_ready")
        mix_even_ready = sem("mix_even_ready")
        ebuf_used = sem("ebuf_used")
        lam_exp_ready = sem("lam_exp_ready")
        lam_ready = sem("lam_ready")
        gla_min_ready = sem("gla_min_ready")
        gla_log_ready = sem("gla_log_ready")
        gla_cum_ready = sem("gla_cum_ready")
        gla_exps_ready = sem("gla_exps_ready")
        gla_inputs_ready = sem("gla_inputs_ready")
        gla_pt_ready = sem("gla_pt_ready")
        gla_state_ready = sem("gla_state_ready")
        gla_mix_ready = sem("gla_mix_ready")
        gla_o_used = sem("gla_o_used")
        stored = sem("stored")

        plan = slab_plan()
        slab_index = {name: n for n, (name, _) in enumerate(plan)}
        split_slabs = [name for name, _ in plan if is_split(name)]
        split_index = {name: n for n, name in enumerate(split_slabs)}
        HN_HIGH, HN_LOW = 31, 39
        FF_HIGH, FF_LOW = list(range(10, 21)), list(range(21, 31)) + [4]
        slab_group = {}
        book = {}
        order = []
        owned = {"act": [], "dve": []}

        def rg_a(d):
            return A((30, 47)[d])[:, 0, :]

        def gla_t(hd, d, i):
            return A(25 + 6 * (hd % 2) + 3 * d + i)[:, 0, :]

        def gv(j):
            return flat(8 + 2 * j, 2)

        def gla_state(d, n):
            o = (d * 7 + n - 1) * 256
            return flat(41, 7)[:, o:o + 256]

        def gla_mix(m):
            return m // 2 + 4 * (m % 2)

        def finished(key):
            return book[key][0] + 1

        def bank(key):
            return banks[book[key][0] % BANKS]

        def taken(key):
            _, who, count = book[key]
            return released[who], count

        block = ctx.enter_context(nc.Block())

        @block.tensor
        def _(pe):
            cnt = Count()

            def group(key, owner):
                n = len(order)
                if n >= BANKS:
                    _, who, count = book[order[n - BANKS]]
                    pe.wait_ge(released[who], count)
                owned[owner].append(key)
                book[key] = (n, owner, len(owned[owner]))
                order.append(key)
                return banks[n % BANKS]

            def slab(name):
                n = slab_index[name]
                slot = n % SLOTS
                pe.wait_ge(slab_loaded[slot], 16 * (n // SLOTS + 1))
                slab_group[n] = len(order)
                return ring[:, slot, :]

            def split_slab(name):
                slab_group[slab_index[name]] = len(order)
                n = split_index[name]
                pe.wait_ge(slab_split, n + 1)
                return ring_high[:, n % SLOTS, :], ring_low[:, n % SLOTS, :]

            def product(out, weight, right, start, stop):
                pe.matmul(out, weight[0], right[0], start=start, stop=False)
                pe.matmul(out, weight[0], right[1], start=False, stop=False)
                return pe.matmul(out, weight[1], right[0], start=False, stop=stop)

            def split_gemm(key, owner, weights, rights, step=None):
                b = group(key, owner)
                for k, (w, r) in enumerate(zip(weights, rights)):
                    if step:
                        step(k)
                    mm = product(b[:, :], w, r, k == 0, k == len(weights) - 1)
                mm.then_inc(psum_ready, 1)

            def parts(highs, lows):
                return [(R(a), R(b)) for a, b in zip(highs, lows)]

            def split_tiles(pair_of_views, first, kt):
                high, low = pair_of_views
                return [(high[:, first + k * P:first + (k + 1) * P], low[:, first + k * P:first + (k + 1) * P])
                        for k in range(kt)]

            def gemm(key, owner, out_rows, weights, rights, step=None, N=T):
                b = group(key, owner)
                for k, (w, r) in enumerate(zip(weights, rights)):
                    if step:
                        step(k)
                    mm = pe.matmul(b[out_rows, 0:N], w, r, start=(k == 0), stop=(k == len(weights) - 1))
                mm.then_inc(psum_ready, 1)

            hn_parts = parts(range(HN_HIGH, HN_HIGH + DT), range(HN_LOW, HN_LOW + DT))
            rows = slice(0, P)

            def wtiles(view, first, kt, m=P):
                return [view[:, first + k * m:first + (k + 1) * m] for k in range(kt)]

            def pair(name, keys, owners, step=None):
                for n, (key, owner) in enumerate(zip(keys, owners)):
                    split_gemm(key, owner, split_tiles(split_slab(name), n * DT * P, DT), hn_parts,
                               step if n == 0 else None)

            def parts_step(k):
                pe.wait_ge(parts_ready, cnt.next(parts_ready))

            def token_major(out, name, j, start, stop):
                high, low = split_slab(name)
                js = slice(j * P, (j + 1) * P)
                for k in range(DT):
                    ks = slice(k * 256, (k + 1) * 256)
                    mm = product(out, tuple(x[:, js] for x in hn_parts[k]), (high[:, ks], low[:, ks]),
                                 start and k == 0, stop and k == DT - 1)
                return mm

            def norm_sum(tag):
                pe.wait_ge(squares_summed, cnt.next(squares_summed))
                gemm(("ss", tag), "dve", rows, [cst("ones")], [A(51)[:, 0, :]])

            def mla(l):
                q96, k96 = A(0, 8), A(31, 8)
                pe.wait_ge(latent_squares_ready, cnt.next(latent_squares_ready))
                gemm(("mqs", l), "dve", rows, [cst("ones")] * QT, [A(43 + m)[:, 0, :] for m in range(QT)])
                gemm(("mkvs", l), "dve", rows, [cst("ones")] * KVT, [A(46 + m)[:, 0, :] for m in range(KVT)])
                gemm(("krot", l), "dve", slice(64, 96), [cst("rot_mla")[64:96, :]], [A(30)[64:96, 0, :]])
                pe.wait_ge(latent_ready, cnt.next(latent_ready))
                for n in range(2):
                    v = slab(f"q_up{l}_{n}")
                    for i in range(4):
                        hd = 4 * n + i
                        v = slab(f"q_up{l}_{n}")
                        gemm(("q", l, hd), "act", slice(0, MLA_QK), wtiles(v, i * QT * MLA_QK, QT, MLA_QK),
                             [A(25 + k)[:, 0, :] for k in range(QT)])
                lat = [A(28 + k)[:, 0, :] for k in range(KVT)]
                for hd in range(MLA_H):
                    v = slab(f"kv_up{l}")
                    gemm(("kn", l, hd), "act", slice(0, 64), wtiles(v, hd * KVT * 64, KVT, 64), lat)
                    pe.wait_ge(*taken(("q", l, hd)))
                    gemm(("qrot", l, hd), "dve", slice(64, 96), [cst("rot_mla")[64:96, :]], [q96[64:96, hd, :]])
                for j in range(NT):
                    v = slab(f"kv_up{l}")
                    gemm(("vt", l, j), "act", rows, [r[:, j * P:(j + 1) * P] for r in lat],
                         wtiles(v, MLA_H * KVT * 64, KVT, T))
                pe.wait_ge(krope_spread, cnt.next(krope_spread))
                units = [(hd, i) for hd in range(MLA_H) for i in range(NT)]
                for u in range(len(units) + 3):
                    if u < len(units):
                        hd, i = units[u]
                        if i == 0:
                            pe.wait_ge(*taken(("kn", l, hd)))
                            pe.wait_ge(qrope_ready, cnt.next(qrope_ready))
                        gemm(("s", l, u), "act", rows, [q96[0:MLA_QK, hd, i * P:(i + 1) * P]],
                             [k96[0:MLA_QK, hd, 0:(i + 1) * P]], N=(i + 1) * P)
                    if 0 <= u - 2 < len(units):
                        w = u - 2
                        pe.wait_ge(*taken(("s", l, w)))
                        b = group(("t", l, w), "dve")
                        for j in range(units[w][1] + 1):
                            mm = pe.transpose(b[:, j * P:(j + 1) * P], A(47 + w % 3)[:, 0, j * P:(j + 1) * P],
                                              cst("ident"))
                        mm.then_inc(psum_ready, 1)
                    if 0 <= u - 3 < len(units):
                        w = u - 3
                        hd, i = units[w]
                        pe.wait_ge(*taken(("t", l, w)))
                        if w == 0:
                            pe.wait_ge(*taken(("vt", l, NT - 1)))
                        gemm(("pv", l, w), "dve", rows, [A(50 + w % 2)[:, 0, j * P:(j + 1) * P] for j in range(i + 1)],
                             [A(39 + j)[:, 0, hd * 64:(hd + 1) * 64] for j in range(i + 1)], N=64)
                pe.wait_ge(attn_done, cnt.next(attn_done))
                for m in range(4):
                    b = group(("ot", l, m), "act")
                    for i in range(NT):
                        mm = pe.transpose(b[:, i * P:(i + 1) * P], A(43 + i)[:, 0, m * P:(m + 1) * P], cst("ident"))
                    mm.then_inc(psum_ready, 1)

            def retention(l):
                for i in range(4):
                    gemm(("rrot", l, i), "dve", rows, [cst("rot_ret")], [A(17 + i)[:, 0, :]])
                for hp in range(2):
                    if hp == 0:
                        pe.wait_ge(ret_rope_ready, cnt.next(ret_rope_ready))
                    for e in range(2):
                        r = slice(64 * e, 64 * e + 64)
                        for j in range(NT):
                            gemm(("rs", l, 2 * hp + e, j), "dve", rows, [A(19 + hp)[r, 0, j * P:(j + 1) * P]],
                                 [A(17 + hp)[r, 0, j * P:T]], N=T - j * P)
                for hp in range(2):
                    b = group(("ry", l, hp), "act")
                    for e in range(2):
                        off = 0
                        for j in range(NT):
                            hd = 2 * hp + e
                            pe.wait_ge(*taken(("rs", l, hd, j)))
                            n = T - j * P
                            pt = flat(25 + 5 * hp, 5)[:, e * 1280 + off:e * 1280 + off + n]
                            mm = pe.matmul(b[64 * e:64 * e + 64, j * P:T],
                                           flat(21, 2)[:, j * RW_DIM + hd * 64:j * RW_DIM + (hd + 1) * 64], pt,
                                           start=(j == 0), stop=(j == NT - 1))
                            off += n
                    mm.then_inc(psum_ready, 1)
                for hp in range(2):
                    pe.wait_ge(*taken(("ry", l, hp)))
                    gemm(("rss", l, hp), "dve", rows, [cst("ones64")], [A(37 + hp)[:, 0, :]])

            def rwkv(l):
                lo = A(16)
                pe.wait_ge(lora_ready, cnt.next(lora_ready))
                w = small[:, LORA + l * RW_DIM:LORA + (l + 1) * RW_DIM]
                for n, (r, who) in enumerate(((slice(0, 32), "act"), (slice(32, 64), "act"), (slice(64, 128), "act"))):
                    for hp in range(2):
                        gemm(("z", l, n, hp), who, rows, [w[r, hp * P:(hp + 1) * P]], [lo[r, 0, :]])
                if l:
                    gemm(("vlow", l), "act", slice(0, 32), [small[:, V1 + 32 * k:V1 + 32 * (k + 1)] for k in range(2)],
                         [A(14 + k)[:, 0, :] for k in range(2)])
                    pe.wait_ge(*taken(("vlow", l)))
                    for hp in range(2):
                        gemm(("vgate", l, hp), "act", rows, [small[0:32, V2 + hp * P:V2 + (hp + 1) * P]],
                             [A(49)[0:32, 0, :]])
                pe.wait_ge(kk_square_ready, cnt.next(kk_square_ready))
                for hp in range(2):
                    gemm(("kks", l, hp), "dve", rows, [cst("ones64")], [A(35 + hp)[:, 0, :]])
                pe.wait_ge(bonus_product_ready, cnt.next(bonus_product_ready))
                for hp in range(2):
                    gemm(("bonus", l, hp), "dve", rows, [cst("ones64")], [A(37 + hp)[:, 0, :]])
                pe.wait_ge(scan_inputs_ready, cnt.next(scan_inputs_ready))
                for n, src in enumerate((14, 33, 35, 27)):
                    for hp in range(2):
                        b = group(("tok", l, n, hp), "act")
                        for j in range(NT):
                            mm = pe.transpose(b[:, j * P:(j + 1) * P], A(src + hp)[:, 0, j * P:(j + 1) * P],
                                              cst("ident"))
                        mm.then_inc(psum_ready, 1)
                Af, Bf, Kf, Rf = 33, 29, 12, 10

                def gram(key, owner, left, right, hp, e):
                    b = group(key, owner)
                    r = slice(64 * e, 64 * e + 64)
                    for j in range(NT):
                        mm = pe.matmul(b[:, j * P:(j + 1) * P], A(left + hp)[r, 0, j * P:(j + 1) * P],
                                       A(right + hp)[r, 0, j * P:(j + 1) * P], start=(j == 0), stop=(j == NT - 1))
                    mm.then_inc(psum_ready, 1)

                def tokm(t, j, hd):
                    return flat(t, 2)[:, j * RW_DIM + hd * 64:j * RW_DIM + (hd + 1) * 64]

                for hp in range(2):
                    for e in range(2):
                        gram(("L", l, hp, e), "act", Af, Bf, hp, e)
                        gram(("N", l, hp, e), "dve", Bf, Af, hp, e)
                    for e in range(2):
                        gram(("M", l, hp, e), "dve", Kf, Af, hp, e)
                    Xt, X, Lo, T1 = A(23, 2), A(21, 2), A(19, 2), A(49, 2)
                    for n, b in enumerate(LEVELS):
                        pe.wait_ge(lower_off_ready, cnt.next(lower_off_ready))
                        pe.wait_ge(inverse_ready, cnt.next(inverse_ready))
                        for e in range(2):
                            bk = group(("T1", l, hp, n, e), "act")
                            for j in range(NT):
                                js = slice(j * P, (j + 1) * P)
                                mm = pe.matmul(bk[:, js], Lo[:, e, js], Xt[:, e, js], start=(j == 0), stop=(j == 3))
                            mm.then_inc(psum_ready, 1)
                        for e in range(2):
                            pe.wait_ge(*taken(("T1", l, hp, n, e)))
                            bk = group(("Xt", l, hp, n, e), "dve")
                            for j in range(NT):
                                js = slice(j * P, (j + 1) * P)
                                mm = pe.matmul(bk[:, js], X[:, e, js], T1[:, e, js], start=(j == 0), stop=(j == 3))
                            mm.then_inc(psum_ready, 1)
                        if n < len(LEVELS) - 1:
                            for e in range(2):
                                bk = group(("X", l, hp, n, e), "dve")
                                for j in range(NT):
                                    js = slice(j * P, (j + 1) * P)
                                    mm = pe.matmul(bk[:, js], T1[:, e, js], X[:, e, js], start=(j == 0), stop=(j == 3))
                                mm.then_inc(psum_ready, 1)
                    pe.wait_ge(inverse_ready, cnt.next(inverse_ready))
                    bk = group(("MV", l, hp), "act")
                    pe.wait_ge(*taken(("tok", l, 0, 1)))
                    for j in range(NT):
                        for e in range(2):
                            js = slice(j * P, (j + 1) * P)
                            c0 = j * P + e * 64
                            mm = pe.matmul(bk[:, c0:c0 + 64], A(51 + e)[:, 0, js], tokm(41, j, 2 * hp + e),
                                           start=(j == 0 and e == 0), stop=(j == 3 and e == 1))
                    mm.then_inc(psum_ready, 1)
                    bk = group(("WT", l, hp), "act")
                    for e in range(2):
                        for j in range(NT):
                            js = slice(j * P, (j + 1) * P)
                            mm = pe.matmul(bk[64 * e:64 * e + 64, js], tokm(43, j, 2 * hp + e), Xt[:, e, js],
                                           start=(j == 0), stop=(j == 3))
                    mm.then_inc(psum_ready, 1)
                    pe.wait_ge(*taken(("MV", l, hp)))
                    bk = group(("U", l, hp), "act")
                    for j in range(NT):
                        for e in range(2):
                            js = slice(j * P, (j + 1) * P)
                            c0 = j * P + e * 64
                            mm = pe.matmul(bk[:, c0:c0 + 64], Xt[:, e, js], A(35 + hp)[:, 0, c0:c0 + 64],
                                           start=(j == 0 and e == 0), stop=(j == 3 and e == 1))
                    mm.then_inc(psum_ready, 1)
                state = flat(14, 3)
                for c in range(NC):
                    j, r = c // 2, slice(64 * (c % 2), 64 * (c % 2) + 64)
                    cs = slice(c * 64, (c + 1) * 64)
                    if c:
                        pe.wait_ge(state_ready, cnt.next(state_ready))
                        for e in range(2):
                            bk = group(("sa", l, c, e), "dve")
                            er = slice(64 * e, 64 * e + 64)
                            for hp in range(2):
                                mm = pe.matmul(bk[r, hp * 64:(hp + 1) * 64], A(25 + hp)[er, 0, cs],
                                               state[er, c * P + hp * 64:c * P + (hp + 1) * 64],
                                               start=(hp == 0), stop=(hp == 1))
                            mm.then_inc(psum_ready, 1)
                    pe.wait_ge(state_input_ready, cnt.next(state_input_ready))
                    if c < NC - 1:
                        bk = group(("st", l, c), "dve")
                        for e in range(2):
                            for hp in range(2):
                                hd = 2 * hp + e
                                o = bk[64 * e:64 * e + 64, hp * 64:(hp + 1) * 64]
                                mm = pe.matmul(o, tokm(45, j, hd)[r], tokm(27, j, hd)[r], start=(hp == 0), stop=False)
                                mm = pe.matmul(o, tokm(47, j, hd)[r], tokm(41, j, hd)[r], start=False, stop=(hp == 1))
                        mm.then_inc(psum_ready, 1)
                for hp in range(2):
                    for e in range(2):
                        gram(("RB", l, hp, e), "dve", Bf, Rf, hp, e)
                        gram(("RK", l, hp, e), "dve", Kf, Rf, hp, e)
                for hp in range(2):
                    bk = group(("y", l, hp), "act")
                    for e in range(2):
                        er, hd = slice(64 * e, 64 * e + 64), 2 * hp + e
                        pe.wait_ge(*taken(("RB", l, hp, e)))
                        pe.wait_ge(*taken(("RK", l, hp, e)))
                        for j in range(NT):
                            js = slice(j * P, (j + 1) * P)
                            pe.matmul(bk[er, js], tokm(27, j, hd), A(17 + 2 * hp + e)[:, 0, js], start=(j == 0), stop=False)
                            pe.matmul(bk[er, js], tokm(41, j, hd), A(21 + 2 * hp + e)[:, 0, js], start=False, stop=False)
                        for c in range(1, NC):
                            cs = slice(c * 64, (c + 1) * 64)
                            mm = pe.matmul(bk[er, cs], state[er, c * P + hp * 64:c * P + (hp + 1) * 64],
                                           A(Rf + hp)[er, 0, cs], start=False, stop=(c == NC - 1))
                    mm.then_inc(psum_ready, 1)
                for hp in range(2):
                    pe.wait_ge(*taken(("y", l, hp)))
                    gemm(("ymean", l, hp), "dve", rows, [cst("ones64")], [A(49 + hp)[:, 0, :]])
                for hp in range(2):
                    pe.wait_ge(y_squares_ready, cnt.next(y_squares_ready))
                    gemm(("yvar", l, hp), "dve", rows, [cst("ones64")], [A(51 + hp)[:, 0, :]])

            pe.wait_ge(con_loaded, 16)
            pe.wait_ge(small_loaded, 16)
            for l in range(DEPTH):
                norm_sum(("attn", l))
                pair(f"in{l}_r", [("pa", l, 0), ("pa", l, 1)], ["act"] * 2, parts_step)
                pair(f"in{l}_k", [("pa", l, 2), ("pa", l, 3)], ["act"] * 2)
                pair(f"in{l}_v", [("pa", l, 4), ("pa", l, 5)], ["act"] * 2)
                pair(f"in{l}_lo_rq0", [("pa", l, 6), ("rqk", l, 0)], ["act"] * 2)
                pair(f"in{l}_rq1_rk0", [("rqk", l, 1), ("rqk", l, 2)], ["act"] * 2)
                pair(f"in{l}_rk1_rg0", [("rqk", l, 3), ("rg", l, 0)], ["act"] * 2)
                pair(f"in{l}_rg1_mq0", [("rg", l, 1), ("lat", l, 0)], ["act"] * 2)
                pair(f"in{l}_mq12", [("lat", l, 1), ("lat", l, 2)], ["act"] * 2)
                pair(f"in{l}_mkv", [("lat", l, 3), ("lat", l, 4)], ["act"] * 2)
                split_gemm(("kr", l), "act", split_tiles(split_slab(f"in{l}_krope"), 0, DT), hn_parts)
                for n in range(2):
                    b = group(("rv", l, n), "act")
                    for i in range(2):
                        slab_group[slab_index[f"in{l}_rv"]] = len(order) - 1
                        mm = token_major(b[:, i * 256:(i + 1) * 256], f"in{l}_rv", 2 * n + i, i == 0, i == 1)
                    slab_group[slab_index[f"in{l}_rv"]] = len(order) - 1
                    mm.then_inc(psum_ready, 1)
                mla(l)
                retention(l)
                rwkv(l)
                ks = [4, 5, 6, 7, 2, 3, 0, 1]
                for m in range(DT):
                    o = (m % 2) * DT * P
                    w = split_tiles(split_slab(f"out{l}_{m // 2}"), o, DT)
                    split_gemm(("o", l, m), "dve", [w[k] for k in ks], parts([17 + k for k in ks], [25 + k for k in ks]),
                               parts_step if m == 0 else None)
                norm_sum(("ffn", l))
                for half in range(2):
                    for j in range(half * FH, (half + 1) * FH):
                        pair(f"gu{l}_{j}", [("gate", l, j), ("up", l, j)], ["act", "dve"], parts_step if j == 0 else None)
                    for m in range(DT):
                        split_gemm(("down", l, m, half), "dve", split_tiles(split_slab(f"down{l}_{m}_{half}"), 0, FH),
                                   parts(FF_HIGH, FF_LOW), parts_step if m == 0 else None)
            norm_sum("final")

            norm_sum("even")

            def rg_gates(m):
                pe.wait_ge(conv_ready, cnt.next(conv_ready))
                for n in range(4):
                    w = slab(f"gates{m}")[:, n * P:(n + 1) * P]
                    gemm(("gate_ri", m, n // 2, n % 2), "act", rows, [w], [A(19 + m % 2)[:, 0, :]])

            for m in range(DT):
                pair(f"even_xa_za{m}", [("xa", m), ("za", m)], ["act"] * 2, parts_step if m == 0 else None)
                pair(f"even_xb_gc{m}", [("xb", m), ("gc", m)], ["act", "dve"])
                pair(f"even_gb_zb{m}", [("gb", m), ("zb", m)], ["dve", "act"])
                if m:
                    rg_gates(m - 1)
            rg_gates(DT - 1)
            ks = list(range(DT, 2 * DT)) + list(range(DT))
            for m in range(DT):
                w = split_tiles(split_slab(f"even_out{m}"), 0, 2 * DT)
                split_gemm(("eo", m), "act", [w[k] for k in ks], parts([16 + k for k in ks], [32 + k for k in ks]),
                           parts_step if m == 0 else None)
            norm_sum("even_post")

            norm_sum("odd")
            for n in range(4):
                pair(f"odd_qk{n}", [("qk", 2 * n), ("qk", 2 * n + 1)], ["act"] * 2, parts_step if n == 0 else None)
            for n in range(4):
                for jj in range(2):
                    b = group(("gv", n, jj), "act")
                    for i in range(2):
                        mm = token_major(b[:, i * 256:(i + 1) * 256], f"odd_v{n}", 2 * jj + i, i == 0, i == 1)
                    slab_group[slab_index[f"odd_v{n}"]] = len(order) - 1
                    mm.then_inc(psum_ready, 1)
            split_gemm("lr", "act", split_tiles(split_slab("odd_lr"), 0, DT), hn_parts)
            for n in range(4):
                pair(f"odd_r{n}", [("gr", 2 * n), ("gr", 2 * n + 1)], ["act"] * 2)

            def gla_gates(hd):
                for d in range(2):
                    gemm(("gz", hd, d), "dve", rows, [small[0:32, GLR + d * T + hd * P:GLR + d * T + (hd + 1) * P]],
                         [A(24)[0:32, 0, :]])

            def gla_head(hd):
                pe.wait_ge(gla_inputs_ready, cnt.next(gla_inputs_ready))
                for d in range(2):
                    b = group(("gs", hd, d), "dve")
                    for j in range(NT):
                        js = slice(j * P, (j + 1) * P)
                        mm = pe.matmul(b[:, js], gla_t(hd, d, 2)[:, js], gla_t(hd, d, 1)[:, js], start=(j == 0), stop=(j == NT - 1))
                    mm.then_inc(psum_ready, 1)
                for d in range(2):
                    b = group(("gkt", hd, d), "act")
                    for j in range(NT):
                        js = slice(j * P, (j + 1) * P)
                        mm = pe.transpose(b[:, js], gla_t(hd, d, 0)[:, js], cst("ident"))
                    mm.then_inc(psum_ready, 1)
                for steps in GLA_PARTS:
                    for d in range(2):
                        pe.wait_ge(*taken(("gkt", hd, d)))
                        b = group(("gkv", hd, d, steps), "dve")
                        for i, step in enumerate(steps):
                            c = step if d == 0 else NC - 1 - step
                            j, r = c // 2, slice(64 * (c % 2), 64 * (c % 2) + 64)
                            mm = pe.matmul(b[:, i * 256:(i + 1) * 256], A(37 + d)[r, 0, j * P:(j + 1) * P],
                                           gv(j)[r, hd * 256:(hd + 1) * 256], start=(i == 0),
                                           stop=(i == len(steps) - 1))
                        mm.then_inc(psum_ready, 1)
                pe.wait_ge(gla_pt_ready, cnt.next(gla_pt_ready))
                pe.wait_ge(gla_state_ready, cnt.next(gla_state_ready))
                for eh in range(2):
                    b = group(("go", hd, eh), "act")
                    for j in range(NT):
                        js = slice(j * P, (j + 1) * P)
                        pe.matmul(b[:, js], gv(j)[:, hd * 256 + eh * P:hd * 256 + (eh + 1) * P], A(39)[:, 0, js],
                                  start=(j == 0), stop=False)
                    for n in range(1, NC):
                        for d in range(2):
                            c = n if d == 0 else NC - 1 - n
                            s = gla_state(d, n)
                            mm = pe.matmul(b[:, c * 64:(c + 1) * 64], s[:, eh * P:(eh + 1) * P],
                                           gla_t(hd, d, 1)[:, c * 64:(c + 1) * 64], start=False,
                                           stop=(n == NC - 1 and d == 1))
                    mm.then_inc(psum_ready, 1)
                for eh in range(2):
                    pe.wait_ge(*taken(("go", hd, eh)))
                gemm(("gss", hd), "dve", rows, [cst("ones")] * 2, [A(50 + eh)[:, 0, :] for eh in range(2)])

            gla_gates(0)
            for hd in range(GLA_H):
                if hd + 1 < GLA_H:
                    gla_gates(hd + 1)
                gla_head(hd)
            for m in range(DT):
                w = split_tiles(split_slab(f"odd_out{m // 2}"), (m % 2) * DT * P, DT)
                split_gemm(("oo", m), "act", w, parts(range(25, 33), range(33, 41)), parts_step if m == 0 else None)
            norm_sum("odd_post")

        @block.scalar
        def _(act):
            cnt = Count()
            f = act.activation

            def copy_out(key, dst, rows=slice(0, P), n=T, scale=1.0, func=ACT.Copy):
                act.wait_ge(psum_ready, finished(key))
                b = bank(key)
                f(dst, b[rows, 0:n], func, scale=scale).then_inc(cnt.up(act_released), 1)

            def squares(source, arrived):
                for m in range(DT):
                    arrived(m)
                    if m >= 2:
                        act.wait_ge(square_used, cnt.next(square_used))
                    f(A(49 + m % 2)[:, 0, :], source(m), ACT.Square).then_inc(cnt.up(square_ready), 1)
                act.wait_ge(square_used, cnt.next(square_used))

            def deviation(key, t):
                act.wait_ge(*taken(key))
                f(A(t)[:, 0, :], A(t)[:, 0, :], ACT.Sqrt).then_inc(cnt.up(deviation_ready), 1)

            splits = []

            def prepare(name):
                for n in range(len(splits), min(split_index[name] + 2, len(split_slabs))):
                    slab, cols = plan[slab_index[split_slabs[n]]]
                    at = slab_index[slab]
                    act.wait_ge(slab_loaded[at % SLOTS], 16 * (at // SLOTS + 1))
                    if n >= SLOTS:
                        act.wait_ge(psum_ready, slab_group[slab_index[split_slabs[n - SLOTS]]] + 1)
                    f(ring_high[:, n % SLOTS, 0:cols], ring[:, at % SLOTS, 0:cols],
                      ACT.Copy).then_inc(cnt.up(slab_high_ready), 1)
                    splits.append(slab)

            def high(dst, src):
                f(R(dst), src, ACT.Copy).then_inc(cnt.up(high_ready), 1)

            def hn_highs():
                for m in range(DT):
                    act.wait_ge(value_ready, cnt.next(value_ready))
                    high(HN_HIGH + m, A(47 + m % 2)[:, 0, :])

            h_tile = lambda m: h[:, m, :]

            for n in range(2):
                act.wait_ge(angle_ready, cnt.next(angle_ready))
                f(trig[:, 2 * n + 1, :], trig[:, 2 * n, :], ACT.Sin).then_inc(cnt.up(act_done), 1)
                act.wait_ge(cnt.sem, cnt.value)
                f(trig[:, 2 * n, :], trig[:, 2 * n, :], ACT.Sin, scale=0.5).then_inc(cnt.up(act_done), 1)
                act.wait_ge(cnt.sem, cnt.value)
                f(trig[:, 2 * n, :], trig[:, 2 * n, :], ACT.Square).then_inc(cnt.up(sine_ready), 1)
            act.wait_ge(par_loaded, 16)
            act.wait_ge(lam_exp_ready, cnt.next(lam_exp_ready))
            f(sp_t[:, 0, :], sp_t[:, 0, :], ACT.Exp, scale=-1.0).then_inc(cnt.up(lam_ready), 1)

            for l in range(DEPTH):
                prepare(f"in{l}_r")
                if l == 0:
                    squares(h_tile, lambda m: act.wait_ge(x_loaded, 16))
                deviation(("ss", ("attn", l)), 52)
                hn_highs()
                praw = flat(47, 4)
                for m in range(RW_PA):
                    if m % 2 == 0 and m:
                        prepare(f"in{l}_" + ("r", "k", "v", "lo_rq0")[m // 2])
                    if m >= 3:
                        act.wait_ge(praw_used, cnt.next(praw_used))
                    o = (m % 3) * 513 + 1
                    copy_out(("pa", l, m), praw[:, o:o + T])
                copy_out(("rqk", l, 0), A(17)[:, 0, :])
                prepare(f"in{l}_rq1_rk0")
                copy_out(("rqk", l, 1), A(18)[:, 0, :])
                copy_out(("rqk", l, 2), A(19)[:, 0, :])
                prepare(f"in{l}_rk1_rg0")
                copy_out(("rqk", l, 3), A(20)[:, 0, :])
                copy_out(("rg", l, 0), A(23)[:, 0, :], func=ACT.Silu)
                prepare(f"in{l}_rg1_mq0")
                copy_out(("rg", l, 1), A(24)[:, 0, :], func=ACT.Silu)
                copy_out(("lat", l, 0), A(25)[:, 0, :])
                prepare(f"in{l}_mq12")
                copy_out(("lat", l, 1), A(26)[:, 0, :])
                copy_out(("lat", l, 2), A(27)[:, 0, :])
                prepare(f"in{l}_mkv")
                copy_out(("lat", l, 3), A(28)[:, 0, :])
                copy_out(("lat", l, 4), A(29)[:, 0, :])
                prepare(f"in{l}_krope")
                copy_out(("kr", l), A(30)[64:96, 0, :], rows=slice(64, 96))
                for n in range(2):
                    copy_out(("rv", l, n), A(21 + n)[:, 0, :])
                act.wait_ge(praw_used, cnt.next(praw_used, 3))
                act.wait_ge(cnt.sem, cnt.value)
                for m in range(QT + KVT):
                    ins = f(A(43 + m)[:, 0, :], A(25 + m)[:, 0, :], ACT.Square)
                    ins.then_inc(cnt.up(latent_squares_ready if m == QT + KVT - 1 else act_done), 1)

                deviation(("mqs", l), 51)
                deviation(("mkvs", l), 52)
                for hd in range(MLA_H):
                    copy_out(("q", l, hd), A(hd)[0:MLA_QK, 0, :], rows=slice(0, MLA_QK))
                for hd in range(MLA_H):
                    copy_out(("kn", l, hd), A(31 + hd)[0:64, 0, :], rows=slice(0, 64))
                for j in range(NT):
                    copy_out(("vt", l, j), A(39 + j)[:, 0, :])
                for u in range(MLA_H * NT):
                    act.wait_ge(psum_ready, finished(("s", l, u)))
                    b = bank(("s", l, u))
                    n = (u % NT + 1) * P
                    act.wait_ge(bias_ready, cnt.next(bias_ready))
                    if u >= 3:
                        act.wait_ge(psum_ready, finished(("t", l, u - 3)))
                    f(A(47 + u % 3)[:, 0, 0:n], b[:, 0:n], ACT.Exp, bias=stat[:, 1, u:u + 1],
                                 scale=MLA_SCALE, accum_out=stat[:, 2, u:u + 1]).then_inc(cnt.up(act_released), 1)
                for m in range(4):
                    copy_out(("ot", l, m), A(4 + m)[:, 0, :])

                for hp in range(2):
                    act.wait_ge(psum_ready, finished(("ry", l, hp)))
                    b = bank(("ry", l, hp))
                    f(A(35 + hp)[:, 0, :], b[:, :], ACT.Copy).then_inc(cnt.up(act_done), 1)
                    f(A(37 + hp)[:, 0, :], b[:, :], ACT.Square).then_inc(cnt.up(act_released), 1)
                for hp in range(2):
                    deviation(("rss", l, hp), 43 + hp)

                prepare(f"out{l}_0")
                lo = A(16)
                act.wait_ge(shifted_ready, cnt.next(shifted_ready))
                f(lo[0:32, 0, :], lo[0:32, 0, :], ACT.Tanh).then_inc(cnt.up(act_done), 1)
                f(lo[64:128, 0, :], lo[64:128, 0, :], ACT.Sigmoid).then_inc(cnt.up(lora_ready), 1)
                for hp in range(2):
                    act.wait_ge(psum_ready, finished(("z", l, 0, hp)))
                    b = bank(("z", l, 0, hp))
                    f(A(25 + hp)[:, 0, :], b[:, :], ACT.Sigmoid, bias=pr(f"w0{l}", hp)).then_inc(cnt.up(act_released), 1)
                for hp in range(2):
                    act.wait_ge(psum_ready, finished(("z", l, 1, hp)))
                    b = bank(("z", l, 1, hp))
                    f(A(29 + hp)[:, 0, :], b[:, :], ACT.Sigmoid, bias=pr(f"a0{l}", hp)).then_inc(cnt.up(act_released), 1)
                for hp in range(2):
                    copy_out(("z", l, 2, hp), A(39 + hp)[:, 0, :])
                if l:
                    copy_out(("vlow", l), A(49)[0:32, 0, :], rows=slice(0, 32))
                    for hp in range(2):
                        act.wait_ge(psum_ready, finished(("vgate", l, hp)))
                        b = bank(("vgate", l, hp))
                        f(A(45 + hp)[:, 0, :], b[:, :], ACT.Sigmoid, bias=pr(f"v0{l}", hp)).then_inc(cnt.up(act_released), 1)
                for hp in range(2):
                    ins = f(A(35 + hp)[:, 0, :], A(12 + hp)[:, 0, :], ACT.Square, scale=pr(f"k_k{l}", hp))
                    ins.then_inc(cnt.up(kk_square_ready if hp else act_done), 1)
                for hp in range(2):
                    deviation(("kks", l, hp), 31 + hp)
                act.wait_ge(decay_summed, cnt.next(decay_summed))
                f(A(33, 2), A(25, 2), ACT.Exp, scale=-HALF_E).then_inc(cnt.up(decays_ready), 1)
                f(A(47, 2), A(27, 2), ACT.Exp, scale=HALF_E).then_inc(cnt.up(decays_ready), 1)
                f(decay_end[:, :, :], A(27, 2).rearrange("p a (c t) -> p a c t", t=RW_CHUNK)[:, :, :, RW_CHUNK - 1],
                         ACT.Exp, scale=-HALF_E).then_inc(cnt.up(decays_ready), 1)
                act.wait_ge(cnt.sem, cnt.value)
                f(A(27, 2), A(27, 2), ACT.Exp, scale=-HALF_E).then_inc(cnt.up(decays_ready), 1)
                for n in range(4):
                    for hp in range(2):
                        dst = A((41, 43, 45, 47)[n], 2).rearrange("p a (j d) -> p (a j) d", d=RW_DIM)
                        act.wait_ge(psum_ready, finished(("tok", l, n, hp)))
                        b = bank(("tok", l, n, hp))
                        f(dst[:, :, hp * P:(hp + 1) * P], b[:, :].rearrange("p (j d) -> p j d", d=P),
                                     ACT.Copy).then_inc(cnt.up(act_released), 1)
                for hp in range(2):
                    for e in range(2):
                        copy_out(("L", l, hp, e), A(17 + e)[:, 0, :])
                    for n in range(len(LEVELS)):
                        for e in range(2):
                            copy_out(("T1", l, hp, n, e), A(49 + e)[:, 0, :])
                    copy_out(("MV", l, hp), A(35 + hp)[:, 0, :])
                    copy_out(("WT", l, hp), A(25 + hp)[:, 0, :])
                    act.wait_ge(psum_ready, finished(("U", l, hp)))
                    b = bank(("U", l, hp))
                    dst = A(31, 2).rearrange("p a (j d) -> p (a j) d", d=RW_DIM)
                    f(dst[:, :, hp * P:(hp + 1) * P], b[:, :].rearrange("p (j d) -> p j d", d=P), ACT.Copy).then_inc(cnt.up(act_released), 1)
                for hp in range(2):
                    copy_out(("y", l, hp), A(49 + hp)[:, 0, :])
                for hp in range(2):
                    act.wait_ge(centred_ready, cnt.next(centred_ready))
                    f(A(51 + hp)[:, 0, :], A(49 + hp)[:, 0, :], ACT.Square).then_inc(cnt.up(y_squares_ready), 1)
                for hp in range(2):
                    deviation(("yvar", l, hp), 51 + hp)

                for k in (4, 5, 6, 7, 2, 3, 0, 1):
                    if k == 4:
                        act.wait_ge(*taken(("ymean", l, 1)))
                    if k == 0:
                        act.wait_ge(mix_rw_ready, cnt.next(mix_rw_ready))
                    high(17 + k, A(k)[:, 0, :])

                for m in range(DT):
                    if m % 2 == 0:
                        prepare(f"out{l}_{m // 2}")
                    act.wait_ge(*taken(("o", l, m)))
                    if m >= 2:
                        act.wait_ge(square_used, cnt.next(square_used))
                    f(A(49 + m % 2)[:, 0, :], h[:, m, :], ACT.Square).then_inc(cnt.up(square_ready), 1)
                act.wait_ge(square_used, cnt.next(square_used))
                prepare(f"gu{l}_0")
                deviation(("ss", ("ffn", l)), 52)
                hn_highs()

                def ff_high(j):
                    act.wait_ge(*taken(("up", l, j)))
                    high(FF_HIGH[j % FH], A(2 + j % 2)[:, 0, :])

                for half in range(2):
                    for j in range(half * FH, (half + 1) * FH):
                        prepare(f"gu{l}_{j}")
                        if j % FH >= 2:
                            act.wait_ge(*taken(("up", l, j - 2)))
                        copy_out(("gate", l, j), A(j % 2)[:, 0, :], func=ACT.Silu)
                        if j % FH:
                            ff_high(j - 1)
                    prepare(f"down{l}_0_{half}")
                    ff_high((half + 1) * FH - 1)
                    if half == 0:
                        for m in range(DT):
                            prepare(f"down{l}_{m}_0")
                for m in range(DT):
                    prepare(f"down{l}_{m}_1")
                    act.wait_ge(*taken(("down", l, m, 1)))
                    if m >= 2:
                        act.wait_ge(square_used, cnt.next(square_used))
                    f(A(49 + m % 2)[:, 0, :], h[:, m, :], ACT.Square).then_inc(cnt.up(square_ready), 1)
                act.wait_ge(square_used, cnt.next(square_used))

            deviation(("ss", "final"), 52)

            squares(h_tile, lambda m: act.wait_ge(residual_ready, cnt.next(residual_ready)))
            deviation(("ss", "even"), 52)
            hn_highs()

            def recurrence(m):
                for d in range(2):
                    for g in range(2):
                        act.wait_ge(psum_ready, finished(("gate_ri", m, d, g)))
                        b = bank(("gate_ri", m, d, g))
                        if m and d == 0 and g == 0:
                            act.wait_ge(gated_ready, cnt.next(gated_ready))
                        f(A(26 + 2 * d + g)[:, 0, :], b[:, :], ACT.Sigmoid,
                                     bias=pr("gate_b", (d * 2 + g) * DT + m)).then_inc(cnt.up(act_released), 1)
                act.wait_ge(cnt.sem, cnt.value)
                for d in range(2):
                    r = A(26 + 2 * d)[:, 0, :]
                    f(A(48 + d)[:, 0, :], r, ACT.Tanh, scale=splus[:, d * DT + m:d * DT + m + 1]).then_inc(cnt.up(act_done), 1)
                    f(rg_a(d), r, ACT.Exp, scale=sp_t[:, 1, d * DT + m:d * DT + m + 1]).then_inc(cnt.up(act_done), 1)
                act.wait_ge(cnt.sem, cnt.value)
                for d in range(2):
                    f(A(26 + 2 * d)[:, 0, :], rg_a(d), ACT.Square).then_inc(cnt.up(conv_padded), 1)
                for d in range(2):
                    act.wait_ge(sqrt_ready, cnt.next(sqrt_ready))
                    f(A(48 + d)[:, 0, :], A(48 + d)[:, 0, :], ACT.Sqrt).then_inc(cnt.up(ebuf_used), 1)

            for m in range(DT):
                prepare(f"even_xa_za{m}")
                if m:
                    act.wait_ge(conv_ready, cnt.next(conv_ready))
                copy_out(("xa", m), flat(16, 3)[:, 2:2 + T])
                if m >= 2:
                    act.wait_ge(mix_even_ready, cnt.next(mix_even_ready))
                copy_out(("za", m), A(21 + m % 2)[:, 0, :], func=ACT.Silu)
                if m:
                    act.wait_ge(*taken(("gb", m - 1)))
                prepare(f"even_xb_gc{m}")
                copy_out(("xb", m), A(23)[:, 0, :])
                prepare(f"even_gb_zb{m}")
                if m:
                    act.wait_ge(silu_used, cnt.next(silu_used))
                copy_out(("zb", m), A(25)[:, 0, :], func=ACT.Silu)
                if m:
                    recurrence(m - 1)
            recurrence(DT - 1)
            act.wait_ge(mix_even_ready, cnt.next(mix_even_ready, 2))
            for k in list(range(DT, 2 * DT)) + list(range(DT)):
                high(16 + k, A(k)[:, 0, :])

            def outputs(name, tag, slab_of, base):
                for m in range(DT):
                    prepare(slab_of(m))
                    copy_out((name, m), A(base + m)[:, 0, :])
                    if m >= 2:
                        act.wait_ge(square_used, cnt.next(square_used))
                    act.wait_ge(cnt.sem, cnt.value)
                    f(A(49 + m % 2)[:, 0, :], A(base + m)[:, 0, :], ACT.Square).then_inc(cnt.up(square_ready), 1)
                act.wait_ge(square_used, cnt.next(square_used))
                deviation(("ss", tag), 52)

            outputs("eo", "even_post", lambda m: f"even_out{m}", 0)

            squares(h_tile, lambda m: act.wait_ge(residual_ready, cnt.next(residual_ready)))
            deviation(("ss", "odd"), 52)
            hn_highs()
            for m in range(8):
                prepare(f"odd_qk{m // 2}")
                copy_out(("qk", m), A(m)[:, 0, :], scale=P ** -0.5 if m < 4 else 1.0)
            for n in range(4):
                prepare(f"odd_v{n}")
                for jj in range(2):
                    act.wait_ge(psum_ready, finished(("gv", n, jj)))
                    b = bank(("gv", n, jj))
                    dst = A(8 + 4 * jj, 4).rearrange("p (i a) d -> p i (a d)", i=2)
                    f(dst[:, :, n * 256:(n + 1) * 256], b[:, :].rearrange("p (i d) -> p i d", i=2),
                                 ACT.Copy).then_inc(cnt.up(act_released), 1)
            prepare("odd_lr")
            copy_out("lr", A(24)[0:32, 0, :], rows=slice(0, 32))
            for m in range(8):
                prepare(f"odd_r{m // 2}")
                copy_out(("gr", m), A(16 + m)[:, 0, :], func=ACT.Silu)

            def gla_exps(hd):
                for d in range(2):
                    act.wait_ge(gla_min_ready, cnt.next(gla_min_ready))
                    z = gla_t(hd, d, 1)
                    f(z, z, ACT.Exp, scale=-1.0).then_inc(cnt.up(act_done), 1)
                    act.wait_ge(cnt.sem, cnt.value)
                    f(z, z, ACT.Ln, bias=1.0).then_inc(cnt.up(gla_log_ready), 1)
                for d in range(2):
                    act.wait_ge(gla_cum_ready, cnt.next(gla_cum_ready))
                    cum = gla_t(hd, d, 0)
                    end = RW_CHUNK - 1 if d == 0 else 0
                    f(gla_t(hd, d, 1), cum, ACT.Exp, scale=1 / 16.0).then_inc(cnt.up(act_done), 1)
                    f(gla_t(hd, d, 2), cum, ACT.Exp, scale=-1 / 16.0).then_inc(cnt.up(act_done), 1)
                    f(gla_dec[:, hd % 2, d, :], cum.rearrange("p (c t) -> p c t", t=GLA_CHUNK)[:, :, end],
                             ACT.Exp, scale=1 / 16.0).then_inc(cnt.up(gla_exps_ready), 1)

            gla_exps(0)
            for hd in range(GLA_H):
                if hd + 1 < GLA_H:
                    gla_exps(hd + 1)
                for d in range(2):
                    copy_out(("gkt", hd, d), A(37 + d)[:, 0, :])
                for eh in range(2):
                    act.wait_ge(psum_ready, finished(("go", hd, eh)))
                    b = bank(("go", hd, eh))
                    if hd and eh == 0:
                        act.wait_ge(gla_o_used, cnt.next(gla_o_used))
                    f(A(48 + eh)[:, 0, :], b[:, :], ACT.Copy).then_inc(cnt.up(act_done), 1)
                    f(A(50 + eh)[:, 0, :], b[:, :], ACT.Square).then_inc(cnt.up(act_released), 1)
                deviation(("gss", hd), 52)
            act.wait_ge(gla_o_used, cnt.next(gla_o_used))
            for k in range(DT):
                high(25 + k, A(gla_mix(k))[:, 0, :])
            outputs("oo", "odd_post", lambda m: f"odd_out{m // 2}", 8)

        @block.vector
        def _(dve):
            cnt = Count()
            tt, stt, ts, cp = dve.tensor_tensor, dve.scalar_tensor_tensor, dve.tensor_scalar, dve.tensor_copy
            MUL, ADD, SUB, MAX, MIN = ALU.mult, ALU.add, ALU.subtract, ALU.max, ALU.min

            def sum_squares(before=None):
                acc = A(51)[:, 0, :]
                for m in range(DT):
                    if before:
                        before(m)
                    dve.wait_ge(square_ready, cnt.next(square_ready))
                    sq = A(49 + m % 2)[:, 0, :]
                    sig = squares_summed if m == DT - 1 else square_used
                    if m:
                        dve.wait_ge(cnt.sem, cnt.value)
                        tt(acc, acc, sq, ADD).then_inc(cnt.up(sig), 1)
                    else:
                        cp(acc, sq).then_inc(cnt.up(sig), 1)

            def variance(key, t, n, eps):
                dve.wait_ge(psum_ready, finished(key))
                b = bank(key)
                ts(A(t)[:, 0, :], b[:, :], 1.0 / n, eps, MUL, ADD).then_inc(cnt.up(dve_released), 1)

            def invert(t):
                dve.wait_ge(deviation_ready, cnt.next(deviation_ready))
                dve.reciprocal(A(t)[:, 0, :], A(t)[:, 0, :]).then_inc(cnt.up(dve_done), 1)
                dve.wait_ge(cnt.sem, cnt.value)

            splits = []

            def prepare(name):
                for n in range(len(splits), min(split_index[name] + 2, len(split_slabs))):
                    slab, cols = plan[slab_index[split_slabs[n]]]
                    at = slab_index[slab] % SLOTS
                    dve.wait_ge(slab_high_ready, cnt.next(slab_high_ready))
                    tt(ring_low[:, n % SLOTS, 0:cols], ring[:, at, 0:cols], ring_high[:, n % SLOTS, 0:cols].bitcast(F32),
                       SUB).then_inc(cnt.up(slab_split), 1)
                    splits.append(slab)

            def low(dst, src, high):
                dve.wait_ge(high_ready, cnt.next(high_ready))
                tt(R(dst), src, R(high).bitcast(F32), SUB).then_inc(cnt.up(parts_ready), 1)

            def norm(tag, gain):
                variance(("ss", tag), 52, D, EPS)
                invert(52)
                for m in range(DT + 1):
                    if m < DT:
                        if m > 1:
                            dve.wait_ge(cnt.sem, cnt.value)
                        stt(A(47 + m % 2)[:, 0, :], h[:, m, :], pr(gain, m), A(52)[:, 0, :], MUL,
                            MUL).then_inc(cnt.up(value_ready), 1)
                    if m:
                        low(HN_LOW + m - 1, A(47 + (m - 1) % 2)[:, 0, :], HN_HIGH + m - 1)
                dve.wait_ge(cnt.sem, cnt.value)

            dve.wait_ge(par_loaded, 16)
            for l in range(DEPTH):
                o, n = PAR[f"mu{l}"]
                ts(omu[:, l, :], par[:, o:o + n], -1.0, 1.0, MUL, ADD).then_inc(cnt.up(dve_done), 1)
                o, n = PAR[f"k_a{l}"]
                ts(oka[:, l, :], par[:, o:o + n], -1.0, 1.0, MUL, ADD).then_inc(cnt.up(dve_done), 1)
            o, n = PAR["lam"]
            lam = par[:, o:o + n]
            ts(sp_t[:, 1, :], lam, -1.0, None, MUL).then_inc(cnt.up(dve_done), 1)
            dve.wait_ge(cnt.sem, cnt.value)
            tt(sp_t[:, 0, :], sp_t[:, 1, :], lam, MAX).then_inc(cnt.up(lam_exp_ready), 1)
            dve.memset(stat[:, :, :], 0.0).then_inc(cnt.up(dve_done), 1)
            dve.wait_ge(cnt.sem, cnt.value)

            dve.wait_ge(pos_loaded, 16)
            dve.wait_ge(con_loaded, 16)
            TWO_PI = 2 * np.pi
            C1 = 6.28125
            C2 = 2.0 ** -21 * int((TWO_PI - C1) * 2.0 ** 21)
            C3 = float(TWO_PI - C1 - C2)
            MAGIC = 1.5 * 2.0 ** 23
            posf, turns = A(1)[:, 0, :], A(2)[:, 0, :]
            cp(posf, A(0)[:, 0, :].bitcast(I32)).then_inc(cnt.up(dve_done), 1)
            dve.wait_ge(cnt.sem, cnt.value)
            for n in range(2):
                ang = trig[:, 2 * n, :]
                o, _ = CON["inv_freq"]
                ts(ang, posf, con[:, o + n:o + n + 1], None, MUL).then_inc(cnt.up(dve_done), 1)
                dve.wait_ge(cnt.sem, cnt.value)
                ts(turns, ang, 1.0 / TWO_PI, MAGIC, MUL, ADD).then_inc(cnt.up(dve_done), 1)
                dve.wait_ge(cnt.sem, cnt.value)
                ts(turns, turns, MAGIC, None, SUB).then_inc(cnt.up(dve_done), 1)
                dve.wait_ge(cnt.sem, cnt.value)
                for c in (C1, C2, C3):
                    stt(ang, turns, -c, ang, MUL, ADD).then_inc(cnt.up(dve_done), 1)
                    dve.wait_ge(cnt.sem, cnt.value)
                ts(ang, ang, 3.1415925, -3.1415925, MIN, MAX).then_inc(cnt.up(angle_ready), 1)
            for n in range(2):
                dve.wait_ge(sine_ready, cnt.next(sine_ready))
                ts(trig[:, 2 * n, :], trig[:, 2 * n, :], -2.0, 1.0, MUL, ADD).then_inc(cnt.up(dve_done), 1)
            dve.wait_ge(cnt.sem, cnt.value)
            cos_r, sin_r, cos_m, sin_m = (trig[:, n, :] for n in range(4))

            dve.wait_ge(lam_ready, cnt.next(lam_ready))
            y, mx = sp_t[:, 0, :], sp_t[:, 1, :]
            ts(mx, mx, 0.0, None, MAX).then_inc(cnt.up(dve_done), 1)
            ts(splus[:, :], y, 2.0, None, ADD).then_inc(cnt.up(dve_done), 1)
            dve.wait_ge(cnt.sem, cnt.value)
            dve.reciprocal(splus[:, :], splus[:, :]).then_inc(cnt.up(dve_done), 1)
            dve.wait_ge(cnt.sem, cnt.value)
            tt(y, y, splus[:, :], MUL).then_inc(cnt.up(dve_done), 1)
            dve.wait_ge(cnt.sem, cnt.value)
            sq = stat[:, 0, 0:2 * DT]
            tt(sq, y, y, MUL).then_inc(cnt.up(dve_done), 1)
            dve.wait_ge(cnt.sem, cnt.value)
            ts(splus[:, :], sq, 1.0 / 17, 1.0 / 15, MUL, ADD).then_inc(cnt.up(dve_done), 1)
            for k in (13, 11, 9, 7, 5, 3, 1):
                dve.wait_ge(cnt.sem, cnt.value)
                tt(splus[:, :], splus[:, :], sq, MUL).then_inc(cnt.up(dve_done), 1)
                dve.wait_ge(cnt.sem, cnt.value)
                ts(splus[:, :], splus[:, :], 1.0 / k, None, ADD).then_inc(cnt.up(dve_done), 1)
            dve.wait_ge(cnt.sem, cnt.value)
            stt(splus[:, :], splus[:, :], 2.0, y, MUL, MUL).then_inc(cnt.up(dve_done), 1)
            dve.wait_ge(cnt.sem, cnt.value)
            tt(splus[:, :], splus[:, :], mx, ADD).then_inc(cnt.up(dve_done), 1)
            dve.wait_ge(cnt.sem, cnt.value)
            ts(splus[:, :], splus[:, :], 8.0, None, MUL).then_inc(cnt.up(dve_done), 1)
            dve.wait_ge(cnt.sem, cnt.value)
            ts(sp_t[:, 1, :], splus[:, :], -1.0, None, MUL).then_inc(cnt.up(dve_done), 1)

            def residual(key, slab_of):
                acc = A(51)[:, 0, :]
                for m in range(DT + 1):
                    if m < DT:
                        prepare(slab_of(m))
                        dve.wait_ge(psum_ready, finished(key(m)))
                        b = bank(key(m))
                        tt(h[:, m, :], h[:, m, :], b[:, :], ADD).then_inc(cnt.up(dve_released), 1)
                    if m:
                        dve.wait_ge(square_ready, cnt.next(square_ready))
                        sqm = A(49 + (m - 1) % 2)[:, 0, :]
                        sig = squares_summed if m == DT else square_used
                        ins = cp(acc, sqm) if m == 1 else tt(acc, acc, sqm, ADD)
                        ins.then_inc(cnt.up(sig), 1)
                        dve.wait_ge(cnt.sem, cnt.value)

            for l in range(DEPTH):
                prepare(f"in{l}_r")
                if l == 0:
                    sum_squares()
                norm(("attn", l), f"attn_norm{l}")
                praw = flat(47, 4)
                for m in range(3):
                    dve.memset(praw[:, m * 513:m * 513 + 1], 0.0).then_inc(cnt.up(dve_done), 1)
                for m in range(RW_PA):
                    if m % 2 == 0 and m:
                        prepare(f"in{l}_" + ("r", "k", "v", "lo_rq0")[m // 2])
                    dve.wait_ge(*taken(("pa", l, m)))
                    o = (m % 3) * 513
                    dst = A(10 + m)[:, 0, :]
                    ts(dst, praw[:, o + 1:o + 513], omu[:, l, m:m + 1], None, MUL).then_inc(cnt.up(dve_done), 1)
                    dve.wait_ge(cnt.sem, cnt.value)
                    stt(dst, praw[:, o:o + T], pr(f"mu{l}", m), dst, MUL, ADD).then_inc(cnt.up(praw_used), 1)

                prepare(f"in{l}_krope")

                variance(("mqs", l), 51, Q_RANK, EPS)
                variance(("mkvs", l), 52, KV_RANK, EPS)
                dve.wait_ge(psum_ready, finished(("krot", l)))
                b = bank(("krot", l))
                kr, tmp = A(30)[64:96, 0, :], A(50)[64:96, 0, :]
                tt(tmp, b[64:96, :], sin_m[64:96], MUL).then_inc(cnt.up(dve_released), 1)
                tt(kr, kr, cos_m[64:96], MUL).then_inc(cnt.up(dve_done), 1)
                dve.wait_ge(cnt.sem, cnt.value)
                tt(A(31)[64:96, 0, :], kr, tmp, ADD).then_inc(cnt.up(krope_ready), 1)
                invert(51)
                for m in range(QT):
                    stt(A(25 + m)[:, 0, :], A(25 + m)[:, 0, :], pr(f"q_norm{l}", m), A(51)[:, 0, :], MUL, MUL).then_inc(cnt.up(dve_done), 1)
                invert(52)
                for m in range(KVT):
                    stt(A(28 + m)[:, 0, :], A(28 + m)[:, 0, :], pr(f"kv_norm{l}", m), A(52)[:, 0, :],
                               MUL, MUL).then_inc(cnt.up(latent_ready if m == KVT - 1 else dve_done), 1)
                dve.wait_ge(cnt.sem, cnt.value)
                for hd in range(MLA_H):
                    dve.wait_ge(psum_ready, finished(("qrot", l, hd)))
                    b = bank(("qrot", l, hd))
                    q, tmp = A(hd)[64:96, 0, :], A(50 + hd % 3)[64:96, 0, :]
                    tt(tmp, b[64:96, :], sin_m[64:96], MUL).then_inc(cnt.up(dve_released), 1)
                    tt(q, q, cos_m[64:96], MUL).then_inc(cnt.up(dve_done), 1)
                    dve.wait_ge(cnt.sem, cnt.value)
                    tt(q, q, tmp, ADD).then_inc(cnt.up(qrope_ready), 1)
                dve.wait_ge(cnt.sem, cnt.value)
                for u in range(MLA_H * NT + 3):
                    if u < MLA_H * NT:
                        i = u % NT
                        dve.wait_ge(psum_ready, finished(("s", l, u)))
                        b = bank(("s", l, u))
                        diag = b[:, i * P:(i + 1) * P]
                        tt(diag, diag, cst("causal"), ADD).then_inc(cnt.up(dve_done), 1)
                        dve.wait_ge(cnt.sem, cnt.value)
                        dve.tensor_reduce(stat[:, 0, u:u + 1], b[:, 0:(i + 1) * P], AX_X, MAX).then_inc(cnt.up(dve_done), 1)
                        dve.wait_ge(cnt.sem, cnt.value)
                        ts(stat[:, 1, u:u + 1], stat[:, 0, u:u + 1], -MLA_SCALE, None, MUL).then_inc(cnt.up(bias_ready), 1)
                    w = u - 2
                    if 0 <= w < MLA_H * NT:
                        n = (w % NT + 1) * P
                        dve.wait_ge(psum_ready, finished(("t", l, w)))
                        b = bank(("t", l, w))
                        if w >= 2:
                            dve.wait_ge(psum_ready, finished(("pv", l, w - 2)))
                        cp(A(50 + w % 2)[:, 0, 0:n], b[:, 0:n]).then_inc(cnt.up(dve_released), 1)
                        dve.reciprocal(stat[:, 3, w:w + 1], stat[:, 2, w:w + 1]).then_inc(cnt.up(dve_done), 1)
                    w = u - 3
                    if w >= 0:
                        hd, i = w // NT, w % NT
                        if u >= MLA_H * NT:
                            dve.wait_ge(cnt.sem, cnt.value)
                        dve.wait_ge(psum_ready, finished(("pv", l, w)))
                        b = bank(("pv", l, w))
                        ts(A(43 + i)[:, 0, hd * 64:(hd + 1) * 64], b[:, 0:64], stat[:, 3, w:w + 1], None,
                                      MUL).then_inc(cnt.up(dve_released), 1)
                dve.wait_ge(cnt.sem, cnt.value)
                cp(stat[:, 0, 0:1], stat[:, 1, 0:1]).then_inc(cnt.up(attn_done), 1)

                for i in range(4):
                    dve.wait_ge(psum_ready, finished(("rrot", l, i)))
                    b = bank(("rrot", l, i))
                    x, tmp = A(17 + i)[:, 0, :], A(39 + i)[:, 0, :]
                    tt(tmp, b[:, :], sin_r, MUL).then_inc(cnt.up(dve_released), 1)
                    tt(x, x, cos_r, MUL).then_inc(cnt.up(dve_done), 1)
                    dve.wait_ge(cnt.sem, cnt.value)
                    tt(x, x, tmp, ADD).then_inc(cnt.up(ret_rope_ready if i == 3 else dve_done), 1)
                dve.wait_ge(cnt.sem, cnt.value)
                o, _ = CON["decay"]
                for hd in range(RET_H):
                    off = 0
                    for j in range(NT):
                        n = T - j * P
                        dve.wait_ge(psum_ready, finished(("rs", l, hd, j)))
                        b = bank(("rs", l, hd, j))
                        dst = flat(25 + 5 * (hd // 2), 5)[:, (hd % 2) * 1280 + off:(hd % 2) * 1280 + off + n]
                        tt(dst, b[:, 0:n], con[:, o + hd * T:o + hd * T + n], MUL).then_inc(cnt.up(dve_released), 1)
                        off += n
                for hp in range(2):
                    variance(("rss", l, hp), 43 + hp, 64, EPS)
                for hp in range(2):
                    invert(43 + hp)
                    y = A(35 + hp)[:, 0, :]
                    tt(y, y, A(43 + hp)[:, 0, :], MUL).then_inc(cnt.up(dve_done), 1)
                    dve.wait_ge(cnt.sem, cnt.value)
                    tt(A(2 + hp)[:, 0, :], y, A(23 + hp)[:, 0, :], MUL).then_inc(cnt.up(mix_ret_ready if hp else dve_done), 1)

                prepare(f"out{l}_0")
                cp(stat[:, 0, 0:1], stat[:, 1, 0:1]).then_inc(cnt.up(shifted_ready), 1)
                r_, k_, v_ = (lambda hp: A(10 + hp)[:, 0, :]), (lambda hp: A(12 + hp)[:, 0, :]), (
                    lambda hp: A(14 + hp)[:, 0, :])
                carry = cst("carry")
                for hp in range(2):
                    dve.wait_ge(*taken(("z", l, 0, hp)))
                    dve.tensor_tensor_scan(A(27 + hp)[:, 0, :], carry, A(25 + hp)[:, 0, :], 0.0, MUL, ADD).then_inc(cnt.up(dve_done), 1)
                dve.wait_ge(cnt.sem, cnt.value)
                tt(A(25, 2), A(27, 2), A(25, 2), SUB).then_inc(cnt.up(decay_summed), 1)
                if l:
                    for hp in range(2):
                        tt(A(43 + hp)[:, 0, :], A(8 + hp)[:, 0, :], v_(hp), SUB).then_inc(cnt.up(dve_done), 1)
                    for hp in range(2):
                        dve.wait_ge(*taken(("vgate", l, hp)))
                        dve.wait_ge(cnt.sem, cnt.value)
                        tt(A(43 + hp)[:, 0, :], A(43 + hp)[:, 0, :], A(45 + hp)[:, 0, :], MUL).then_inc(cnt.up(dve_done), 1)
                        dve.wait_ge(cnt.sem, cnt.value)
                        tt(v_(hp), v_(hp), A(43 + hp)[:, 0, :], ADD).then_inc(cnt.up(dve_done), 1)
                else:
                    for hp in range(2):
                        cp(A(8 + hp)[:, 0, :], v_(hp)).then_inc(cnt.up(dve_done), 1)
                for hp in range(2):
                    dve.wait_ge(psum_ready, finished(("kks", l, hp)))
                    b = bank(("kks", l, hp))
                    ts(A(31 + hp)[:, 0, :], b[:, :], 1e-24, None, MAX).then_inc(cnt.up(dve_released), 1)
                for hp in range(2):
                    invert(31 + hp)
                    stt(A(31 + hp)[:, 0, :], k_(hp), pr(f"k_k{l}", hp), A(31 + hp)[:, 0, :], MUL, MUL).then_inc(cnt.up(dve_done), 1)
                for hp in range(2):
                    a = A(29 + hp)[:, 0, :]
                    dve.wait_ge(*taken(("z", l, 1, hp)))
                    ts(A(37 + hp)[:, 0, :], a, pr(f"k_a{l}", hp), oka[:, l, hp:hp + 1], MUL, ADD).then_inc(cnt.up(dve_done), 1)
                    dve.wait_ge(cnt.sem, cnt.value)
                    tt(k_(hp), k_(hp), A(37 + hp)[:, 0, :], MUL).then_inc(cnt.up(dve_done), 1)
                    tt(a, a, A(31 + hp)[:, 0, :], MUL).then_inc(cnt.up(dve_done), 1)
                    dve.wait_ge(cnt.sem, cnt.value)
                    stt(A(37 + hp)[:, 0, :], r_(hp), pr(f"r_k{l}", hp), k_(hp), MUL, MUL).then_inc(cnt.up(bonus_product_ready if hp else dve_done), 1)
                dve.wait_ge(decays_ready, cnt.next(decays_ready))
                for hp in range(2):
                    stt(A(33 + hp)[:, 0, :], A(31 + hp)[:, 0, :], -1.0, A(33 + hp)[:, 0, :], MUL, MUL).then_inc(cnt.up(dve_done), 1)
                dve.wait_ge(decays_ready, cnt.next(decays_ready))
                dve.wait_ge(cnt.sem, cnt.value)
                tt(A(29, 2), A(29, 2), A(47, 2), MUL).then_inc(cnt.up(dve_done), 1)
                tt(A(12, 2), A(12, 2), A(47, 2), MUL).then_inc(cnt.up(dve_done), 1)
                dve.wait_ge(decays_ready, cnt.next(decays_ready, 2))
                tt(A(10, 2), A(10, 2), A(27, 2), MUL).then_inc(cnt.up(dve_done), 1)
                dve.wait_ge(cnt.sem, cnt.value)
                for hp in range(2):
                    end = decay_end[:, hp, :, None].broadcast_to((P, NC, RW_CHUNK))
                    chunked = lambda t: A(t + hp)[:, 0, :].rearrange("p (c t) -> p c t", t=RW_CHUNK)
                    tt(chunked(35), chunked(29), end, MUL).then_inc(cnt.up(dve_done), 1)
                    tt(chunked(27), chunked(12), end, MUL).then_inc(cnt.up(scan_inputs_ready if hp else dve_done), 1)
                for hp in range(2):
                    dve.wait_ge(psum_ready, finished(("bonus", l, hp)))
                    b = bank(("bonus", l, hp))
                    tt(A(37 + hp)[:, 0, :], b[:, :], v_(hp), MUL).then_inc(cnt.up(dve_released), 1)

                def bc(name):
                    return cst(name)[:, None, :].broadcast_to((P, NT, P))

                def four(ap):
                    return ap.rearrange("p (j t) -> p j t", t=P)

                for hp in range(2):
                    Xt, X = A(23, 2), A(21, 2)
                    for e in range(2):
                        dve.wait_ge(psum_ready, finished(("N", l, hp, e)))
                        b = bank(("N", l, hp, e))
                        tt(four(Xt[:, e, :]), four(b[:, :]), bc("upper_pair"), MUL).then_inc(cnt.up(dve_released), 1)
                        dve.wait_ge(*taken(("L", l, hp, e)))
                        tt(four(X[:, e, :]), four(A(17 + e)[:, 0, :]), bc("lower_pair"), MUL).then_inc(cnt.up(dve_done), 1)
                    dve.wait_ge(cnt.sem, cnt.value)
                    for e in range(2):
                        tt(four(X[:, e, :]), four(X[:, e, :]), bc("ident"), ADD).then_inc(cnt.up(dve_done), 1)
                        tt(four(Xt[:, e, :]), four(Xt[:, e, :]), bc("ident"), ADD).then_inc(cnt.up(inverse_ready if e else dve_done), 1)
                    for e in range(2):
                        dve.wait_ge(psum_ready, finished(("M", l, hp, e)))
                        b = bank(("M", l, hp, e))
                        tt(four(A(51 + e)[:, 0, :]), four(b[:, :]), bc("upper_strict"), MUL).then_inc(cnt.up(dve_released), 1)
                    for n in range(len(LEVELS)):
                        for e in range(2):
                            dve.wait_ge(psum_ready, finished(("Xt", l, hp, n, e)))
                            b = bank(("Xt", l, hp, n, e))
                            if n < len(LEVELS) - 1:
                                dve.wait_ge(psum_ready, finished(("X", l, hp, n, 1)))
                            last = n == len(LEVELS) - 1 and e
                            dve.wait_ge(cnt.sem, cnt.value)
                            tt(Xt[:, e, :], Xt[:, e, :], b[:, :], ADD).then_inc(cnt.up(dve_released), 1)
                        if n < len(LEVELS) - 1:
                            for e in range(2):
                                dve.wait_ge(psum_ready, finished(("X", l, hp, n, e)))
                                b = bank(("X", l, hp, n, e))
                                tt(X[:, e, :], X[:, e, :], b[:, :], ADD).then_inc(cnt.up(dve_released), 1)
                        dve.wait_ge(cnt.sem, cnt.value)
                        cp(stat[:, 0, 0:1], stat[:, 1, 0:1]).then_inc(cnt.up(inverse_ready), 1)
                state = flat(14, 3)
                U = A(31, 2).rearrange("p a (j d) -> p (a j) d", d=RW_DIM)
                SA = A(27, 2).rearrange("p a (j d) -> p (a j) d", d=RW_DIM)
                dve.wait_ge(*taken(("U", l, 1)))
                for c in range(NC):
                    j, r = c // 2, slice(64 * (c % 2), 64 * (c % 2) + 64)
                    if c:
                        for e in range(2):
                            dve.wait_ge(psum_ready, finished(("sa", l, c, e)))
                            b = bank(("sa", l, c, e))
                            by_pair = lambda x: x[r, j, :].rearrange("p (a e d) -> p a e d", a=2, e=2)[:, :, e, :]
                            tt(by_pair(SA), b[r, 0:P].rearrange("p (a d) -> p a d", a=2), by_pair(U), ADD).then_inc(cnt.up(dve_released), 1)
                        dve.wait_ge(cnt.sem, cnt.value)
                        cp(stat[:, 0, 0:1], stat[:, 1, 0:1]).then_inc(cnt.up(state_input_ready), 1)
                    else:
                        cp(SA[r, j, :], U[r, j, :]).then_inc(cnt.up(state_input_ready), 1)
                    if c < NC - 1:
                        dve.wait_ge(psum_ready, finished(("st", l, c)))
                        b = bank(("st", l, c))
                        new = state[:, (c + 1) * P:(c + 2) * P]
                        if c:
                            old = state[:, c * P:(c + 1) * P]
                            for hp in range(2):
                                hs = slice(hp * 64, hp * 64 + 64)
                                ins = stt(new[:, hs], old[:, hs], decay_end[:, hp, c:c + 1], b[:, hs], MUL, ADD)
                                if hp:
                                    ins.then_inc(cnt.up(dve_released), 1)
                                else:
                                    ins.then_inc(cnt.up(dve_done), 1)
                        else:
                            cp(new, b[:, 0:P]).then_inc(cnt.up(dve_released), 1)
                        dve.wait_ge(cnt.sem, cnt.value)
                        cp(stat[:, 0, 0:1], stat[:, 1, 0:1]).then_inc(cnt.up(state_ready), 1)
                for hp in range(2):
                    for e in range(2):
                        dve.wait_ge(psum_ready, finished(("RB", l, hp, e)))
                        b = bank(("RB", l, hp, e))
                        tt(four(A(17 + 2 * hp + e)[:, 0, :]), four(b[:, :]), bc("upper"), MUL).then_inc(cnt.up(dve_released), 1)
                        dve.wait_ge(psum_ready, finished(("RK", l, hp, e)))
                        b = bank(("RK", l, hp, e))
                        tt(four(A(21 + 2 * hp + e)[:, 0, :]), four(b[:, :]), bc("upper"), MUL).then_inc(cnt.up(dve_released), 1)
                for hp in range(2):
                    dve.wait_ge(psum_ready, finished(("ymean", l, hp)))
                    b = bank(("ymean", l, hp))
                    y = A(49 + hp)[:, 0, :]
                    stt(y, b[:, :], -1.0 / RW_HD, y, MUL, ADD).then_inc(cnt.up(dve_released), 1)
                    dve.wait_ge(cnt.sem, cnt.value)
                    cp(stat[:, 0, 0:1], stat[:, 1, 0:1]).then_inc(cnt.up(centred_ready), 1)
                for hp in range(2):
                    variance(("yvar", l, hp), 51 + hp, RW_HD, RW_GN_EPS)
                for hp in range(2):
                    invert(51 + hp)
                    y = A(49 + hp)[:, 0, :]
                    stt(y, y, pr(f"gn_w{l}", hp), A(51 + hp)[:, 0, :], MUL, MUL).then_inc(cnt.up(dve_done), 1)
                    dve.wait_ge(cnt.sem, cnt.value)
                    stt(y, y, pr(f"gn_b{l}", hp), A(37 + hp)[:, 0, :], ADD, ADD).then_inc(cnt.up(dve_done), 1)
                    dve.wait_ge(cnt.sem, cnt.value)
                    tt(A(hp)[:, 0, :], y, A(39 + hp)[:, 0, :], MUL).then_inc(cnt.up(mix_rw_ready if hp else dve_done), 1)

                for k in (4, 5, 6, 7, 2, 3, 0, 1):
                    low(25 + k, A(k)[:, 0, :], 17 + k)
                dve.wait_ge(cnt.sem, cnt.value)

                residual(lambda m: ("o", l, m), lambda m: f"out{l}_{m // 2}")
                prepare(f"gu{l}_0")
                norm(("ffn", l), f"ffn_norm{l}")

                def ff_low(j):
                    low(FF_LOW[j % FH], A(2 + j % 2)[:, 0, :], FF_HIGH[j % FH])

                for half in range(2):
                    for j in range(half * FH, (half + 1) * FH):
                        prepare(f"gu{l}_{j}")
                        dve.wait_ge(psum_ready, finished(("up", l, j)))
                        b = bank(("up", l, j))
                        dve.wait_ge(*taken(("gate", l, j)))
                        if j % FH > 1:
                            dve.wait_ge(cnt.sem, cnt.value)
                        tt(A(2 + j % 2)[:, 0, :], A(j % 2)[:, 0, :], b[:, :], MUL).then_inc(cnt.up(dve_released), 1)
                        if j % FH:
                            ff_low(j - 1)
                    prepare(f"down{l}_0_{half}")
                    dve.wait_ge(cnt.sem, cnt.value)
                    ff_low((half + 1) * FH - 1)
                    if half == 0:
                        for m in range(DT):
                            prepare(f"down{l}_{m}_0")
                            dve.wait_ge(psum_ready, finished(("down", l, m, 0)))
                            b = bank(("down", l, m, 0))
                            tt(h[:, m, :], h[:, m, :], b[:, :], ADD).then_inc(cnt.up(dve_released), 1)
                residual(lambda m: ("down", l, m, 1), lambda m: f"down{l}_{m}_1")

            variance(("ss", "final"), 52, D, EPS)
            invert(52)
            for m in range(DT):
                stt(h[:, m, :], h[:, m, :], pr("final_norm", m), A(52)[:, 0, :], MUL, MUL).then_inc(cnt.up(residual_ready), 1)

            sum_squares()
            norm("even", "even_pre")
            xa, xg = flat(16, 3)[:, 0:T + 3], flat(16, 3)[:, T + 3:2 * T + 5]
            dve.memset(xa[:, 0:2], 0.0).then_inc(cnt.up(dve_done), 1)
            dve.memset(xa[:, T + 2:T + 3], 0.0).then_inc(cnt.up(dve_done), 1)
            dve.memset(xg[:, 0:1], 0.0).then_inc(cnt.up(dve_done), 1)
            dve.memset(xg[:, T + 1:T + 2], 0.0).then_inc(cnt.up(dve_done), 1)
            dve.wait_ge(cnt.sem, cnt.value)

            def gated(m):
                ua = A(19 + m % 2)[:, 0, :]
                for d in range(2):
                    i = A(27 + 2 * d)[:, 0, :]
                    dve.wait_ge(*taken(("gate_ri", m, d, 1)))
                    tt(i, i, ua, MUL).then_inc(cnt.up(dve_done), 1)
                for d in range(2):
                    dve.wait_ge(conv_padded, cnt.next(conv_padded))
                    t = A(48 + d)[:, 0, :]
                    stt(t, A(26 + 2 * d)[:, 0, :], 1.0, t, ADD, MUL).then_inc(cnt.up(sqrt_ready), 1)
                for d in range(2):
                    dve.wait_ge(ebuf_used, cnt.next(ebuf_used))
                    i = A(27 + 2 * d)[:, 0, :]
                    tt(i, i, A(48 + d)[:, 0, :], MUL).then_inc(cnt.up(dve_done), 1)
                    dve.wait_ge(cnt.sem, cnt.value)
                    step = slice(None) if d == 0 else slice(None, None, -1)
                    dve.tensor_tensor_scan(A(50 + d)[:, 0, step], rg_a(d)[:, step], i[:, step], 0.0,
                                                  MUL, ADD).then_inc(cnt.up(gated_ready if d else dve_done), 1)
                dve.wait_ge(cnt.sem, cnt.value)
                tt(A(50)[:, 0, :], A(50)[:, 0, :], A(51)[:, 0, :], ADD).then_inc(cnt.up(dve_done), 1)
                dve.wait_ge(cnt.sem, cnt.value)
                tt(A(m)[:, 0, :], A(50)[:, 0, :], A(21 + m % 2)[:, 0, :], MUL).then_inc(cnt.up(mix_even_ready), 1)

            for m in range(DT):
                ua = A(19 + m % 2)[:, 0, :]
                prepare(f"even_xa_za{m}")
                dve.wait_ge(*taken(("xa", m)))
                ts(ua, xa[:, 0:T], pr("conv_w", m), pr("conv_b", m), MUL, ADD).then_inc(cnt.up(dve_done), 1)
                for k in range(1, 4):
                    dve.wait_ge(cnt.sem, cnt.value)
                    stt(ua, xa[:, k:k + T], pr("conv_w", k * DT + m), ua, MUL, ADD).then_inc(cnt.up(conv_ready if k == 3 else dve_done), 1)
                c, yb = A(24)[:, 0, :], A(DT + m)[:, 0, :]
                prepare(f"even_xb_gc{m}")
                dve.wait_ge(psum_ready, finished(("gc", m)))
                b = bank(("gc", m))
                dve.wait_ge(*taken(("xb", m)))
                tt(xg[:, 1:1 + T], b[:, :], A(23)[:, 0, :], MUL).then_inc(cnt.up(dve_released), 1)
                dve.wait_ge(cnt.sem, cnt.value)
                ts(c, xg[:, 0:T], pr("sc_w", m), None, MUL).then_inc(cnt.up(dve_done), 1)
                for k in range(1, 3):
                    dve.wait_ge(cnt.sem, cnt.value)
                    stt(c, xg[:, k:k + T], pr("sc_w", k * DT + m), c, MUL, ADD).then_inc(cnt.up(dve_done), 1)
                dve.wait_ge(cnt.sem, cnt.value)
                prepare(f"even_gb_zb{m}")
                dve.wait_ge(psum_ready, finished(("gb", m)))
                b = bank(("gb", m))
                tt(yb, b[:, :], c, MUL).then_inc(cnt.up(dve_released), 1)
                dve.wait_ge(cnt.sem, cnt.value)
                dve.wait_ge(*taken(("zb", m)))
                tt(yb, yb, A(25)[:, 0, :], MUL).then_inc(cnt.up(silu_used), 1)
                if m:
                    gated(m - 1)
            gated(DT - 1)
            for k in list(range(DT, 2 * DT)) + list(range(DT)):
                low(32 + k, A(k)[:, 0, :], 16 + k)

            def post_norm(tag, gain, signal, slab_of, base):
                sum_squares(lambda m: prepare(slab_of(m)))
                variance(("ss", tag), 52, D, EPS)
                invert(52)
                for m in range(DT):
                    y = A(base + m)[:, 0, :]
                    stt(y, y, pr(gain, m), A(52)[:, 0, :], MUL, MUL).then_inc(cnt.up(dve_done), 1)
                dve.wait_ge(cnt.sem, cnt.value)
                for m in range(DT):
                    tt(h[:, m, :], h[:, m, :], A(base + m)[:, 0, :], ADD).then_inc(cnt.up(signal), 1)

            post_norm("even_post", "even_post", residual_ready, lambda m: f"even_out{m}", 0)
            sum_squares()
            norm("odd", "odd_pre")
            for m in range(4):
                prepare(f"odd_qk{m}")
            for m in range(4):
                prepare(f"odd_v{m}")
            prepare("odd_lr")
            for m in range(4):
                prepare(f"odd_r{m}")

            def gla_inputs(hd):
                for d in range(2):
                    dve.wait_ge(psum_ready, finished(("gz", hd, d)))
                    b = bank(("gz", hd, d))
                    g, z = gla_t(hd, d, 0), gla_t(hd, d, 1)
                    ts(g, b[:, :], pr("b_gate", d * GLA_H + hd), 0.0, ADD, MIN).then_inc(cnt.up(dve_done), 1)
                    ts(z, b[:, :], pr("b_gate", d * GLA_H + hd), 0.0, ADD, MAX).then_inc(cnt.up(dve_released), 1)
                    dve.wait_ge(cnt.sem, cnt.value)
                    tt(z, z, g, SUB).then_inc(cnt.up(gla_min_ready), 1)
                for d in range(2):
                    dve.wait_ge(gla_log_ready, cnt.next(gla_log_ready))
                    g, z, cum = gla_t(hd, d, 0), gla_t(hd, d, 1), gla_t(hd, d, 2)
                    tt(cum, g, z, SUB).then_inc(cnt.up(dve_done), 1)
                    dve.wait_ge(cnt.sem, cnt.value)
                    step = slice(None) if d == 0 else slice(None, None, -1)
                    dve.tensor_tensor_scan(g[:, step], cst("carry"), cum[:, step], 0.0, MUL, ADD).then_inc(cnt.up(gla_cum_ready), 1)
                for d in range(2):
                    dve.wait_ge(gla_exps_ready, cnt.next(gla_exps_ready))
                    kst, q, k = (gla_t(hd, d, i) for i in range(3))
                    dve.wait_ge(*taken(("qk", 7)))
                    tt(q, q, A(hd)[:, 0, :], MUL).then_inc(cnt.up(dve_done), 1)
                    tt(k, k, A(4 + hd)[:, 0, :], MUL).then_inc(cnt.up(dve_done), 1)
                    dve.wait_ge(cnt.sem, cnt.value)
                    end = gla_dec[:, hd % 2, d, :, None].broadcast_to((P, NC, GLA_CHUNK))
                    ch = lambda ap: ap.rearrange("p (c t) -> p c t", t=GLA_CHUNK)
                    tt(ch(kst), ch(k), end, MUL).then_inc(cnt.up(gla_inputs_ready if d else dve_done), 1)

            def bc4(name):
                return cst(name)[:, None, :].broadcast_to((P, NT, P))

            gla_inputs(0)
            for hd in range(GLA_H):
                if hd + 1 < GLA_H:
                    gla_inputs(hd + 1)
                f4 = lambda ap: ap.rearrange("p (j t) -> p j t", t=P)
                dve.wait_ge(psum_ready, finished(("gs", hd, 0)))
                b = bank(("gs", hd, 0))
                tt(f4(A(39)[:, 0, :]), f4(b[:, :]), bc4("upper"), MUL).then_inc(cnt.up(dve_released), 1)
                dve.wait_ge(psum_ready, finished(("gs", hd, 1)))
                b = bank(("gs", hd, 1))
                tt(f4(A(40)[:, 0, :]), f4(b[:, :]), bc4("lower"), MUL).then_inc(cnt.up(dve_released), 1)
                dve.wait_ge(cnt.sem, cnt.value)
                tt(A(39)[:, 0, :], A(39)[:, 0, :], A(40)[:, 0, :], ADD).then_inc(cnt.up(gla_pt_ready), 1)
                for parts in (GLA_PARTS[0:2], GLA_PARTS[2:4]):
                    kv = {}
                    for steps in parts:
                        for d in range(2):
                            dve.wait_ge(psum_ready, finished(("gkv", hd, d, steps)))
                            b = bank(("gkv", hd, d, steps))
                            for i, step in enumerate(steps):
                                kv[d, step] = b[:, i * 256:(i + 1) * 256], step == steps[-1]
                    for step in sorted({step for steps in parts for step in steps}):
                        dve.wait_ge(cnt.sem, cnt.value)
                        for d in range(2):
                            c = step if d == 0 else NC - 1 - step
                            fresh, last = kv[d, step]
                            new = gla_state(d, step + 1)
                            if step:
                                ins = stt(new, gla_state(d, step), gla_dec[:, hd % 2, d, c:c + 1], fresh, MUL, ADD)
                            else:
                                ins = cp(new, fresh)
                            if last:
                                ins.then_inc(cnt.up(dve_released), 1)
                            else:
                                ins.then_inc(cnt.up(dve_done), 1)
                dve.wait_ge(cnt.sem, cnt.value)
                cp(stat[:, 0, 0:1], stat[:, 1, 0:1]).then_inc(cnt.up(gla_state_ready), 1)
                variance(("gss", hd), 52, GLA_DV, EPS)
                invert(52)
                for eh in range(2):
                    o = A(48 + eh)[:, 0, :]
                    stt(o, o, pr("gla_norm", eh), A(52)[:, 0, :], MUL, MUL).then_inc(cnt.up(dve_done), 1)
                dve.wait_ge(cnt.sem, cnt.value)
                for eh in range(2):
                    m = 2 * hd + eh
                    tt(A(gla_mix(m))[:, 0, :], A(48 + eh)[:, 0, :], A(16 + m)[:, 0, :], MUL).then_inc(cnt.up(gla_mix_ready if eh else dve_done), 1)
                dve.wait_ge(cnt.sem, cnt.value)
                cp(stat[:, 0, 0:1], stat[:, 1, 0:1]).then_inc(cnt.up(gla_o_used), 1)
            for k in range(DT):
                low(33 + k, A(gla_mix(k))[:, 0, :], 25 + k)
            post_norm("odd_post", "odd_post", output_ready, lambda m: f"odd_out{m // 2}", 8)

        @block.gpsimd
        def _(pool):
            cnt = Count()
            pool.wait_ge(con_loaded, 16)
            for l in range(DEPTH):
                pool.wait_ge(krope_ready, cnt.next(krope_ready))
                src = A(31)[64:96]
                pool.tensor_copy(A(32, 7)[64:96], src.broadcast_to((32, 7, T))).then_inc(cnt.up(krope_spread), 1)
                for hp in range(2):
                    pool.wait_ge(*taken(("L", l, hp, 1)))
                    for n, b in enumerate(LEVELS):
                        if n:
                            pool.wait_ge(psum_ready, finished(("T1", l, hp, n - 1, 1)))
                        mask = cst(f"lower_off{b}")[:, None, :].broadcast_to((P, 2 * NT, P))
                        pool.tensor_tensor(A(19, 2).rearrange("p e (j t) -> p (e j) t", t=P),
                                                  A(17, 2).rearrange("p e (j t) -> p (e j) t", t=P), mask,
                                                  ALU.mult).then_inc(cnt.up(lower_off_ready), 1)

        @block.sync
        def _(sp):
            cnt = Count()
            sp.dma_start(A(0)[:, 0, :].bitcast(I32), pos_in).then_inc(pos_loaded, 16)
            sp.dma_start(con[:, :], con_in).then_inc(con_loaded, 16)
            sp.dma_start(par[:, :], par_in).then_inc(par_loaded, 16)
            sp.dma_start(h[:, :, :], x_in).then_inc(x_loaded, 16)
            sp.dma_start(small[:, :], small_in).then_inc(small_loaded, 16)
            at = 0
            for n, (name, cols) in enumerate(plan):
                if n >= SLOTS:
                    before = plan[n - SLOTS][0]
                    if is_split(before):
                        sp.wait_ge(slab_split, split_index[before] + 1)
                    else:
                        sp.wait_ge(psum_ready, slab_group[n - SLOTS] + 1)
                src = slabs_in[at:at + P * cols].rearrange("(p n) -> p n", p=P)
                sp.dma_start(ring[:, n % SLOTS, 0:cols], src).then_inc(slab_loaded[n % SLOTS], 16)
                at += P * cols
            sp.wait_ge(output_ready, cnt.next(output_ready, DT))
            sp.dma_start(out, h[:, :, :]).then_inc(stored, 16)
            sp.wait_ge(stored, 16)


def kernel(**inputs):
    import concourse.bacc as bacc
    from concourse.bass_utils import run_bass_kernel_spmd

    x = {k: np.asarray(v) for k, v in inputs.items()}
    arrays = {
        "x_in": np.ascontiguousarray(x["x"][0].T.reshape(DT, P, T).transpose(1, 0, 2)),
        "pos_in": np.ascontiguousarray(np.broadcast_to(x["positions"].reshape(1, T), (P, T))),
        "slabs_in": pack_slabs(x),
        "par_in": pack_params(x),
        "small_in": pack_small(x),
        "con_in": constants(),
    }
    nc = bacc.Bacc("TRN2", target_bir_lowering=False, num_devices=1)
    args = [nc.dram_tensor(k, a.shape, mybir.dt.from_np(a.dtype), kind="ExternalInput").ap() for k, a in arrays.items()]
    out = nc.dram_tensor("out", (P, DT, T), F32, kind="ExternalOutput").ap()
    two_blocks(nc, *args, out)
    r = run_bass_kernel_spmd(nc, [arrays], core_ids=[0])
    y = r.results[0]["out"]
    return y.transpose(1, 0, 2).reshape(1, D, T).transpose(0, 2, 1)
```

```python
from contextlib import ExitStack

import numpy as np
import concourse.bass as bass
from concourse import mybir

ALU = mybir.AluOpType
ACT = mybir.ActivationFunctionType
F32 = mybir.dt.float32
F32R = mybir.dt.float32r
I32 = mybir.dt.int32
AX_X = mybir.AxisListType.X

P = 128
D = 1024
T = 512
NT = T // P
DT = D // P
DEPTH = 2
EPS = 1e-6

RW_H, RW_HD = 4, 64
RW_DIM = RW_H * RW_HD
RW_HP = RW_DIM // P
RW_PA = 7
RW_GN_EPS = 64e-5
RW_CHUNK = 64
NC = T // RW_CHUNK
HALF_E = float(np.exp(-0.5))

RET_H = 4
MLA_H, MLA_NOPE, MLA_ROPE, MLA_V = 8, 64, 32, 64
MLA_QK = MLA_NOPE + MLA_ROPE
QT, KVT = 3, 2
Q_RANK, KV_RANK = QT * P, KVT * P
MLA_SCALE = MLA_QK ** -0.5
D_FF = 2816
FT = D_FF // P
FH = FT // 2
GLA_H, GLA_DV = 4, 256
GLA_CHUNK = 64

BANKS = 8
SLOTS = 2
SLOT = 2048
NEG = -3.0e38
LEVELS = (2, 4, 8, 16, 32)
GLA_PARTS = ((0, 2), (1, 3), (5,), (4, 6))

PAR = {}


def _par(name, n):
    PAR[name] = (sum(c for _, c in PAR.values()), n)


for _l in range(DEPTH):
    for _name, _n in (("attn_norm", DT), ("mu", RW_PA), ("w0", 2), ("a0", 2), ("k_k", 2), ("k_a", 2),
                      ("r_k", 2), ("gn_w", 2), ("gn_b", 2), ("v0", 2), ("q_norm", QT), ("kv_norm", KVT),
                      ("ffn_norm", DT)):
        _par(f"{_name}{_l}", _n)
_par("final_norm", DT)
for _name, _n in (("even_pre", DT), ("even_post", DT), ("conv_w", 4 * DT), ("conv_b", DT), ("gate_b", 4 * DT),
                  ("lam", 2 * DT), ("sc_w", 3 * DT), ("odd_pre", DT), ("odd_post", DT), ("b_gate", 2 * GLA_H),
                  ("gla_norm", 2)):
    _par(_name, _n)
NPAR = sum(c for _, c in PAR.values())

CON = {}


def _con(name, n):
    CON[name] = (sum(c for _, c in CON.values()), n)


_con("ident", P)
_con("ones", P)
_con("inv_freq", 2)
_con("ones_eps", P)
FIRST_CON = 3 * P + 2
for _name in ("ones64", "rot_ret", "upper", "upper_strict", "lower", "lower_strict",
              "upper_pair", "lower_pair", "causal"):
    _con(_name, P)
for _b in LEVELS:
    _con(f"lower_off{_b}", P)
_con("rot_mla", MLA_ROPE)
_con("decay", RET_H * T)
_con("carry", T)
NCON = sum(c for _, c in CON.values())


def constants():
    c = np.zeros((P, NCON), np.float32)

    def put(name, a):
        o, n = CON[name]
        c[:, o:o + n] = a

    i = np.arange(P)
    row, col = i[:, None], i[None, :]
    same = row // RW_CHUNK == col // RW_CHUNK
    put("ident", np.eye(P))
    put("ones", 1.0)
    put("ones_eps", EPS)
    put("ones64", same)
    rot = np.zeros((P, P))
    for m in range(P):
        if m % 64 < 32:
            rot[m + 32, m] = -1.0
        else:
            rot[m - 32, m] = 1.0
    put("rot_ret", rot)
    rot = np.zeros((P, MLA_ROPE))
    for m in range(MLA_ROPE):
        if m < 16:
            rot[MLA_NOPE + m + 16, m] = -1.0
        else:
            rot[MLA_NOPE + m - 16, m] = 1.0
    put("rot_mla", rot)
    put("upper", same & (row <= col))
    put("upper_strict", same & (row < col))
    put("lower", same & (row >= col))
    put("lower_strict", same & (row > col))
    put("upper_pair", (row // 2 == col // 2) & (row < col))
    put("lower_pair", (row // 2 == col // 2) & (row > col))
    for b in LEVELS:
        put(f"lower_off{b}", (row // (2 * b) == col // (2 * b)) & (row // b > col // b))
    put("causal", np.where(col <= row, 0.0, NEG))
    inv = np.stack([
        np.float32(10000.0) ** (-(np.float32(2) * (i % 32).astype(np.float32)) / np.float32(64)),
        np.float32(10000.0) ** (-(np.float32(2) * (i % 16).astype(np.float32)) / np.float32(32)),
    ], axis=1)
    put("inv_freq", inv)
    gap = np.arange(T)[None, :] - i[:, None]
    for h in range(RET_H):
        o, _ = CON["decay"]
        gamma = 1.0 - 2.0 ** (-5.0 - h)
        c[:, o + h * T:o + (h + 1) * T] = np.where(gap >= 0, gamma ** np.maximum(gap, 0), 0.0) * 64 ** -0.5
    put("carry", (np.arange(T) % GLA_CHUNK != 0)[None, :])
    return c


def slab_plan():
    plan = []
    tile2 = 2 * DT * P
    for l in range(DEPTH):
        for n in ("r", "k", "v", "lo_mq0", "mq12", "mkv"):
            plan.append((f"in{l}_{n}", tile2))
        plan.append((f"in{l}_krope", DT * P))
        for n in ("rq", "rk", "rg"):
            plan.append((f"in{l}_{n}", tile2))
        plan.append((f"in{l}_rv", DT * RW_DIM))
        for n in range(2):
            plan.append((f"q_up{l}_{n}", 4 * QT * MLA_QK))
        plan.append((f"kv_up{l}", KVT * MLA_H * (MLA_NOPE + MLA_V)))
        for n in range(DT // 2):
            plan.append((f"out{l}_{n}", tile2))
        for half in range(2):
            for j in range(half * FH, (half + 1) * FH):
                plan.append((f"gu{l}_{j}", tile2))
            for m in range(DT):
                plan.append((f"down{l}_{m}_{half}", FH * P))
    for m in range(DT):
        plan.append((f"even_xa_za{m}", tile2))
        plan.append((f"even_xb_gc{m}", tile2))
        plan.append((f"even_gb_zb{m}", tile2))
    for m in range(DT):
        plan.append((f"even_out{m}", 2 * DT * P))
    for n in range(4):
        plan.append((f"odd_qk{n}", tile2))
    plan.append(("odd_lr", DT * P))
    for n in range(4):
        plan.append((f"odd_v{n}", DT * 256))
    for n in range(4):
        plan.append((f"odd_r{n}", tile2))
    for n in range(4):
        plan.append((f"odd_out{n}", tile2))
    return plan


def is_split(name):
    return not name.startswith(("q_up", "kv_up"))


def pack_slabs(x):

    def cols(w, start, n):
        k = w.shape[0] // P
        return np.transpose(w[:, start:start + n].reshape(k, P, n), (1, 0, 2)).reshape(P, k * n)

    def padded(w, start, n, at):
        z = np.zeros((P, w.shape[0] // P, P), np.float32)
        z[:, :, at:at + n] = cols(w, start, n).reshape(P, -1, n)
        return z.reshape(P, -1)

    def tiles(w, *starts):
        return np.concatenate([cols(w, s, P) for s in starts], axis=1)

    out = {}
    for l in range(DEPTH):
        w = x["w_in"][l]
        ret, mla = 896, 896 + 1024
        rq, rk, rv, rg = ret, ret + 256, ret + 512, ret + 768
        out[f"in{l}_r"] = tiles(w, 0, 128)
        out[f"in{l}_k"] = tiles(w, 256, 384)
        out[f"in{l}_v"] = tiles(w, 512, 640)
        out[f"in{l}_lo_mq0"] = tiles(w, 768, mla)
        for n, start in (("rq", rq), ("rk", rk), ("rg", rg)):
            out[f"in{l}_{n}"] = tiles(w, start, start + P)
        out[f"in{l}_mq12"] = tiles(w, mla + P, mla + 2 * P)
        out[f"in{l}_mkv"] = tiles(w, mla + Q_RANK, mla + Q_RANK + P)
        out[f"in{l}_krope"] = padded(w, mla + Q_RANK + KV_RANK, MLA_ROPE, 64)
        out[f"in{l}_rv"] = cols(w, rv, RW_DIM)
        q = x["mla_w_q_up"][l]
        for n in range(2):
            out[f"q_up{l}_{n}"] = np.concatenate([cols(q, h * MLA_QK, MLA_QK) for h in range(4 * n, 4 * n + 4)], 1)
        kv = x["mla_w_kv_up"][l].reshape(KV_RANK, MLA_H, MLA_NOPE + MLA_V)
        v = kv[:, :, MLA_NOPE:].reshape(KV_RANK, MLA_H * MLA_V)
        out[f"kv_up{l}"] = np.concatenate([cols(kv[:, h], 0, MLA_NOPE) for h in range(MLA_H)]
                                          + [cols(v, 0, MLA_H * MLA_V)], axis=1)
        for n in range(DT // 2):
            out[f"out{l}_{n}"] = tiles(x["w_out"][l], 2 * n * P, (2 * n + 1) * P)
        for j in range(FT):
            out[f"gu{l}_{j}"] = tiles(x["w_gate_up"][l], j * P, D_FF + j * P)
        for m in range(DT):
            for half in range(2):
                wd = x["w_down"][l][half * FH * P:(half + 1) * FH * P]
                out[f"down{l}_{m}_{half}"] = cols(wd, m * P, P)
    w = x["even_w_in_2"][0]
    for m in range(DT):
        xa, za, xb, gb, gc, zb = (n * D + m * P for n in range(6))
        out[f"even_xa_za{m}"] = tiles(w, xa, za)
        out[f"even_xb_gc{m}"] = tiles(w, xb, gc)
        out[f"even_gb_zb{m}"] = tiles(w, gb, zb)
        out[f"even_out{m}"] = cols(x["even_w_out_2"][0], m * P, P)
    w = x["odd_w_in_2"][0]
    for n in range(4):
        out[f"odd_qk{n}"] = tiles(w, 2 * n * P, (2 * n + 1) * P)
        out[f"odd_v{n}"] = cols(w, 1024 + n * 256, 256)
        out[f"odd_r{n}"] = tiles(w, 2048 + 2 * n * P, 2048 + (2 * n + 1) * P)
        out[f"odd_out{n}"] = tiles(x["odd_w_out_2"][0], 2 * n * P, (2 * n + 1) * P)
    out["odd_lr"] = padded(w, 3072, 32, 0)
    return np.concatenate([out[name].ravel() for name, _ in slab_plan()])


def pack_gates(x):
    return np.ascontiguousarray(x["rg_gate_w_2"][0].reshape(4, DT, P, P).transpose(2, 1, 0, 3).reshape(P, DT, 4 * P))


def pack_params(x):
    a = np.zeros((P, NPAR), np.float32)

    def put(name, v):
        o, n = PAR[name]
        a[:, o:o + n] = v.reshape(n, P).T

    for l in range(DEPTH):
        for name, src in (("attn_norm", "attn_norm"), ("mu", "rw_mu"), ("w0", "rw_w0"), ("a0", "rw_a0"),
                          ("k_k", "rw_k_k"), ("k_a", "rw_k_a"), ("r_k", "rw_r_k"), ("gn_w", "rw_gn_w"),
                          ("gn_b", "rw_gn_b"), ("q_norm", "mla_q_norm"), ("kv_norm", "mla_kv_norm"),
                          ("ffn_norm", "ffn_norm")):
            put(f"{name}{l}", x[src][l])
        if l:
            put(f"v0{l}", x["rw_v0"][l - 1])
    put("final_norm", x["final_norm"])
    put("even_pre", x["even_norm_pre_2"][0])
    put("even_post", x["even_norm_post_2"][0])
    put("conv_w", x["rg_conv_w_2"][0])
    put("conv_b", x["rg_conv_b_2"][0])
    put("gate_b", x["rg_gate_b_2"][0])
    put("lam", x["rg_lambda_2"][0])
    put("sc_w", x["sc_conv_w_2"][0])
    put("odd_pre", x["odd_norm_pre_2"][0])
    put("odd_post", x["odd_norm_post_2"][0])
    put("b_gate", x["gla_b_gate_2"][0])
    put("gla_norm", x["gla_norm_g_2"][0])
    return a


LORA, V1, V2, GLR = 0, 2 * RW_DIM, 2 * RW_DIM + 64, 2 * RW_DIM + 64 + RW_DIM
NSMALL = GLR + 2 * T


def pack_small(x):
    a = np.zeros((P, NSMALL), np.float32)
    for l in range(DEPTH):
        o = LORA + l * RW_DIM
        a[0:32, o:o + RW_DIM] = x["rw_w2"][l]
        a[32:64, o:o + RW_DIM] = x["rw_a2"][l]
        a[64:128, o:o + RW_DIM] = x["rw_g2"][l]
    a[:, V1:V1 + 64] = np.transpose(x["rw_v1"][0].reshape(2, P, 32), (1, 0, 2)).reshape(P, 64)
    a[0:32, V2:V2 + RW_DIM] = x["rw_v2"][0]
    for d in range(2):
        a[16 * d:16 * d + 16, GLR + d * T:GLR + (d + 1) * T] = x["gla_w_gate_lr_2"][0, d]
    return a


class Count:

    def __init__(self):
        self.given, self.seen = {}, {}
        self.sem, self.value = None, 0

    def up(self, sem):
        self.given[id(sem)] = self.given.get(id(sem), 0) + 1
        self.sem, self.value = sem, self.given[id(sem)]
        return sem

    def next(self, sem, n=1):
        self.seen[id(sem)] = self.seen.get(id(sem), 0) + n
        return self.seen[id(sem)]


def two_blocks(nc, x_in, pos_in, slabs_in, par_in, small_in, gates_in, con_in, out):
    with ExitStack() as ctx:
        def sb(name, shape, dt=F32):
            return ctx.enter_context(nc.sbuf_tensor(name, shape, dt))

        def sem(name):
            return ctx.enter_context(nc.semaphore(name))

        h = sb("h", [P, DT, T])
        ring = sb("ring", [P, SLOTS, SLOT])
        high_at = nc.sbuf_base
        ring_high = sb("ring_high", [P, SLOTS, SLOT], F32R)
        low_at = nc.sbuf_base
        ring_low = sb("ring_low", [P, SLOTS, SLOT], F32R)
        ring_high_plain = nc.alloc_sbuf_tensor_at("ring_high_plain", [P, SLOTS, SLOT], F32, offset=high_at)
        ring_low_plain = nc.alloc_sbuf_tensor_at("ring_low_plain", [P, SLOTS, SLOT], F32, offset=low_at)
        arena_at = nc.sbuf_base
        arena = sb("arena", [P, 53, T])
        arena_split = nc.alloc_sbuf_tensor_at("arena_split", [P, 53, T], F32R, offset=arena_at)
        con = sb("con", [P, NCON])
        par = sb("par", [P, NPAR])
        small = sb("small", [P, NSMALL])
        trig = sb("trig", [P, 4, T])
        omu = sb("omu", [P, DEPTH, RW_PA])
        oka = sb("oka", [P, DEPTH, 2])
        splus = sb("splus", [P, 2 * DT])
        sp_t = sb("sp_t", [P, 2, 2 * DT])
        stat = sb("stat", [P, 4, MLA_H * NT])
        both_gains = sb("both_gains", [P, DT])
        epsilon = sb("epsilon", [P, 4])
        decay_end = sb("decay_end", [P, 2, NC])
        gla_dec = sb("gla_dec", [P, 3, 2, NC])
        banks = [ctx.enter_context(nc.psum_tensor(f"bank{i}", [P, T], F32)) for i in range(BANKS)]

        def A(t, n=1):
            return arena[:, t:t + n, :]

        def R(t):
            return arena_split[:, t, :]

        def flat(t, n):
            return arena[:, t:t + n, :].rearrange("p a b -> p (a b)")

        def cst(name):
            o, n = CON[name]
            return con[:, o:o + n]

        def pr(name, m=0):
            o, _ = PAR[name]
            return par[:, o + m:o + m + 1]

        x_loaded = [sem(f"x_loaded{n}") for n in range(4)]
        ones_loaded = sem("ones_loaded")
        first_gates_loaded = sem("first_gates_loaded")
        pos_loaded, con_loaded, par_loaded, small_loaded, gates_loaded = (
            sem(n) for n in ("pos_loaded", "con_loaded", "par_loaded", "small_loaded",
                              "gates_loaded"))
        slab_high_ready, slab_split = sem("slab_high_ready"), sem("slab_split")
        high_ready, parts_ready = sem("high_ready"), sem("parts_ready")
        slab_loaded = [sem(f"slab_loaded{i}") for i in range(SLOTS)]
        psum_ready, act_released, dve_released = sem("psum_ready"), sem("act_released"), sem("dve_released")
        act_done, dve_done, pool_done = sem("act_done"), sem("dve_done"), sem("pool_done")
        released = {"act": act_released, "dve": dve_released}
        square_ready = sem("square_ready")
        residual_square_ready = sem("residual_square_ready")
        square_used = sem("square_used")
        squares_summed = sem("squares_summed")
        epsilon_ready = sem("epsilon_ready")
        value_ready = sem("value_ready")
        residual_ready = sem("residual_ready")
        output_ready = sem("output_ready")
        angle_ready = sem("angle_ready")
        sine_ready = sem("sine_ready")
        praw_used = sem("praw_used")
        shifted_ready = sem("shifted_ready")
        lora_ready = sem("lora_ready")
        latent_squares_ready = sem("latent_squares_ready")
        latent_ready = sem("latent_ready")
        krope_ready = sem("krope_ready")
        krope_spread = sem("krope_spread")
        qrope_ready = sem("qrope_ready")
        bias_ready = sem("bias_ready")
        ret_rope_ready = sem("ret_rope_ready")
        mix_ret_ready = sem("mix_ret_ready")
        kk_square_ready = sem("kk_square_ready")
        decay_summed = sem("decay_summed")
        decays_ready = sem("decays_ready")
        scan_inputs_ready = sem("scan_inputs_ready")
        values_ready = sem("values_ready")
        r_decayed, k_decayed, k_carried = sem("r_decayed"), sem("k_decayed"), sem("k_carried")
        bonus_product_ready = sem("bonus_product_ready")
        lower_off_ready = sem("lower_off_ready")
        inverse_ready = sem("inverse_ready")
        state_input_ready = sem("state_input_ready")
        state_ready = sem("state_ready")
        y_squares_ready = sem("y_squares_ready")
        mix_rw_ready = sem("mix_rw_ready")
        silu_used = sem("silu_used")
        conv_padded = sem("conv_padded")
        conv_ready = sem("conv_ready")
        sqrt_ready = sem("sqrt_ready")
        gated_ready = sem("gated_ready")
        mix_even_ready = sem("mix_even_ready")
        ebuf_used = sem("ebuf_used")
        lam_exp_ready = sem("lam_exp_ready")
        lam_ready = sem("lam_ready")
        gla_min_ready = sem("gla_min_ready")
        gla_log_ready = sem("gla_log_ready")
        gla_cum_ready = sem("gla_cum_ready")
        gla_exps_ready = sem("gla_exps_ready")
        gla_inputs_ready = sem("gla_inputs_ready")
        gla_pt_ready = sem("gla_pt_ready")
        gla_mix_ready = sem("gla_mix_ready")
        gla_o_used = sem("gla_o_used")
        stored = sem("stored")

        plan = slab_plan()
        slab_index = {name: n for n, (name, _) in enumerate(plan)}
        split_slabs = [name for name, _ in plan if is_split(name)]
        split_index = {name: n for n, name in enumerate(split_slabs)}
        HN_HIGH, HN_LOW = 31, 39
        MIX_ORDER = (4, 5, 6, 7, 2, 3, 0, 1)
        MIX_HIGH = {4: 33, 5: 34, 6: 35, 7: 36, 2: 31, 3: 32, 0: 25, 1: 26}
        EVEN_ORDER = (8, 9, 10, 11, 12, 13, 14, 0, 1, 2, 3, 4, 5, 6, 15, 7)
        FF_HIGH, FF_LOW = list(range(10, 21)), list(range(21, 31)) + [4]
        slab_group = {}
        book = {}
        order = []
        owned = {"act": [], "dve": []}

        def rg_a(d):
            return A((30, 47)[d])[:, 0, :]

        def ring_tile(side, n):
            return side[:, n // 4, n % 4 * T:(n % 4 + 1) * T]

        def gla_t(hd, d, i):
            n = 3 * d + i
            return ring_tile(ring_high_plain, n) if hd % 3 == 2 else A((25, 47)[hd % 3] + n)[:, 0, :]

        def gv(j):
            return flat(8 + 2 * j, 2)

        def gla_state(hd, d, n):
            o = (d * 7 + n - 1) * 256
            if hd % 2:
                return flat(35, 7)[:, o:o + 256]
            return ring_low_plain[:, o // SLOT, o % SLOT:o % SLOT + 256]

        GLA_KT, GLA_PT, GLA_O, GLA_SQ, GLA_DEV = 31, 33, 42, 44, 46

        def gla_mix(m):
            return m // 2 + 4 * (m % 2)

        def finished(key):
            return book[key][0] + 1

        def bank(key):
            return banks[book[key][0] % BANKS]

        def taken(key):
            _, who, count = book[key]
            return released[who], count

        block = ctx.enter_context(nc.Block())

        @block.tensor
        def _(pe):
            cnt = Count()

            def group(key, owner):
                n = len(order)
                if n >= BANKS:
                    _, who, count = book[order[n - BANKS]]
                    pe.wait_ge(released[who], count)
                owned[owner].append(key)
                book[key] = (n, owner, len(owned[owner]))
                order.append(key)
                return banks[n % BANKS]

            def slab(name):
                n = slab_index[name]
                slot = n % SLOTS
                pe.wait_ge(slab_loaded[slot], 16 * (n // SLOTS + 1))
                slab_group[n] = len(order)
                return ring[:, slot, :]

            def split_slab(name):
                slab_group[slab_index[name]] = len(order)
                n = split_index[name]
                pe.wait_ge(slab_split, n + 1)
                return ring_high[:, n % SLOTS, :], ring_low[:, n % SLOTS, :]

            def product(out, weight, right, start, stop):
                pe.matmul(out, weight[0], right[0], start=start, stop=False)
                pe.matmul(out, weight[0], right[1], start=False, stop=False)
                return pe.matmul(out, weight[1], right[0], start=False, stop=stop)

            def split_gemm(key, owner, weights, rights, step=None):
                b = group(key, owner)
                for k, (w, r) in enumerate(zip(weights, rights)):
                    if step:
                        step(k)
                    mm = product(b[:, :], w, r, k == 0, k == len(weights) - 1)
                mm.then_inc(psum_ready, 1)

            def parts(highs, lows):
                return [(R(a), R(b)) for a, b in zip(highs, lows)]

            def split_tiles(pair_of_views, first, kt):
                high, low = pair_of_views
                return [(high[:, first + k * P:first + (k + 1) * P], low[:, first + k * P:first + (k + 1) * P])
                        for k in range(kt)]

            def gemm(key, owner, out_rows, weights, rights, step=None, N=T):
                b = group(key, owner)
                for k, (w, r) in enumerate(zip(weights, rights)):
                    if step:
                        step(k)
                    mm = pe.matmul(b[out_rows, 0:N], w, r, start=(k == 0), stop=(k == len(weights) - 1))
                mm.then_inc(psum_ready, 1)

            hn_parts = parts(range(HN_HIGH, HN_HIGH + DT), range(HN_LOW, HN_LOW + DT))
            rows = slice(0, P)

            def wtiles(view, first, kt, m=P):
                return [view[:, first + k * m:first + (k + 1) * m] for k in range(kt)]

            def pair(name, keys, owners, step=None):
                for n, (key, owner) in enumerate(zip(keys, owners)):
                    split_gemm(key, owner, split_tiles(split_slab(name), n * DT * P, DT), hn_parts,
                               step if n == 0 else None)

            def parts_step(k):
                pe.wait_ge(parts_ready, cnt.next(parts_ready))

            def token_major(out, name, j, start, stop):
                high, low = split_slab(name)
                js = slice(j * P, (j + 1) * P)
                for k in range(DT):
                    ks = slice(k * 256, (k + 1) * 256)
                    mm = product(out, tuple(x[:, js] for x in hn_parts[k]), (high[:, ks], low[:, ks]),
                                 start and k == 0, stop and k == DT - 1)
                return mm

            def norm_sum(tag):
                pe.wait_ge(squares_summed, cnt.next(squares_summed))
                gemm(("ss", tag), "act", rows, [cst("ones")], [A(51)[:, 0, :]])

            def latent_norms(l):
                pe.wait_ge(con_loaded, 16)
                pe.wait_ge(small_loaded, 16)
                pe.wait_ge(latent_squares_ready, cnt.next(latent_squares_ready))
                gemm(("mqs", l), "act", rows, [cst("ones")] * QT, [A(m)[:, 0, :] for m in range(QT)])
                gemm(("mkvs", l), "act", rows, [cst("ones")] * KVT, [A(QT + m)[:, 0, :] for m in range(KVT)])
                gemm(("krot", l), "dve", slice(64, 96), [cst("rot_mla")[64:96, :]], [A(30)[64:96, 0, :]])

            def retention_rope(l):
                for i in range(4):
                    pe.wait_ge(*taken(("rqk", l, i)))
                    gemm(("rrot", l, i), "dve", rows, [cst("rot_ret")], [A(17 + i)[:, 0, :]])

            def low_rank(l, n, r):
                w = small[:, LORA + l * RW_DIM:LORA + (l + 1) * RW_DIM]
                for hp in range(2):
                    gemm(("z", l, n, hp), "act", rows, [w[r, hp * P:(hp + 1) * P]], [A(16)[r, 0, :]])

            def decay_and_rate(l):
                pe.wait_ge(lora_ready, cnt.next(lora_ready))
                low_rank(l, 0, slice(0, 32))
                low_rank(l, 1, slice(32, 64))

            def mla(l):
                q96, k96 = A(0, 8), A(31, 8)
                pe.wait_ge(latent_ready, cnt.next(latent_ready))
                for n in range(2):
                    v = slab(f"q_up{l}_{n}")
                    for i in range(4):
                        hd = 4 * n + i
                        v = slab(f"q_up{l}_{n}")
                        gemm(("q", l, hd), "act", slice(0, MLA_QK), wtiles(v, i * QT * MLA_QK, QT, MLA_QK),
                             [A(25 + k)[:, 0, :] for k in range(QT)])
                lat = [A(28 + k)[:, 0, :] for k in range(KVT)]
                for hd in range(MLA_H):
                    v = slab(f"kv_up{l}")
                    gemm(("kn", l, hd), "act", slice(0, 64), wtiles(v, hd * KVT * 64, KVT, 64), lat)
                    pe.wait_ge(*taken(("q", l, hd)))
                    gemm(("qrot", l, hd), "dve", slice(64, 96), [cst("rot_mla")[64:96, :]], [q96[64:96, hd, :]])
                for j in range(NT):
                    v = slab(f"kv_up{l}")
                    gemm(("vt", l, j), "act", rows, [r[:, j * P:(j + 1) * P] for r in lat],
                         wtiles(v, MLA_H * KVT * 64, KVT, T))
                decay_and_rate(l)
                pe.wait_ge(krope_spread, cnt.next(krope_spread))
                units = [(hd, i) for hd in range(MLA_H) for i in range(NT)]
                for u in range(len(units) + 3):
                    if u < len(units):
                        hd, i = units[u]
                        if i == 0:
                            pe.wait_ge(*taken(("kn", l, hd)))
                            pe.wait_ge(qrope_ready, cnt.next(qrope_ready))
                        gemm(("s", l, u), "act", rows, [q96[0:MLA_QK, hd, i * P:(i + 1) * P]],
                             [k96[0:MLA_QK, hd, 0:(i + 1) * P]], N=(i + 1) * P)
                    if 0 <= u - 2 < len(units):
                        w = u - 2
                        pe.wait_ge(*taken(("s", l, w)))
                        b = group(("t", l, w), "dve")
                        for j in range(units[w][1] + 1):
                            mm = pe.transpose(b[:, j * P:(j + 1) * P], A(47 + w % 3)[:, 0, j * P:(j + 1) * P],
                                              cst("ident"))
                        mm.then_inc(psum_ready, 1)
                    if 0 <= u - 3 < len(units):
                        w = u - 3
                        hd, i = units[w]
                        pe.wait_ge(*taken(("t", l, w)))
                        if w == 0:
                            pe.wait_ge(*taken(("vt", l, NT - 1)))
                        gemm(("pv", l, w), "dve", rows, [A(50 + w % 2)[:, 0, j * P:(j + 1) * P] for j in range(i + 1)],
                             [A(39 + j)[:, 0, hd * 64:(hd + 1) * 64] for j in range(i + 1)], N=64)
                if l:
                    gemm(("vlow", l), "act", slice(0, 32), [small[:, V1 + 32 * k:V1 + 32 * (k + 1)] for k in range(2)],
                         [A(14 + k)[:, 0, :] for k in range(2)])
                pe.wait_ge(kk_square_ready, cnt.next(kk_square_ready))
                for hp in range(2):
                    gemm(("kks", l, hp), "act", rows, [cst("ones64")], [A(hp)[:, 0, :]])
                pe.wait_ge(*taken(("pv", l, len(units) - 1)))
                for m in range(4):
                    b = group(("ot", l, m), "act")
                    for i in range(NT):
                        mm = pe.transpose(b[:, i * P:(i + 1) * P], A(43 + i)[:, 0, m * P:(m + 1) * P], cst("ident"))
                    mm.then_inc(psum_ready, 1)
                if l:
                    pe.wait_ge(*taken(("vlow", l)))
                    for hp in range(2):
                        gemm(("vgate", l, hp), "act", rows, [small[0:32, V2 + hp * P:V2 + (hp + 1) * P]],
                             [A(2)[0:32, 0, :]])

            def retention(l):
                for hp in range(2):
                    if hp == 0:
                        pe.wait_ge(ret_rope_ready, cnt.next(ret_rope_ready))
                    for e in range(2):
                        r = slice(64 * e, 64 * e + 64)
                        for j in range(NT):
                            gemm(("rs", l, 2 * hp + e, j), "dve", rows, [A(19 + hp)[r, 0, j * P:(j + 1) * P]],
                                 [A(17 + hp)[r, 0, j * P:T]], N=T - j * P)
                for hp in range(2):
                    b = group(("ry", l, hp), "act")
                    for e in range(2):
                        off = 0
                        for j in range(NT):
                            hd = 2 * hp + e
                            pe.wait_ge(*taken(("rs", l, hd, j)))
                            n = T - j * P
                            pt = flat(43 + 5 * hp, 5)[:, e * 1280 + off:e * 1280 + off + n]
                            mm = pe.matmul(b[64 * e:64 * e + 64, j * P:T],
                                           flat(21, 2)[:, j * RW_DIM + hd * 64:j * RW_DIM + (hd + 1) * 64], pt,
                                           start=(j == 0), stop=(j == NT - 1))
                            off += n
                    mm.then_inc(psum_ready, 1)
                for hp in range(2):
                    pe.wait_ge(*taken(("ry", l, hp)))
                    gemm(("rss", l, hp), "act", rows, [cst("ones64")], [A(41 + hp)[:, 0, :]])

            def rwkv(l):
                pe.wait_ge(bonus_product_ready, cnt.next(bonus_product_ready))
                for hp in range(2):
                    gemm(("bonus", l, hp), "dve", rows, [cst("ones64")], [A(37 + hp)[:, 0, :]])
                pe.wait_ge(scan_inputs_ready, cnt.next(scan_inputs_ready))
                pe.wait_ge(values_ready, cnt.next(values_ready))
                for n, src in enumerate((14, 33, 35, 27)):
                    if src == 27:
                        pe.wait_ge(k_carried, cnt.next(k_carried))
                    for hp in range(2):
                        b = group(("tok", l, n, hp), "act")
                        for j in range(NT):
                            mm = pe.transpose(b[:, j * P:(j + 1) * P], A(src + hp)[:, 0, j * P:(j + 1) * P],
                                              cst("ident"))
                        mm.then_inc(psum_ready, 1)
                Af, Bf, Kf, Rf = 33, 29, 12, 10

                def gram(key, owner, left, right, hp, e):
                    b = group(key, owner)
                    r = slice(64 * e, 64 * e + 64)
                    for j in range(NT):
                        mm = pe.matmul(b[:, j * P:(j + 1) * P], A(left + hp)[r, 0, j * P:(j + 1) * P],
                                       A(right + hp)[r, 0, j * P:(j + 1) * P], start=(j == 0), stop=(j == NT - 1))
                    mm.then_inc(psum_ready, 1)

                def tokm(t, j, hd):
                    return flat(t, 2)[:, j * RW_DIM + hd * 64:j * RW_DIM + (hd + 1) * 64]

                for hp in range(2):
                    for e in range(2):
                        gram(("L", l, hp, e), "act", Af, Bf, hp, e)
                        gram(("N", l, hp, e), "dve", Bf, Af, hp, e)
                    for e in range(2):
                        gram(("M", l, hp, e), "dve", Kf, Af, hp, e)
                    if hp == 0:
                        low_rank(l, 2, slice(64, 128))
                    Xt, X, Lo, T1 = A(23, 2), A(21, 2), A(19, 2), A(49, 2)
                    for n, b in enumerate(LEVELS):
                        pe.wait_ge(lower_off_ready, cnt.next(lower_off_ready))
                        for e in range(2):
                            if n:
                                pe.wait_ge(*taken(("Xt", l, hp, n - 1, e)))
                            else:
                                pe.wait_ge(inverse_ready, cnt.next(inverse_ready))
                            bk = group(("T1", l, hp, n, e), "act")
                            for j in range(NT):
                                js = slice(j * P, (j + 1) * P)
                                mm = pe.matmul(bk[:, js], Lo[:, e, js], Xt[:, e, js], start=(j == 0), stop=(j == 3))
                            mm.then_inc(psum_ready, 1)
                        for e in range(2):
                            pe.wait_ge(*taken(("T1", l, hp, n, e)))
                            if n:
                                pe.wait_ge(*taken(("X", l, hp, n - 1, e)))
                            bk = group(("Xt", l, hp, n, e), "dve")
                            for j in range(NT):
                                js = slice(j * P, (j + 1) * P)
                                mm = pe.matmul(bk[:, js], X[:, e, js], T1[:, e, js], start=(j == 0), stop=(j == 3))
                            mm.then_inc(psum_ready, 1)
                            if n < len(LEVELS) - 1:
                                bk = group(("X", l, hp, n, e), "dve")
                                for j in range(NT):
                                    js = slice(j * P, (j + 1) * P)
                                    mm = pe.matmul(bk[:, js], T1[:, e, js], X[:, e, js], start=(j == 0), stop=(j == 3))
                                mm.then_inc(psum_ready, 1)
                    for e in range(2):
                        pe.wait_ge(*taken(("Xt", l, hp, len(LEVELS) - 1, e)))
                    bk = group(("MV", l, hp), "act")
                    pe.wait_ge(*taken(("tok", l, 0, 1)))
                    for j in range(NT):
                        for e in range(2):
                            js = slice(j * P, (j + 1) * P)
                            c0 = j * P + e * 64
                            mm = pe.matmul(bk[:, c0:c0 + 64], A(51 + e)[:, 0, js], tokm(41, j, 2 * hp + e),
                                           start=(j == 0 and e == 0), stop=(j == 3 and e == 1))
                    mm.then_inc(psum_ready, 1)
                    bk = group(("WT", l, hp), "act")
                    for e in range(2):
                        for j in range(NT):
                            js = slice(j * P, (j + 1) * P)
                            mm = pe.matmul(bk[64 * e:64 * e + 64, js], tokm(43, j, 2 * hp + e), Xt[:, e, js],
                                           start=(j == 0), stop=(j == 3))
                    mm.then_inc(psum_ready, 1)
                    pe.wait_ge(*taken(("MV", l, hp)))
                    bk = group(("U", l, hp), "act")
                    for j in range(NT):
                        for e in range(2):
                            js = slice(j * P, (j + 1) * P)
                            c0 = j * P + e * 64
                            mm = pe.matmul(bk[:, c0:c0 + 64], Xt[:, e, js], A(35 + hp)[:, 0, c0:c0 + 64],
                                           start=(j == 0 and e == 0), stop=(j == 3 and e == 1))
                    mm.then_inc(psum_ready, 1)
                state = flat(14, 3)
                own = [(name, left, hp, e) for hp in range(2) for e in range(2) for name, left in (("RB", Bf), ("RK", Kf))]

                def own_scores(n):
                    name, left, hp, e = own[n]
                    gram((name, l, hp, e), "dve", left, Rf, hp, e)

                for c in range(NC):
                    j, r = c // 2, slice(64 * (c % 2), 64 * (c % 2) + 64)
                    cs = slice(c * 64, (c + 1) * 64)
                    if c:
                        pe.wait_ge(state_ready, cnt.next(state_ready))
                        for e in range(2):
                            bk = group(("sa", l, c, e), "dve")
                            er = slice(64 * e, 64 * e + 64)
                            for hp in range(2):
                                mm = pe.matmul(bk[r, hp * 64:(hp + 1) * 64], A(25 + hp)[er, 0, cs],
                                               state[er, c * P + hp * 64:c * P + (hp + 1) * 64],
                                               start=(hp == 0), stop=(hp == 1))
                            mm.then_inc(psum_ready, 1)
                        own_scores(c)
                    pe.wait_ge(state_input_ready, cnt.next(state_input_ready))
                    if c < NC - 1:
                        bk = group(("st", l, c), "dve")
                        for e in range(2):
                            for hp in range(2):
                                hd = 2 * hp + e
                                o = bk[64 * e:64 * e + 64, hp * 64:(hp + 1) * 64]
                                mm = pe.matmul(o, tokm(45, j, hd)[r], tokm(27, j, hd)[r], start=(hp == 0), stop=False)
                                mm = pe.matmul(o, tokm(47, j, hd)[r], tokm(41, j, hd)[r], start=False, stop=(hp == 1))
                        mm.then_inc(psum_ready, 1)
                    if c == 0:
                        own_scores(0)
                for hp in range(2):
                    bk = group(("y", l, hp), "act")
                    for e in range(2):
                        er, hd = slice(64 * e, 64 * e + 64), 2 * hp + e
                        pe.wait_ge(*taken(("RB", l, hp, e)))
                        pe.wait_ge(*taken(("RK", l, hp, e)))
                        for j in range(NT):
                            js = slice(j * P, (j + 1) * P)
                            pe.matmul(bk[er, js], tokm(27, j, hd), A(17 + 2 * hp + e)[:, 0, js], start=(j == 0), stop=False)
                            pe.matmul(bk[er, js], tokm(41, j, hd), A(21 + 2 * hp + e)[:, 0, js], start=False, stop=False)
                        for c in range(1, NC):
                            cs = slice(c * 64, (c + 1) * 64)
                            mm = pe.matmul(bk[er, cs], state[er, c * P + hp * 64:c * P + (hp + 1) * 64],
                                           A(Rf + hp)[er, 0, cs], start=False, stop=(c == NC - 1))
                    mm.then_inc(psum_ready, 1)
                for hp in range(2):
                    pe.wait_ge(*taken(("y", l, hp)))
                    gemm(("ymean", l, hp), "dve", rows, [cst("ones64")], [A(49 + hp)[:, 0, :]])
                for hp in range(2):
                    pe.wait_ge(y_squares_ready, cnt.next(y_squares_ready))
                    gemm(("yvar", l, hp), "act", rows, [cst("ones64")], [A(51 + hp)[:, 0, :]])

            pe.wait_ge(ones_loaded, 16)
            for l in range(DEPTH):
                norm_sum(("attn", l))
                pair(f"in{l}_r", [("pa", l, 0), ("pa", l, 1)], ["act"] * 2, parts_step)
                pair(f"in{l}_k", [("pa", l, 2), ("pa", l, 3)], ["act"] * 2)
                pair(f"in{l}_v", [("pa", l, 4), ("pa", l, 5)], ["act"] * 2)
                pair(f"in{l}_lo_mq0", [("pa", l, 6), ("lat", l, 0)], ["act"] * 2)
                pair(f"in{l}_mq12", [("lat", l, 1), ("lat", l, 2)], ["act"] * 2)
                pair(f"in{l}_mkv", [("lat", l, 3), ("lat", l, 4)], ["act"] * 2)
                split_gemm(("kr", l), "act", split_tiles(split_slab(f"in{l}_krope"), 0, DT), hn_parts)
                pair(f"in{l}_rq", [("rqk", l, 0), ("rqk", l, 1)], ["act"] * 2)
                latent_norms(l)
                pair(f"in{l}_rk", [("rqk", l, 2), ("rqk", l, 3)], ["act"] * 2)
                pair(f"in{l}_rg", [("rg", l, 0), ("rg", l, 1)], ["act"] * 2)
                retention_rope(l)
                for n in range(2):
                    b = group(("rv", l, n), "act")
                    for i in range(2):
                        slab_group[slab_index[f"in{l}_rv"]] = len(order) - 1
                        mm = token_major(b[:, i * 256:(i + 1) * 256], f"in{l}_rv", 2 * n + i, i == 0, i == 1)
                    slab_group[slab_index[f"in{l}_rv"]] = len(order) - 1
                    mm.then_inc(psum_ready, 1)
                mla(l)
                retention(l)
                rwkv(l)
                mix = dict(zip(MIX_ORDER, parts([MIX_HIGH[k] for k in MIX_ORDER], MIX_ORDER)))

                def out_weights(m):
                    return split_tiles(split_slab(f"out{l}_{m // 2}"), (m % 2) * DT * P, DT)

                held = []
                for m in range(DT // 2):
                    w = out_weights(m)
                    bk = group(("o", l, m), "dve")
                    held.append((bk, w))
                    for k in MIX_ORDER[:-2]:
                        if m == 0:
                            parts_step(k)
                        product(bk[:, :], w[k], mix[k], k == MIX_ORDER[0], False)
                for m, (bk, w) in enumerate(held):
                    for k in MIX_ORDER[-2:]:
                        if m == 0:
                            parts_step(k)
                        mm = product(bk[:, :], w[k], mix[k], False, k == MIX_ORDER[-1])
                    mm.then_inc(psum_ready, 1)
                for m in range(DT // 2, DT):
                    w = out_weights(m)
                    split_gemm(("o", l, m), "dve", [w[k] for k in MIX_ORDER], [mix[k] for k in MIX_ORDER])
                norm_sum(("ffn", l))
                for half in range(2):
                    for j in range(half * FH, (half + 1) * FH):
                        pair(f"gu{l}_{j}", [("gate", l, j), ("up", l, j)], ["act", "dve"], parts_step if j == 0 else None)
                    for m in range(DT):
                        split_gemm(("down", l, m, half), "dve", split_tiles(split_slab(f"down{l}_{m}_{half}"), 0, FH),
                                   parts(FF_HIGH, FF_LOW), parts_step if m == 0 else None)
            pe.wait_ge(squares_summed, cnt.next(squares_summed))
            gemm(("ss", "even"), "act", rows, [cst("ones"), cst("ones_eps")], [A(46)[:, 0, :], A(51)[:, 0, :]])
            gemm(("ss", "final"), "act", rows, [cst("ones")], [A(51)[:, 0, :]])

            def rg_gates(m):
                if m < 2:
                    pe.wait_ge(first_gates_loaded, 16)
                else:
                    pe.wait_ge(gates_loaded, 16)
                pe.wait_ge(conv_ready, cnt.next(conv_ready))
                for n in range(4):
                    w = A(m)[:, 0, n * P:(n + 1) * P]
                    gemm(("gate_ri", m, n // 2, n % 2), "act", rows, [w], [A(19 + m % 2)[:, 0, :]])

            for m in range(DT):
                pair(f"even_xa_za{m}", [("xa", m), ("za", m)], ["act"] * 2, parts_step if m == 0 else None)
                pair(f"even_xb_gc{m}", [("xb", m), ("gc", m)], ["act", "dve"])
                rg_gates(m)
                pair(f"even_gb_zb{m}", [("gb", m), ("zb", m)], ["dve", "act"])
            mix = dict(zip(EVEN_ORDER, parts([HN_HIGH + k for k in EVEN_ORDER], EVEN_ORDER)))
            held = []
            for m in range(2):
                w = split_tiles(split_slab(f"even_out{m}"), 0, 2 * DT)
                bk = group(("eo", m), "act")
                held.append((bk, w))
                for k in EVEN_ORDER[:-2]:
                    if m == 0:
                        parts_step(k)
                    product(bk[:, :], w[k], mix[k], k == EVEN_ORDER[0], False)
            for m, (bk, w) in enumerate(held):
                for k in EVEN_ORDER[-2:]:
                    if m == 0:
                        parts_step(k)
                    mm = product(bk[:, :], w[k], mix[k], False, k == EVEN_ORDER[-1])
                mm.then_inc(psum_ready, 1)
            for m in range(2, DT):
                w = split_tiles(split_slab(f"even_out{m}"), 0, 2 * DT)
                split_gemm(("eo", m), "act", [w[k] for k in EVEN_ORDER], [mix[k] for k in EVEN_ORDER])
            norm_sum("even_post")

            def square_step(m):
                pe.wait_ge(residual_square_ready, m + 1)

            gemm(("ss", "odd"), "act", rows, [cst("ones")] * DT, [A(m)[:, 0, :] for m in range(DT)], square_step)
            for n in range(4):
                pair(f"odd_qk{n}", [("qk", 2 * n), ("qk", 2 * n + 1)], ["act"] * 2, parts_step if n == 0 else None)
            split_gemm("lr", "act", split_tiles(split_slab("odd_lr"), 0, DT), hn_parts)

            def gla_gates(hd):
                pe.wait_ge(*taken("lr"))
                for d in range(2):
                    gemm(("gz", hd, d), "dve", rows, [small[0:32, GLR + d * T + hd * P:GLR + d * T + (hd + 1) * P]],
                         [A(24)[0:32, 0, :]])

            gla_gates(0)
            gla_gates(1)
            for n in range(4):
                for jj in range(2):
                    b = group(("gv", n, jj), "act")
                    for i in range(2):
                        mm = token_major(b[:, i * 256:(i + 1) * 256], f"odd_v{n}", 2 * jj + i, i == 0, i == 1)
                    slab_group[slab_index[f"odd_v{n}"]] = len(order) - 1
                    mm.then_inc(psum_ready, 1)
            for n in range(4):
                pair(f"odd_r{n}", [("gr", 2 * n), ("gr", 2 * n + 1)], ["act"] * 2)

            def gla_squares(hd):
                for eh in range(2):
                    pe.wait_ge(*taken(("go", hd, eh)))
                gemm(("gss", hd), "act", rows, [cst("ones")] * 2, [A(GLA_SQ + eh)[:, 0, :] for eh in range(2)])

            def gla_scores(hd):
                pe.wait_ge(gla_inputs_ready, cnt.next(gla_inputs_ready))
                for d in range(2):
                    b = group(("gs", hd, d), "dve")
                    for j in range(NT):
                        js = slice(j * P, (j + 1) * P)
                        mm = pe.matmul(b[:, js], gla_t(hd, d, 2)[:, js], gla_t(hd, d, 1)[:, js], start=(j == 0), stop=(j == NT - 1))
                    mm.then_inc(psum_ready, 1)
                for d in range(2):
                    b = group(("gkt", hd, d), "act")
                    for j in range(NT):
                        js = slice(j * P, (j + 1) * P)
                        mm = pe.transpose(b[:, js], gla_t(hd, d, 0)[:, js], cst("ident"))
                    mm.then_inc(psum_ready, 1)
                if hd >= 2:
                    gla_squares(hd - 2)
                for steps in GLA_PARTS:
                    for d in range(2):
                        pe.wait_ge(*taken(("gkt", hd, d)))
                        b = group(("gkv", hd, d, steps), "dve")
                        for i, step in enumerate(steps):
                            c = step if d == 0 else NC - 1 - step
                            j, r = c // 2, slice(64 * (c % 2), 64 * (c % 2) + 64)
                            mm = pe.matmul(b[:, i * 256:(i + 1) * 256], A(GLA_KT + d)[r, 0, j * P:(j + 1) * P],
                                           gv(j)[r, hd * 256:(hd + 1) * 256], start=(i == 0),
                                           stop=(i == len(steps) - 1))
                        mm.then_inc(psum_ready, 1)

            def gla_outputs(hd):
                pe.wait_ge(gla_pt_ready, cnt.next(gla_pt_ready))
                for d in range(2):
                    pe.wait_ge(*taken(("gkv", hd, d, GLA_PARTS[-1])))
                for eh in range(2):
                    b = group(("go", hd, eh), "act")
                    for j in range(NT):
                        js = slice(j * P, (j + 1) * P)
                        pe.matmul(b[:, js], gv(j)[:, hd * 256 + eh * P:hd * 256 + (eh + 1) * P], A(GLA_PT + hd % 2)[:, 0, js],
                                  start=(j == 0), stop=False)
                    for n in range(1, NC):
                        for d in range(2):
                            c = n if d == 0 else NC - 1 - n
                            s = gla_state(hd, d, n)
                            mm = pe.matmul(b[:, c * 64:(c + 1) * 64], s[:, eh * P:(eh + 1) * P],
                                           gla_t(hd, d, 1)[:, c * 64:(c + 1) * 64], start=False,
                                           stop=(n == NC - 1 and d == 1))
                    mm.then_inc(psum_ready, 1)

            gla_scores(0)
            gla_gates(2)
            gla_scores(1)
            gla_gates(3)
            gla_outputs(0)
            gla_scores(2)
            gla_outputs(1)
            gla_scores(3)
            gla_outputs(2)
            gla_squares(2)
            gla_outputs(3)
            gla_squares(3)
            mix = parts([16 + k for k in range(DT)], [gla_mix(k) for k in range(DT)])
            held = []
            for m in range(DT // 2):
                w = split_tiles(split_slab(f"odd_out{m // 2}"), (m % 2) * DT * P, DT)
                bk = group(("oo", m), "act")
                held.append((bk, w))
                for k in range(DT - 2):
                    if m == 0:
                        parts_step(k)
                    product(bk[:, :], w[k], mix[k], k == 0, False)
            for m, (bk, w) in enumerate(held):
                for k in range(DT - 2, DT):
                    if m == 0:
                        parts_step(k)
                    mm = product(bk[:, :], w[k], mix[k], False, k == DT - 1)
                mm.then_inc(psum_ready, 1)
            for m in range(DT // 2, DT):
                split_gemm(("oo", m), "act", split_tiles(split_slab(f"odd_out{m // 2}"), (m % 2) * DT * P, DT), mix)
            norm_sum("odd_post")

        @block.scalar
        def _(act):
            cnt = Count()
            f = act.activation

            def copy_out(key, dst, rows=slice(0, P), n=T, scale=1.0, func=ACT.Copy):
                act.wait_ge(psum_ready, finished(key))
                b = bank(key)
                f(dst, b[rows, 0:n], func, scale=scale).then_inc(cnt.up(act_released), 1)

            def squares(source, arrived):
                for m in range(DT):
                    arrived(m)
                    if m >= 2:
                        act.wait_ge(square_used, cnt.next(square_used))
                    f(A(49 + m % 2)[:, 0, :], source(m), ACT.Square).then_inc(cnt.up(square_ready), 1)
                act.wait_ge(square_used, cnt.next(square_used))

            def deviation(key, t, n, eps=0):
                act.wait_ge(psum_ready, finished(key))
                b = bank(key)
                f(A(t)[:, 0, :], b[:, :], ACT.Sqrt, bias=epsilon[:, eps:eps + 1],
                  scale=1.0 / n).then_inc(cnt.up(act_released), 1)

            splits = []

            def prepare(name):
                for n in range(len(splits), min(split_index[name] + 2, len(split_slabs))):
                    slab, cols = plan[slab_index[split_slabs[n]]]
                    at = slab_index[slab]
                    act.wait_ge(slab_loaded[at % SLOTS], 16 * (at // SLOTS + 1))
                    if n >= SLOTS:
                        act.wait_ge(psum_ready, slab_group[slab_index[split_slabs[n - SLOTS]]] + 1)
                    f(ring_high[:, n % SLOTS, 0:cols], ring[:, at % SLOTS, 0:cols],
                      ACT.Copy).then_inc(cnt.up(slab_high_ready), 1)
                    splits.append(slab)

            def high(dst, src):
                f(R(dst), src, ACT.Copy).then_inc(cnt.up(high_ready), 1)

            def hn_highs():
                for m in range(DT):
                    act.wait_ge(value_ready, cnt.next(value_ready))
                    high(HN_HIGH + m, A(47 + m % 2)[:, 0, :])

            h_tile = lambda m: h[:, m, :]
            act.wait_ge(epsilon_ready, cnt.next(epsilon_ready, 4))

            for l in range(DEPTH):
                if l == 0:
                    squares(h_tile, lambda m: act.wait_ge(x_loaded[m // 2], 16))
                prepare(f"in{l}_r")
                deviation(("ss", ("attn", l)), 52, D)
                hn_highs()
                if l == 0:
                    for n in range(2):
                        act.wait_ge(angle_ready, cnt.next(angle_ready))
                        f(trig[:, 2 * n + 1, :], trig[:, 2 * n, :], ACT.Sin).then_inc(cnt.up(act_done), 1)
                        act.wait_ge(cnt.sem, cnt.value)
                        f(trig[:, 2 * n, :], trig[:, 2 * n, :], ACT.Sin, scale=0.5).then_inc(cnt.up(act_done), 1)
                        act.wait_ge(cnt.sem, cnt.value)
                        f(trig[:, 2 * n, :], trig[:, 2 * n, :], ACT.Square).then_inc(cnt.up(sine_ready), 1)
                praw = flat(47, 4)
                for m in range(RW_PA):
                    if m % 2 == 0 and m:
                        prepare(f"in{l}_" + ("r", "k", "v", "lo_mq0")[m // 2])
                    if m >= 3:
                        act.wait_ge(praw_used, cnt.next(praw_used))
                    o = (m % 3) * 513 + 1
                    copy_out(("pa", l, m), praw[:, o:o + T])
                for m in range(QT + KVT):
                    if m == 1:
                        prepare(f"in{l}_mq12")
                    if m == 3:
                        prepare(f"in{l}_mkv")
                    copy_out(("lat", l, m), A(25 + m)[:, 0, :])
                prepare(f"in{l}_krope")
                copy_out(("kr", l), A(30)[64:96, 0, :], rows=slice(64, 96))
                act.wait_ge(cnt.sem, cnt.value)
                for m in range(QT + KVT):
                    ins = f(A(m)[:, 0, :], A(25 + m)[:, 0, :], ACT.Square)
                    ins.then_inc(cnt.up(latent_squares_ready if m == QT + KVT - 1 else act_done), 1)
                prepare(f"in{l}_rq")
                copy_out(("rqk", l, 0), A(17)[:, 0, :])
                copy_out(("rqk", l, 1), A(18)[:, 0, :])
                deviation(("mqs", l), 51, Q_RANK)
                deviation(("mkvs", l), 52, KV_RANK)
                prepare(f"in{l}_rk")
                copy_out(("rqk", l, 2), A(19)[:, 0, :])
                copy_out(("rqk", l, 3), A(20)[:, 0, :])
                prepare(f"in{l}_rg")
                copy_out(("rg", l, 0), A(23)[:, 0, :], func=ACT.Silu)
                copy_out(("rg", l, 1), A(24)[:, 0, :], func=ACT.Silu)
                for n in range(2):
                    copy_out(("rv", l, n), A(21 + n)[:, 0, :])
                lo = A(16)
                act.wait_ge(shifted_ready, cnt.next(shifted_ready))
                f(lo[0:32, 0, :], lo[0:32, 0, :], ACT.Tanh).then_inc(cnt.up(act_done), 1)
                f(lo[64:128, 0, :], lo[64:128, 0, :], ACT.Sigmoid).then_inc(cnt.up(lora_ready), 1)
                if l == 0:
                    act.wait_ge(par_loaded, 16)
                    act.wait_ge(lam_exp_ready, cnt.next(lam_exp_ready))
                    f(sp_t[:, 0, :], sp_t[:, 0, :], ACT.Exp, scale=-1.0).then_inc(cnt.up(lam_ready), 1)

                for hd in range(MLA_H):
                    if hd == 4:
                        act.wait_ge(ret_rope_ready, cnt.next(ret_rope_ready))
                    copy_out(("q", l, hd), A(hd)[0:MLA_QK, 0, :], rows=slice(0, MLA_QK))
                for hd in range(MLA_H):
                    copy_out(("kn", l, hd), A(31 + hd)[0:64, 0, :], rows=slice(0, 64))
                for j in range(NT):
                    copy_out(("vt", l, j), A(39 + j)[:, 0, :])
                act.wait_ge(krope_spread, cnt.next(krope_spread))
                for n, (dst, bias) in enumerate(((25, "w0"), (29, "a0"))):
                    for hp in range(2):
                        act.wait_ge(psum_ready, finished(("z", l, n, hp)))
                        b = bank(("z", l, n, hp))
                        f(A(dst + hp)[:, 0, :], b[:, :], ACT.Sigmoid, bias=pr(f"{bias}{l}", hp)).then_inc(cnt.up(act_released), 1)
                act.wait_ge(praw_used, cnt.next(praw_used, 3))
                for u in range(MLA_H * NT):
                    act.wait_ge(psum_ready, finished(("s", l, u)))
                    b = bank(("s", l, u))
                    n = (u % NT + 1) * P
                    act.wait_ge(bias_ready, cnt.next(bias_ready))
                    if u >= 3:
                        act.wait_ge(psum_ready, finished(("t", l, u - 3)))
                    f(A(47 + u % 3)[:, 0, 0:n], b[:, 0:n], ACT.Exp, bias=stat[:, 1, u:u + 1],
                                 scale=MLA_SCALE, accum_out=stat[:, 2, u:u + 1]).then_inc(cnt.up(act_released), 1)
                for hp in range(2):
                    ins = f(A(hp)[:, 0, :], A(12 + hp)[:, 0, :], ACT.Square, scale=pr(f"k_k{l}", hp))
                    ins.then_inc(cnt.up(kk_square_ready if hp else act_done), 1)
                act.wait_ge(decay_summed, cnt.next(decay_summed))
                f(A(33, 2), A(25, 2), ACT.Exp, scale=-HALF_E).then_inc(cnt.up(decays_ready), 1)
                f(A(35, 2), A(27, 2), ACT.Exp, scale=HALF_E).then_inc(cnt.up(decays_ready), 1)
                f(decay_end[:, :, :], A(27, 2).rearrange("p a (c t) -> p a c t", t=RW_CHUNK)[:, :, :, RW_CHUNK - 1],
                         ACT.Exp, scale=-HALF_E).then_inc(cnt.up(decays_ready), 1)
                act.wait_ge(cnt.sem, cnt.value)
                f(A(27, 2), A(27, 2), ACT.Exp, scale=-HALF_E).then_inc(cnt.up(decays_ready), 1)
                if l:
                    copy_out(("vlow", l), A(2)[0:32, 0, :], rows=slice(0, 32))
                for hp in range(2):
                    deviation(("kks", l, hp), 31 + hp, 1, 2)
                for m in range(4):
                    copy_out(("ot", l, m), A(4 + m)[:, 0, :])
                if l:
                    for hp in range(2):
                        act.wait_ge(psum_ready, finished(("vgate", l, hp)))
                        b = bank(("vgate", l, hp))
                        f(A(hp)[:, 0, :], b[:, :], ACT.Sigmoid, bias=pr(f"v0{l}", hp)).then_inc(cnt.up(act_released), 1)

                for hp in range(2):
                    act.wait_ge(psum_ready, finished(("ry", l, hp)))
                    b = bank(("ry", l, hp))
                    f(A(39 + hp)[:, 0, :], b[:, :], ACT.Copy).then_inc(cnt.up(act_done), 1)
                    f(A(41 + hp)[:, 0, :], b[:, :], ACT.Square).then_inc(cnt.up(act_released), 1)
                act.wait_ge(values_ready, cnt.next(values_ready))
                for hp in range(2):
                    deviation(("rss", l, hp), hp, 64)

                prepare(f"out{l}_0")
                for n in range(4):
                    for hp in range(2):
                        dst = A((41, 43, 45, 47)[n], 2).rearrange("p a (j d) -> p (a j) d", d=RW_DIM)
                        act.wait_ge(psum_ready, finished(("tok", l, n, hp)))
                        b = bank(("tok", l, n, hp))
                        f(dst[:, :, hp * P:(hp + 1) * P], b[:, :].rearrange("p (j d) -> p j d", d=P),
                                     ACT.Copy).then_inc(cnt.up(act_released), 1)
                for hp in range(2):
                    for e in range(2):
                        copy_out(("L", l, hp, e), A(17 + e)[:, 0, :])
                    if hp == 0:
                        act.wait_ge(mix_ret_ready, cnt.next(mix_ret_ready))
                        for i in range(2):
                            copy_out(("z", l, 2, i), A(39 + i)[:, 0, :])
                    for n in range(len(LEVELS)):
                        for e in range(2):
                            copy_out(("T1", l, hp, n, e), A(49 + e)[:, 0, :])
                    copy_out(("MV", l, hp), A(35 + hp)[:, 0, :])
                    copy_out(("WT", l, hp), A(25 + hp)[:, 0, :])
                    act.wait_ge(psum_ready, finished(("U", l, hp)))
                    b = bank(("U", l, hp))
                    dst = A(31, 2).rearrange("p a (j d) -> p (a j) d", d=RW_DIM)
                    f(dst[:, :, hp * P:(hp + 1) * P], b[:, :].rearrange("p (j d) -> p j d", d=P), ACT.Copy).then_inc(cnt.up(act_released), 1)
                for k in MIX_ORDER[0:4]:
                    high(MIX_HIGH[k], A(k)[:, 0, :])
                act.wait_ge(*taken(("sa", l, NC - 1, 1)))
                for k in MIX_ORDER[4:6]:
                    high(MIX_HIGH[k], A(k)[:, 0, :])
                for hp in range(2):
                    copy_out(("y", l, hp), A(49 + hp)[:, 0, :])
                for hp in range(2):
                    act.wait_ge(*taken(("ymean", l, hp)))
                    f(A(51 + hp)[:, 0, :], A(49 + hp)[:, 0, :], ACT.Square).then_inc(cnt.up(y_squares_ready), 1)
                for hp in range(2):
                    deviation(("yvar", l, hp), 51 + hp, RW_HD, 1)

                act.wait_ge(mix_rw_ready, cnt.next(mix_rw_ready))
                for k in MIX_ORDER[6:8]:
                    high(MIX_HIGH[k], A(k)[:, 0, :])

                for m in range(DT):
                    if m % 2 == 0:
                        prepare(f"out{l}_{m // 2}")
                    act.wait_ge(*taken(("o", l, m)))
                    if m >= 2:
                        act.wait_ge(square_used, cnt.next(square_used))
                    f(A(49 + m % 2)[:, 0, :], h[:, m, :], ACT.Square).then_inc(cnt.up(square_ready), 1)
                act.wait_ge(square_used, cnt.next(square_used))
                prepare(f"gu{l}_0")
                deviation(("ss", ("ffn", l)), 52, D)
                hn_highs()

                def ff_high(j):
                    act.wait_ge(*taken(("up", l, j)))
                    high(FF_HIGH[j % FH], A(2 + j % 2)[:, 0, :])

                for half in range(2):
                    for j in range(half * FH, (half + 1) * FH):
                        prepare(f"gu{l}_{j}")
                        if j % FH >= 2:
                            act.wait_ge(*taken(("up", l, j - 2)))
                        copy_out(("gate", l, j), A(j % 2)[:, 0, :], func=ACT.Silu)
                        if j % FH:
                            ff_high(j - 1)
                    prepare(f"down{l}_0_{half}")
                    ff_high((half + 1) * FH - 1)
                    if half == 0:
                        for m in range(DT):
                            prepare(f"down{l}_{m}_0")
                for m in range(DT):
                    prepare(f"down{l}_{m}_1")
                    act.wait_ge(*taken(("down", l, m, 1)))
                    if m >= 2:
                        act.wait_ge(square_used, cnt.next(square_used))
                    if l == DEPTH - 1:
                        f(A(44 + m % 2)[:, 0, :], h[:, m, :], ACT.Square, scale=pr("final_norm", m)).then_inc(cnt.up(act_done), 1)
                    f(A(49 + m % 2)[:, 0, :], h[:, m, :], ACT.Square).then_inc(cnt.up(square_ready), 1)
                act.wait_ge(square_used, cnt.next(square_used))

            deviation(("ss", "even"), 52, D, 3)
            deviation(("ss", "final"), 28, D)
            hn_highs()

            def recurrence(m):
                for d in range(2):
                    for g in range(2):
                        act.wait_ge(psum_ready, finished(("gate_ri", m, d, g)))
                        b = bank(("gate_ri", m, d, g))
                        if m and d == 0 and g == 0:
                            act.wait_ge(gated_ready, cnt.next(gated_ready))
                        f(A(26 + 2 * d + g)[:, 0, :], b[:, :], ACT.Sigmoid,
                                     bias=pr("gate_b", (d * 2 + g) * DT + m)).then_inc(cnt.up(act_released), 1)
                act.wait_ge(cnt.sem, cnt.value)
                for d in range(2):
                    r = A(26 + 2 * d)[:, 0, :]
                    f(A(48 + d)[:, 0, :], r, ACT.Tanh, scale=splus[:, d * DT + m:d * DT + m + 1]).then_inc(cnt.up(act_done), 1)
                    f(rg_a(d), r, ACT.Exp, scale=sp_t[:, 1, d * DT + m:d * DT + m + 1]).then_inc(cnt.up(act_done), 1)
                act.wait_ge(cnt.sem, cnt.value)
                for d in range(2):
                    f(A(26 + 2 * d)[:, 0, :], rg_a(d), ACT.Square).then_inc(cnt.up(conv_padded), 1)
                for d in range(2):
                    act.wait_ge(sqrt_ready, cnt.next(sqrt_ready))
                    f(A(48 + d)[:, 0, :], A(48 + d)[:, 0, :], ACT.Sqrt).then_inc(cnt.up(ebuf_used), 1)

            for m in range(DT):
                prepare(f"even_xa_za{m}")
                if m:
                    act.wait_ge(conv_ready, cnt.next(conv_ready))
                copy_out(("xa", m), flat(16, 3)[:, 2:2 + T])
                if m >= 2:
                    act.wait_ge(mix_even_ready, cnt.next(mix_even_ready))
                copy_out(("za", m), A(21 + m % 2)[:, 0, :], func=ACT.Silu)
                if m:
                    act.wait_ge(*taken(("gb", m - 1)))
                prepare(f"even_xb_gc{m}")
                copy_out(("xb", m), A(23)[:, 0, :])
                prepare(f"even_gb_zb{m}")
                recurrence(m)
                if m:
                    act.wait_ge(silu_used, cnt.next(silu_used))
                copy_out(("zb", m), A(25)[:, 0, :], func=ACT.Silu)
            for k in EVEN_ORDER:
                if k == 15:
                    act.wait_ge(silu_used, cnt.next(silu_used))
                    act.wait_ge(mix_even_ready, cnt.next(mix_even_ready, 2))
                high(HN_HIGH + k, A(k)[:, 0, :])

            def outputs(name, tag, slab_of, base):
                for m in range(DT):
                    prepare(slab_of(m))
                    copy_out((name, m), A(base + m)[:, 0, :])
                    if m >= 2:
                        act.wait_ge(square_used, cnt.next(square_used))
                    act.wait_ge(cnt.sem, cnt.value)
                    f(A(49 + m % 2)[:, 0, :], A(base + m)[:, 0, :], ACT.Square).then_inc(cnt.up(square_ready), 1)
                act.wait_ge(square_used, cnt.next(square_used))
                deviation(("ss", tag), 52, D)

            outputs("eo", "even_post", lambda m: f"even_out{m}", 16)

            for m in range(DT):
                act.wait_ge(residual_ready, cnt.next(residual_ready))
                f(A(m)[:, 0, :], h[:, m, :], ACT.Square).then_inc(cnt.up(residual_square_ready), 1)
            deviation(("ss", "odd"), 52, D)
            hn_highs()
            for m in range(8):
                prepare(f"odd_qk{m // 2}")
                copy_out(("qk", m), A(m)[:, 0, :], scale=P ** -0.5 if m < 4 else 1.0)
            prepare("odd_lr")
            copy_out("lr", A(24)[0:32, 0, :], rows=slice(0, 32))

            def gla_logs(hd):
                for d in range(2):
                    act.wait_ge(gla_min_ready, cnt.next(gla_min_ready))
                    z = gla_t(hd, d, 1)
                    f(z, z, ACT.Exp, scale=-1.0).then_inc(cnt.up(act_done), 1)
                    act.wait_ge(cnt.sem, cnt.value)
                    f(z, z, ACT.Ln, bias=1.0).then_inc(cnt.up(gla_log_ready), 1)

            def gla_exps(hd):
                for d in range(2):
                    act.wait_ge(gla_cum_ready, cnt.next(gla_cum_ready))
                    cum = gla_t(hd, d, 0)
                    end = RW_CHUNK - 1 if d == 0 else 0
                    f(gla_t(hd, d, 1), cum, ACT.Exp, scale=1 / 16.0).then_inc(cnt.up(act_done), 1)
                    f(gla_t(hd, d, 2), cum, ACT.Exp, scale=-1 / 16.0).then_inc(cnt.up(act_done), 1)
                    f(gla_dec[:, hd % 3, d, :], cum.rearrange("p (c t) -> p c t", t=GLA_CHUNK)[:, :, end],
                             ACT.Exp, scale=1 / 16.0).then_inc(cnt.up(gla_exps_ready), 1)

            for n in range(4):
                prepare(f"odd_v{n}")
                if n % 2 == 0:
                    gla_logs(n // 2)
                else:
                    gla_exps(n // 2)
                for jj in range(2):
                    act.wait_ge(psum_ready, finished(("gv", n, jj)))
                    b = bank(("gv", n, jj))
                    dst = A(8 + 4 * jj, 4).rearrange("p (i a) d -> p i (a d)", i=2)
                    f(dst[:, :, n * 256:(n + 1) * 256], b[:, :].rearrange("p (i d) -> p i d", i=2),
                                 ACT.Copy).then_inc(cnt.up(act_released), 1)
            for m in range(8):
                if m < 6:
                    prepare(f"odd_r{m // 2}")
                copy_out(("gr", m), A(16 + m)[:, 0, :], func=ACT.Silu)

            def gla_kt(hd):
                for d in range(2):
                    copy_out(("gkt", hd, d), A(GLA_KT + d)[:, 0, :])

            def gla_out(hd):
                for eh in range(2):
                    act.wait_ge(psum_ready, finished(("go", hd, eh)))
                    b = bank(("go", hd, eh))
                    if hd and eh == 0:
                        act.wait_ge(gla_o_used, cnt.next(gla_o_used))
                    f(A(GLA_O + eh)[:, 0, :], b[:, :], ACT.Copy).then_inc(cnt.up(act_done), 1)
                    f(A(GLA_SQ + eh)[:, 0, :], b[:, :], ACT.Square).then_inc(cnt.up(act_released), 1)

            def gla_deviation(hd):
                deviation(("gss", hd), GLA_DEV, GLA_DV)

            def gla_highs(hd):
                act.wait_ge(gla_mix_ready, cnt.next(gla_mix_ready))
                for m in (2 * hd, 2 * hd + 1):
                    high(16 + m, A(gla_mix(m))[:, 0, :])

            gla_kt(0)
            gla_kt(1)
            gla_logs(2)
            gla_exps(2)
            gla_out(0)
            gla_kt(2)
            gla_deviation(0)
            gla_logs(3)
            gla_exps(3)
            gla_out(1)
            gla_kt(3)
            gla_deviation(1)
            gla_highs(0)
            gla_out(2)
            gla_deviation(2)
            gla_highs(1)
            prepare("odd_out0")
            gla_highs(2)
            gla_out(3)
            gla_deviation(3)
            gla_highs(3)
            outputs("oo", "odd_post", lambda m: f"odd_out{m // 2}", 8)

        @block.vector
        def _(dve):
            cnt = Count()
            tt, stt, ts, cp = dve.tensor_tensor, dve.scalar_tensor_tensor, dve.tensor_scalar, dve.tensor_copy
            MUL, ADD, SUB, MAX, MIN = ALU.mult, ALU.add, ALU.subtract, ALU.max, ALU.min

            def sum_squares(before=None):
                acc = A(51)[:, 0, :]
                for m in range(DT):
                    if before:
                        before(m)
                    dve.wait_ge(square_ready, cnt.next(square_ready))
                    sq = A(49 + m % 2)[:, 0, :]
                    sig = squares_summed if m == DT - 1 else square_used
                    if m:
                        dve.wait_ge(cnt.sem, cnt.value)
                        tt(acc, acc, sq, ADD).then_inc(cnt.up(sig), 1)
                    else:
                        cp(acc, sq).then_inc(cnt.up(sig), 1)

            def invert(key, t):
                dve.wait_ge(*taken(key))
                dve.reciprocal(A(t)[:, 0, :], A(t)[:, 0, :]).then_inc(cnt.up(dve_done), 1)
                dve.wait_ge(cnt.sem, cnt.value)

            splits = []

            def prepare(name):
                for n in range(len(splits), min(split_index[name] + 2, len(split_slabs))):
                    slab, cols = plan[slab_index[split_slabs[n]]]
                    at = slab_index[slab] % SLOTS
                    dve.wait_ge(slab_high_ready, cnt.next(slab_high_ready))
                    tt(ring_low[:, n % SLOTS, 0:cols], ring[:, at, 0:cols], ring_high[:, n % SLOTS, 0:cols].bitcast(F32),
                       SUB).then_inc(cnt.up(slab_split), 1)
                    splits.append(slab)

            def low(dst, src, high):
                dve.wait_ge(high_ready, cnt.next(high_ready))
                tt(R(dst), src, R(high).bitcast(F32), SUB).then_inc(cnt.up(parts_ready), 1)

            def norm(tag, gain):
                invert(("ss", tag), 52)
                for m in range(DT + 1):
                    if m < DT:
                        if m > 1:
                            dve.wait_ge(cnt.sem, cnt.value)
                        stt(A(47 + m % 2)[:, 0, :], h[:, m, :], gain(m), A(52)[:, 0, :], MUL,
                            MUL).then_inc(cnt.up(value_ready), 1)
                    if m:
                        low(HN_LOW + m - 1, A(47 + (m - 1) % 2)[:, 0, :], HN_HIGH + m - 1)
                dve.wait_ge(cnt.sem, cnt.value)

            for n, eps in enumerate((EPS, RW_GN_EPS, 0.0, EPS * EPS)):
                dve.memset(epsilon[:, n:n + 1], eps).then_inc(cnt.up(epsilon_ready), 1)
            dve.wait_ge(par_loaded, 16)
            for l in range(DEPTH):
                o, n = PAR[f"mu{l}"]
                ts(omu[:, l, :], par[:, o:o + n], -1.0, 1.0, MUL, ADD).then_inc(cnt.up(dve_done), 1)
                o, n = PAR[f"k_a{l}"]
                ts(oka[:, l, :], par[:, o:o + n], -1.0, 1.0, MUL, ADD).then_inc(cnt.up(dve_done), 1)
            o, n = PAR["final_norm"]
            o2, _ = PAR["even_pre"]
            tt(both_gains[:, :], par[:, o:o + n], par[:, o2:o2 + n], MUL).then_inc(cnt.up(dve_done), 1)
            dve.memset(stat[:, :, :], 0.0).then_inc(cnt.up(dve_done), 1)
            dve.wait_ge(cnt.sem, cnt.value)

            cos_r, sin_r, cos_m, sin_m = (trig[:, n, :] for n in range(4))

            def residual(key, slab_of, gained=False):
                acc = A(51)[:, 0, :]
                for m in range(DT + 1):
                    if m < DT:
                        prepare(slab_of(m))
                        dve.wait_ge(psum_ready, finished(key(m)))
                        b = bank(key(m))
                        tt(h[:, m, :], h[:, m, :], b[:, :], ADD).then_inc(cnt.up(dve_released), 1)
                    if m:
                        dve.wait_ge(square_ready, cnt.next(square_ready))
                        sqm = A(49 + (m - 1) % 2)[:, 0, :]
                        sig = squares_summed if m == DT else square_used
                        if gained:
                            g, gsq = A(46)[:, 0, :], A(44 + (m - 1) % 2)[:, 0, :]
                            ins = cp(g, gsq) if m == 1 else tt(g, g, gsq, ADD)
                            ins.then_inc(cnt.up(dve_done), 1)
                        ins = cp(acc, sqm) if m == 1 else tt(acc, acc, sqm, ADD)
                        ins.then_inc(cnt.up(sig), 1)
                        dve.wait_ge(cnt.sem, cnt.value)

            for l in range(DEPTH):
                if l == 0:
                    sum_squares()
                prepare(f"in{l}_r")
                norm(("attn", l), lambda m: pr(f"attn_norm{l}", m))
                if l == 0:
                    dve.wait_ge(pos_loaded, 16)
                    dve.wait_ge(ones_loaded, 16)
                    TWO_PI = 2 * np.pi
                    C1 = 6.28125
                    C2 = 2.0 ** -21 * int((TWO_PI - C1) * 2.0 ** 21)
                    C3 = float(TWO_PI - C1 - C2)
                    MAGIC = 1.5 * 2.0 ** 23
                    posf, turns = A(1)[:, 0, :], A(2)[:, 0, :]
                    cp(posf, A(0)[:, 0, :].bitcast(I32)).then_inc(cnt.up(dve_done), 1)
                    dve.wait_ge(cnt.sem, cnt.value)
                    for n in range(2):
                        ang = trig[:, 2 * n, :]
                        o, _ = CON["inv_freq"]
                        ts(ang, posf, con[:, o + n:o + n + 1], None, MUL).then_inc(cnt.up(dve_done), 1)
                        dve.wait_ge(cnt.sem, cnt.value)
                        ts(turns, ang, 1.0 / TWO_PI, MAGIC, MUL, ADD).then_inc(cnt.up(dve_done), 1)
                        dve.wait_ge(cnt.sem, cnt.value)
                        ts(turns, turns, MAGIC, None, SUB).then_inc(cnt.up(dve_done), 1)
                        dve.wait_ge(cnt.sem, cnt.value)
                        for c in (C1, C2, C3):
                            stt(ang, turns, -c, ang, MUL, ADD).then_inc(cnt.up(dve_done), 1)
                            dve.wait_ge(cnt.sem, cnt.value)
                        ts(ang, ang, 3.1415925, -3.1415925, MIN, MAX).then_inc(cnt.up(angle_ready), 1)
                    for n in range(2):
                        dve.wait_ge(sine_ready, cnt.next(sine_ready))
                        ts(trig[:, 2 * n, :], trig[:, 2 * n, :], -2.0, 1.0, MUL, ADD).then_inc(cnt.up(dve_done), 1)
                    dve.wait_ge(cnt.sem, cnt.value)

                praw = flat(47, 4)
                for m in range(3):
                    dve.memset(praw[:, m * 513:m * 513 + 1], 0.0).then_inc(cnt.up(dve_done), 1)
                for m in range(RW_PA):
                    if m % 2 == 0 and m:
                        prepare(f"in{l}_" + ("r", "k", "v", "lo_mq0")[m // 2])
                    dve.wait_ge(*taken(("pa", l, m)))
                    o = (m % 3) * 513
                    dst = A(10 + m)[:, 0, :]
                    ts(dst, praw[:, o + 1:o + 513], omu[:, l, m:m + 1], None, MUL).then_inc(cnt.up(dve_done), 1)
                    dve.wait_ge(cnt.sem, cnt.value)
                    stt(dst, praw[:, o:o + T], pr(f"mu{l}", m), dst, MUL, ADD).then_inc(cnt.up(praw_used), 1)

                cp(stat[:, 0, 0:1], stat[:, 1, 0:1]).then_inc(cnt.up(shifted_ready), 1)
                for n in ("mq12", "mkv", "krope", "rq"):
                    prepare(f"in{l}_{n}")

                dve.wait_ge(psum_ready, finished(("krot", l)))
                b = bank(("krot", l))
                kr, tmp = A(30)[64:96, 0, :], A(5)[64:96, 0, :]
                tt(tmp, b[64:96, :], sin_m[64:96], MUL).then_inc(cnt.up(dve_released), 1)
                tt(kr, kr, cos_m[64:96], MUL).then_inc(cnt.up(dve_done), 1)
                dve.wait_ge(cnt.sem, cnt.value)
                tt(kr, kr, tmp, ADD).then_inc(cnt.up(krope_ready), 1)
                prepare(f"in{l}_rk")
                dve.wait_ge(con_loaded, 16)
                invert(("mqs", l), 51)
                for m in range(QT):
                    stt(A(25 + m)[:, 0, :], A(25 + m)[:, 0, :], pr(f"q_norm{l}", m), A(51)[:, 0, :], MUL, MUL).then_inc(cnt.up(dve_done), 1)
                invert(("mkvs", l), 52)
                for m in range(KVT):
                    stt(A(28 + m)[:, 0, :], A(28 + m)[:, 0, :], pr(f"kv_norm{l}", m), A(52)[:, 0, :],
                               MUL, MUL).then_inc(cnt.up(latent_ready if m == KVT - 1 else dve_done), 1)
                prepare(f"in{l}_rg")
                for i in range(4):
                    dve.wait_ge(psum_ready, finished(("rrot", l, i)))
                    b = bank(("rrot", l, i))
                    x, tmp = A(17 + i)[:, 0, :], A(4 + i)[:, 0, :]
                    tt(tmp, b[:, :], sin_r, MUL).then_inc(cnt.up(dve_released), 1)
                    tt(x, x, cos_r, MUL).then_inc(cnt.up(dve_done), 1)
                    dve.wait_ge(cnt.sem, cnt.value)
                    tt(x, x, tmp, ADD).then_inc(cnt.up(ret_rope_ready if i == 3 else dve_done), 1)
                dve.wait_ge(cnt.sem, cnt.value)
                if l == 0:
                    o, n = PAR["lam"]
                    lam = par[:, o:o + n]
                    ts(sp_t[:, 1, :], lam, -1.0, None, MUL).then_inc(cnt.up(dve_done), 1)
                    dve.wait_ge(cnt.sem, cnt.value)
                    tt(sp_t[:, 0, :], sp_t[:, 1, :], lam, MAX).then_inc(cnt.up(lam_exp_ready), 1)
                    dve.wait_ge(lam_ready, cnt.next(lam_ready))
                    y, mx = sp_t[:, 0, :], sp_t[:, 1, :]
                    ts(mx, mx, 0.0, None, MAX).then_inc(cnt.up(dve_done), 1)
                    ts(splus[:, :], y, 2.0, None, ADD).then_inc(cnt.up(dve_done), 1)
                    dve.wait_ge(cnt.sem, cnt.value)
                    dve.reciprocal(splus[:, :], splus[:, :]).then_inc(cnt.up(dve_done), 1)
                    dve.wait_ge(cnt.sem, cnt.value)
                    tt(y, y, splus[:, :], MUL).then_inc(cnt.up(dve_done), 1)
                    dve.wait_ge(cnt.sem, cnt.value)
                    sq = stat[:, 0, 0:2 * DT]
                    tt(sq, y, y, MUL).then_inc(cnt.up(dve_done), 1)
                    dve.wait_ge(cnt.sem, cnt.value)
                    ts(splus[:, :], sq, 1.0 / 17, 1.0 / 15, MUL, ADD).then_inc(cnt.up(dve_done), 1)
                    for k in (13, 11, 9, 7, 5, 3, 1):
                        dve.wait_ge(cnt.sem, cnt.value)
                        tt(splus[:, :], splus[:, :], sq, MUL).then_inc(cnt.up(dve_done), 1)
                        dve.wait_ge(cnt.sem, cnt.value)
                        ts(splus[:, :], splus[:, :], 1.0 / k, None, ADD).then_inc(cnt.up(dve_done), 1)
                    dve.wait_ge(cnt.sem, cnt.value)
                    stt(splus[:, :], splus[:, :], 2.0, y, MUL, MUL).then_inc(cnt.up(dve_done), 1)
                    dve.wait_ge(cnt.sem, cnt.value)
                    tt(splus[:, :], splus[:, :], mx, ADD).then_inc(cnt.up(dve_done), 1)
                    dve.wait_ge(cnt.sem, cnt.value)
                    ts(splus[:, :], splus[:, :], 8.0, None, MUL).then_inc(cnt.up(dve_done), 1)
                    dve.wait_ge(cnt.sem, cnt.value)
                    ts(sp_t[:, 1, :], splus[:, :], -1.0, None, MUL).then_inc(cnt.up(dve_done), 1)
                for hd in range(MLA_H):
                    dve.wait_ge(psum_ready, finished(("qrot", l, hd)))
                    b = bank(("qrot", l, hd))
                    q, tmp = A(hd)[64:96, 0, :], A(50 + hd % 3)[64:96, 0, :]
                    tt(tmp, b[64:96, :], sin_m[64:96], MUL).then_inc(cnt.up(dve_released), 1)
                    tt(q, q, cos_m[64:96], MUL).then_inc(cnt.up(dve_done), 1)
                    dve.wait_ge(cnt.sem, cnt.value)
                    tt(q, q, tmp, ADD).then_inc(cnt.up(qrope_ready), 1)
                dve.wait_ge(cnt.sem, cnt.value)
                for hp in range(2):
                    dve.wait_ge(*taken(("z", l, 0, hp)))
                    dve.tensor_tensor_scan(A(27 + hp)[:, 0, :], cst("carry"), A(25 + hp)[:, 0, :], 0.0, MUL, ADD).then_inc(cnt.up(dve_done), 1)
                dve.wait_ge(cnt.sem, cnt.value)
                tt(A(25, 2), A(27, 2), A(25, 2), SUB).then_inc(cnt.up(decay_summed), 1)
                for u in range(MLA_H * NT + 3):
                    if u < MLA_H * NT:
                        i = u % NT
                        dve.wait_ge(psum_ready, finished(("s", l, u)))
                        b = bank(("s", l, u))
                        diag = b[:, i * P:(i + 1) * P]
                        tt(diag, diag, cst("causal"), ADD).then_inc(cnt.up(dve_done), 1)
                        dve.wait_ge(cnt.sem, cnt.value)
                        dve.tensor_reduce(stat[:, 0, u:u + 1], b[:, 0:(i + 1) * P], AX_X, MAX).then_inc(cnt.up(dve_done), 1)
                        dve.wait_ge(cnt.sem, cnt.value)
                        ts(stat[:, 1, u:u + 1], stat[:, 0, u:u + 1], -MLA_SCALE, None, MUL).then_inc(cnt.up(bias_ready), 1)
                    w = u - 2
                    if 0 <= w < MLA_H * NT:
                        n = (w % NT + 1) * P
                        dve.wait_ge(psum_ready, finished(("t", l, w)))
                        b = bank(("t", l, w))
                        if w >= 2:
                            dve.wait_ge(psum_ready, finished(("pv", l, w - 2)))
                        cp(A(50 + w % 2)[:, 0, 0:n], b[:, 0:n]).then_inc(cnt.up(dve_released), 1)
                        dve.reciprocal(stat[:, 3, w:w + 1], stat[:, 2, w:w + 1]).then_inc(cnt.up(dve_done), 1)
                    w = u - 3
                    if w >= 0:
                        hd, i = w // NT, w % NT
                        if u >= MLA_H * NT:
                            dve.wait_ge(cnt.sem, cnt.value)
                        dve.wait_ge(psum_ready, finished(("pv", l, w)))
                        b = bank(("pv", l, w))
                        ts(A(43 + i)[:, 0, hd * 64:(hd + 1) * 64], b[:, 0:64], stat[:, 3, w:w + 1], None,
                                      MUL).then_inc(cnt.up(dve_released), 1)

                r_, k_, v_ = (lambda hp: A(10 + hp)[:, 0, :]), (lambda hp: A(12 + hp)[:, 0, :]), (
                    lambda hp: A(14 + hp)[:, 0, :])

                def removal_key():
                    for hp in range(2):
                        dve.wait_ge(*taken(("kks", l, hp)))
                        ts(A(31 + hp)[:, 0, :], A(31 + hp)[:, 0, :], 1e-12, None, MAX).then_inc(cnt.up(dve_done), 1)
                    dve.wait_ge(cnt.sem, cnt.value)
                    for hp in range(2):
                        invert(("kks", l, hp), 31 + hp)
                        stt(A(31 + hp)[:, 0, :], k_(hp), pr(f"k_k{l}", hp), A(31 + hp)[:, 0, :], MUL, MUL).then_inc(cnt.up(dve_done), 1)

                def keys():
                    for hp in range(2):
                        a = A(29 + hp)[:, 0, :]
                        dve.wait_ge(*taken(("z", l, 1, hp)))
                        ts(A(37 + hp)[:, 0, :], a, pr(f"k_a{l}", hp), oka[:, l, hp:hp + 1], MUL, ADD).then_inc(cnt.up(dve_done), 1)
                        dve.wait_ge(cnt.sem, cnt.value)
                        tt(k_(hp), k_(hp), A(37 + hp)[:, 0, :], MUL).then_inc(cnt.up(dve_done), 1)
                        tt(a, a, A(31 + hp)[:, 0, :], MUL).then_inc(cnt.up(dve_done), 1)
                        dve.wait_ge(cnt.sem, cnt.value)
                        stt(A(37 + hp)[:, 0, :], r_(hp), pr(f"r_k{l}", hp), k_(hp), MUL, MUL).then_inc(cnt.up(bonus_product_ready if hp else dve_done), 1)

                def decayed():
                    dve.wait_ge(decays_ready, cnt.next(decays_ready, 4))
                    for hp in range(2):
                        stt(A(33 + hp)[:, 0, :], A(31 + hp)[:, 0, :], -1.0, A(33 + hp)[:, 0, :], MUL, MUL).then_inc(cnt.up(dve_done), 1)
                    dve.wait_ge(cnt.sem, cnt.value)
                    tt(A(29, 2), A(29, 2), A(35, 2), MUL).then_inc(cnt.up(dve_done), 1)
                    tt(A(10, 2), A(10, 2), A(27, 2), MUL).then_inc(cnt.up(r_decayed), 1)
                    dve.wait_ge(k_decayed, cnt.next(k_decayed))
                    dve.wait_ge(cnt.sem, cnt.value)
                    for hp in range(2):
                        end = decay_end[:, hp, :, None].broadcast_to((P, NC, RW_CHUNK))
                        chunked = lambda t: A(t + hp)[:, 0, :].rearrange("p (c t) -> p c t", t=RW_CHUNK)
                        tt(chunked(35), chunked(29), end, MUL).then_inc(cnt.up(scan_inputs_ready if hp else dve_done), 1)

                o, _ = CON["decay"]
                for hd in range(RET_H):
                    off = 0
                    for j in range(NT):
                        n = T - j * P
                        dve.wait_ge(psum_ready, finished(("rs", l, hd, j)))
                        b = bank(("rs", l, hd, j))
                        dst = flat(43 + 5 * (hd // 2), 5)[:, (hd % 2) * 1280 + off:(hd % 2) * 1280 + off + n]
                        tt(dst, b[:, 0:n], con[:, o + hd * T:o + hd * T + n], MUL).then_inc(cnt.up(dve_released), 1)
                        off += n
                    if hd == 1:
                        removal_key()
                    if hd == 2:
                        keys()
                decayed()
                for hp in range(2):
                    invert(("rss", l, hp), hp)
                    y = A(39 + hp)[:, 0, :]
                    tt(y, y, A(hp)[:, 0, :], MUL).then_inc(cnt.up(dve_done), 1)
                    dve.wait_ge(cnt.sem, cnt.value)
                    tt(A(2 + hp)[:, 0, :], y, A(23 + hp)[:, 0, :], MUL).then_inc(cnt.up(mix_ret_ready if hp else dve_done), 1)
                dve.wait_ge(values_ready, cnt.next(values_ready))
                for hp in range(2):
                    dve.wait_ge(psum_ready, finished(("bonus", l, hp)))
                    b = bank(("bonus", l, hp))
                    tt(A(37 + hp)[:, 0, :], b[:, :], v_(hp), MUL).then_inc(cnt.up(dve_released), 1)
                prepare(f"out{l}_0")

                def bc(name):
                    return cst(name)[:, None, :].broadcast_to((P, NT, P))

                def four(ap):
                    return ap.rearrange("p (j t) -> p j t", t=P)

                for hp in range(2):
                    Xt, X = A(23, 2), A(21, 2)
                    for e in range(2):
                        dve.wait_ge(psum_ready, finished(("N", l, hp, e)))
                        b = bank(("N", l, hp, e))
                        tt(four(Xt[:, e, :]), four(b[:, :]), bc("upper_pair"), MUL).then_inc(cnt.up(dve_released), 1)
                        dve.wait_ge(*taken(("L", l, hp, e)))
                        tt(four(X[:, e, :]), four(A(17 + e)[:, 0, :]), bc("lower_pair"), MUL).then_inc(cnt.up(dve_done), 1)
                    dve.wait_ge(cnt.sem, cnt.value)
                    for e in range(2):
                        tt(four(X[:, e, :]), four(X[:, e, :]), bc("ident"), ADD).then_inc(cnt.up(dve_done), 1)
                        tt(four(Xt[:, e, :]), four(Xt[:, e, :]), bc("ident"), ADD).then_inc(cnt.up(inverse_ready), 1)
                    for e in range(2):
                        dve.wait_ge(psum_ready, finished(("M", l, hp, e)))
                        b = bank(("M", l, hp, e))
                        tt(four(A(51 + e)[:, 0, :]), four(b[:, :]), bc("upper_strict"), MUL).then_inc(cnt.up(dve_released), 1)
                    for n in range(len(LEVELS)):
                        for e in range(2):
                            for which, M in (("Xt", Xt), ("X", X))[:1 if n == len(LEVELS) - 1 else 2]:
                                if n:
                                    dve.wait_ge(*taken((which, l, hp, n - 1, e)))
                                dve.wait_ge(psum_ready, finished((which, l, hp, n, e)))
                                b = bank((which, l, hp, n, e))
                                tt(M[:, e, :], M[:, e, :], b[:, :], ADD).then_inc(cnt.up(dve_released), 1)
                state = flat(14, 3)
                U = A(31, 2).rearrange("p a (j d) -> p (a j) d", d=RW_DIM)
                SA = A(27, 2).rearrange("p a (j d) -> p (a j) d", d=RW_DIM)
                dve.wait_ge(*taken(("U", l, 1)))

                def own_scores(n):
                    hp, e, name, to = n // 4, n // 2 % 2, ("RB", "RK")[n % 2], (17, 21)[n % 2]
                    dve.wait_ge(psum_ready, finished((name, l, hp, e)))
                    b = bank((name, l, hp, e))
                    tt(four(A(to + 2 * hp + e)[:, 0, :]), four(b[:, :]), bc("upper"), MUL).then_inc(cnt.up(dve_released), 1)

                for c in range(NC):
                    j, r = c // 2, slice(64 * (c % 2), 64 * (c % 2) + 64)
                    if c:
                        for e in range(2):
                            dve.wait_ge(psum_ready, finished(("sa", l, c, e)))
                            b = bank(("sa", l, c, e))
                            by_pair = lambda x: x[r, j, :].rearrange("p (a e d) -> p a e d", a=2, e=2)[:, :, e, :]
                            tt(by_pair(SA), b[r, 0:P].rearrange("p (a d) -> p a d", a=2), by_pair(U), ADD).then_inc(cnt.up(dve_released), 1)
                        dve.wait_ge(cnt.sem, cnt.value)
                        cp(stat[:, 0, 0:1], stat[:, 1, 0:1]).then_inc(cnt.up(state_input_ready), 1)
                        own_scores(c)
                    else:
                        cp(SA[r, j, :], U[r, j, :]).then_inc(cnt.up(state_input_ready), 1)
                    if c < NC - 1:
                        dve.wait_ge(psum_ready, finished(("st", l, c)))
                        b = bank(("st", l, c))
                        new = state[:, (c + 1) * P:(c + 2) * P]
                        if c:
                            old = state[:, c * P:(c + 1) * P]
                            for hp in range(2):
                                hs = slice(hp * 64, hp * 64 + 64)
                                ins = stt(new[:, hs], old[:, hs], decay_end[:, hp, c:c + 1], b[:, hs], MUL, ADD)
                                if hp:
                                    ins.then_inc(cnt.up(dve_released), 1)
                                else:
                                    ins.then_inc(cnt.up(dve_done), 1)
                        else:
                            cp(new, b[:, 0:P]).then_inc(cnt.up(dve_released), 1)
                        dve.wait_ge(cnt.sem, cnt.value)
                        cp(stat[:, 0, 0:1], stat[:, 1, 0:1]).then_inc(cnt.up(state_ready), 1)
                        if c == 0:
                            own_scores(0)
                for k in MIX_ORDER[0:6]:
                    low(k, A(k)[:, 0, :], MIX_HIGH[k])
                for hp in range(2):
                    dve.wait_ge(psum_ready, finished(("ymean", l, hp)))
                    b = bank(("ymean", l, hp))
                    y = A(49 + hp)[:, 0, :]
                    stt(y, b[:, :], -1.0 / RW_HD, y, MUL, ADD).then_inc(cnt.up(dve_released), 1)
                for hp in range(2):
                    invert(("yvar", l, hp), 51 + hp)
                    y = A(49 + hp)[:, 0, :]
                    stt(y, y, pr(f"gn_w{l}", hp), A(51 + hp)[:, 0, :], MUL, MUL).then_inc(cnt.up(dve_done), 1)
                    dve.wait_ge(cnt.sem, cnt.value)
                    stt(y, y, pr(f"gn_b{l}", hp), A(37 + hp)[:, 0, :], ADD, ADD).then_inc(cnt.up(dve_done), 1)
                    dve.wait_ge(cnt.sem, cnt.value)
                    tt(A(hp)[:, 0, :], y, A(39 + hp)[:, 0, :], MUL).then_inc(cnt.up(mix_rw_ready if hp else dve_done), 1)

                for k in MIX_ORDER[6:8]:
                    low(k, A(k)[:, 0, :], MIX_HIGH[k])
                dve.wait_ge(cnt.sem, cnt.value)

                residual(lambda m: ("o", l, m), lambda m: f"out{l}_{m // 2}")
                prepare(f"gu{l}_0")
                norm(("ffn", l), lambda m: pr(f"ffn_norm{l}", m))

                def ff_low(j):
                    low(FF_LOW[j % FH], A(2 + j % 2)[:, 0, :], FF_HIGH[j % FH])

                for half in range(2):
                    for j in range(half * FH, (half + 1) * FH):
                        prepare(f"gu{l}_{j}")
                        dve.wait_ge(psum_ready, finished(("up", l, j)))
                        b = bank(("up", l, j))
                        dve.wait_ge(*taken(("gate", l, j)))
                        if j % FH > 1:
                            dve.wait_ge(cnt.sem, cnt.value)
                        tt(A(2 + j % 2)[:, 0, :], A(j % 2)[:, 0, :], b[:, :], MUL).then_inc(cnt.up(dve_released), 1)
                        if j % FH:
                            ff_low(j - 1)
                    prepare(f"down{l}_0_{half}")
                    dve.wait_ge(cnt.sem, cnt.value)
                    ff_low((half + 1) * FH - 1)
                    if half == 0:
                        for m in range(DT):
                            prepare(f"down{l}_{m}_0")
                            dve.wait_ge(psum_ready, finished(("down", l, m, 0)))
                            b = bank(("down", l, m, 0))
                            tt(h[:, m, :], h[:, m, :], b[:, :], ADD).then_inc(cnt.up(dve_released), 1)
                residual(lambda m: ("down", l, m, 1), lambda m: f"down{l}_{m}_1", l == DEPTH - 1)

            norm("even", lambda m: both_gains[:, m:m + 1])
            invert(("ss", "final"), 28)
            for m in range(DT):
                stt(h[:, m, :], h[:, m, :], pr("final_norm", m), A(28)[:, 0, :], MUL, MUL).then_inc(cnt.up(dve_done), 1)
            xa, xg = flat(16, 3)[:, 0:T + 3], flat(16, 3)[:, T + 3:2 * T + 5]
            dve.memset(xa[:, 0:2], 0.0).then_inc(cnt.up(dve_done), 1)
            dve.memset(xa[:, T + 2:T + 3], 0.0).then_inc(cnt.up(dve_done), 1)
            dve.memset(xg[:, 0:1], 0.0).then_inc(cnt.up(dve_done), 1)
            dve.memset(xg[:, T + 1:T + 2], 0.0).then_inc(cnt.up(dve_done), 1)
            dve.wait_ge(cnt.sem, cnt.value)

            def gated(m):
                ua = A(19 + m % 2)[:, 0, :]
                for d in range(2):
                    i = A(27 + 2 * d)[:, 0, :]
                    dve.wait_ge(*taken(("gate_ri", m, d, 1)))
                    tt(i, i, ua, MUL).then_inc(cnt.up(dve_done), 1)
                for d in range(2):
                    dve.wait_ge(conv_padded, cnt.next(conv_padded))
                    t = A(48 + d)[:, 0, :]
                    stt(t, A(26 + 2 * d)[:, 0, :], 1.0, t, ADD, MUL).then_inc(cnt.up(sqrt_ready), 1)
                for d in range(2):
                    dve.wait_ge(ebuf_used, cnt.next(ebuf_used))
                    i = A(27 + 2 * d)[:, 0, :]
                    tt(i, i, A(48 + d)[:, 0, :], MUL).then_inc(cnt.up(dve_done), 1)
                    dve.wait_ge(cnt.sem, cnt.value)
                    step = slice(None) if d == 0 else slice(None, None, -1)
                    dve.tensor_tensor_scan(A(50 + d)[:, 0, step], rg_a(d)[:, step], i[:, step], 0.0,
                                                  MUL, ADD).then_inc(cnt.up(gated_ready if d else dve_done), 1)
                dve.wait_ge(cnt.sem, cnt.value)
                tt(A(50)[:, 0, :], A(50)[:, 0, :], A(51)[:, 0, :], ADD).then_inc(cnt.up(dve_done), 1)
                dve.wait_ge(cnt.sem, cnt.value)
                tt(A(m)[:, 0, :], A(50)[:, 0, :], A(21 + m % 2)[:, 0, :], MUL).then_inc(cnt.up(mix_even_ready), 1)

            for m in range(DT):
                ua = A(19 + m % 2)[:, 0, :]
                prepare(f"even_xa_za{m}")
                dve.wait_ge(*taken(("xa", m)))
                ts(ua, xa[:, 0:T], pr("conv_w", m), pr("conv_b", m), MUL, ADD).then_inc(cnt.up(dve_done), 1)
                for k in range(1, 4):
                    dve.wait_ge(cnt.sem, cnt.value)
                    stt(ua, xa[:, k:k + T], pr("conv_w", k * DT + m), ua, MUL, ADD).then_inc(cnt.up(conv_ready if k == 3 else dve_done), 1)
                c, yb = A(24)[:, 0, :], A(DT + m)[:, 0, :]
                prepare(f"even_xb_gc{m}")
                dve.wait_ge(psum_ready, finished(("gc", m)))
                b = bank(("gc", m))
                dve.wait_ge(*taken(("xb", m)))
                tt(xg[:, 1:1 + T], b[:, :], A(23)[:, 0, :], MUL).then_inc(cnt.up(dve_released), 1)
                dve.wait_ge(cnt.sem, cnt.value)
                ts(c, xg[:, 0:T], pr("sc_w", m), None, MUL).then_inc(cnt.up(dve_done), 1)
                for k in range(1, 3):
                    dve.wait_ge(cnt.sem, cnt.value)
                    stt(c, xg[:, k:k + T], pr("sc_w", k * DT + m), c, MUL, ADD).then_inc(cnt.up(dve_done), 1)
                dve.wait_ge(cnt.sem, cnt.value)
                prepare(f"even_gb_zb{m}")
                gated(m)
                dve.wait_ge(psum_ready, finished(("gb", m)))
                b = bank(("gb", m))
                tt(yb, b[:, :], c, MUL).then_inc(cnt.up(dve_released), 1)
                dve.wait_ge(cnt.sem, cnt.value)
                dve.wait_ge(*taken(("zb", m)))
                tt(yb, yb, A(25)[:, 0, :], MUL).then_inc(cnt.up(silu_used), 1)
            for k in EVEN_ORDER:
                low(k, A(k)[:, 0, :], HN_HIGH + k)

            def post_norm(tag, gain, signal, slab_of, base):
                sum_squares(lambda m: prepare(slab_of(m)))
                invert(("ss", tag), 52)
                scaled = []
                for m in range(DT + 1):
                    if m < DT:
                        y = A(base + m)[:, 0, :]
                        stt(y, y, pr(gain, m), A(52)[:, 0, :], MUL, MUL).then_inc(cnt.up(dve_done), 1)
                        scaled.append(cnt.value)
                    if m:
                        dve.wait_ge(dve_done, scaled[m - 1])
                        tt(h[:, m - 1, :], h[:, m - 1, :], A(base + m - 1)[:, 0, :], ADD).then_inc(cnt.up(signal), 1)

            post_norm("even_post", "even_post", residual_ready, lambda m: f"even_out{m}", 16)
            norm("odd", lambda m: pr("odd_pre", m))
            for m in range(4):
                prepare(f"odd_qk{m}")
            prepare("odd_lr")

            def gla_inputs(hd):
                for d in range(2):
                    dve.wait_ge(psum_ready, finished(("gz", hd, d)))
                    b = bank(("gz", hd, d))
                    g, z = gla_t(hd, d, 0), gla_t(hd, d, 1)
                    ts(g, b[:, :], pr("b_gate", d * GLA_H + hd), 0.0, ADD, MIN).then_inc(cnt.up(dve_done), 1)
                    ts(z, b[:, :], pr("b_gate", d * GLA_H + hd), 0.0, ADD, MAX).then_inc(cnt.up(dve_released), 1)
                    dve.wait_ge(cnt.sem, cnt.value)
                    tt(z, z, g, SUB).then_inc(cnt.up(gla_min_ready), 1)

            def gla_cum(hd):
                for d in range(2):
                    dve.wait_ge(gla_log_ready, cnt.next(gla_log_ready))
                    g, z, cum = gla_t(hd, d, 0), gla_t(hd, d, 1), gla_t(hd, d, 2)
                    tt(cum, g, z, SUB).then_inc(cnt.up(dve_done), 1)
                    dve.wait_ge(cnt.sem, cnt.value)
                    step = slice(None) if d == 0 else slice(None, None, -1)
                    dve.tensor_tensor_scan(g[:, step], cst("carry"), cum[:, step], 0.0, MUL, ADD).then_inc(cnt.up(gla_cum_ready), 1)

            def gla_decayed(hd):
                for d in range(2):
                    dve.wait_ge(gla_exps_ready, cnt.next(gla_exps_ready))
                    kst, q, k = (gla_t(hd, d, i) for i in range(3))
                    dve.wait_ge(*taken(("qk", 7)))
                    tt(q, q, A(hd)[:, 0, :], MUL).then_inc(cnt.up(dve_done), 1)
                    tt(k, k, A(4 + hd)[:, 0, :], MUL).then_inc(cnt.up(dve_done), 1)
                    dve.wait_ge(cnt.sem, cnt.value)
                    end = gla_dec[:, hd % 3, d, :, None].broadcast_to((P, NC, GLA_CHUNK))
                    ch = lambda ap: ap.rearrange("p (c t) -> p c t", t=GLA_CHUNK)
                    tt(ch(kst), ch(k), end, MUL).then_inc(cnt.up(gla_inputs_ready if d else dve_done), 1)

            def bc4(name):
                return cst(name)[:, None, :].broadcast_to((P, NT, P))

            def gla_states(hd):
                f4 = lambda ap: ap.rearrange("p (j t) -> p j t", t=P)
                pt = A(GLA_PT + hd % 2)[:, 0, :]
                backward = A(47)[:, 0, :] if hd == 3 else ring_tile(ring_high_plain, 6)
                if hd == 0:
                    dve.wait_ge(psum_ready, finished(("gr", 7)))
                dve.wait_ge(psum_ready, finished(("gs", hd, 0)))
                b = bank(("gs", hd, 0))
                tt(f4(pt), f4(b[:, :]), bc4("upper"), MUL).then_inc(cnt.up(dve_released), 1)
                dve.wait_ge(psum_ready, finished(("gs", hd, 1)))
                b = bank(("gs", hd, 1))
                tt(f4(backward), f4(b[:, :]), bc4("lower"), MUL).then_inc(cnt.up(dve_released), 1)
                dve.wait_ge(cnt.sem, cnt.value)
                tt(pt, pt, backward, ADD).then_inc(cnt.up(gla_pt_ready), 1)
                for parts in (GLA_PARTS[0:2], GLA_PARTS[2:4]):
                    kv = {}
                    for steps in parts:
                        for d in range(2):
                            dve.wait_ge(psum_ready, finished(("gkv", hd, d, steps)))
                            b = bank(("gkv", hd, d, steps))
                            for i, step in enumerate(steps):
                                kv[d, step] = b[:, i * 256:(i + 1) * 256], step == steps[-1]
                    for step in sorted({step for steps in parts for step in steps}):
                        dve.wait_ge(cnt.sem, cnt.value)
                        for d in range(2):
                            c = step if d == 0 else NC - 1 - step
                            fresh, last = kv[d, step]
                            new = gla_state(hd, d, step + 1)
                            if step:
                                ins = stt(new, gla_state(hd, d, step), gla_dec[:, hd % 3, d, c:c + 1], fresh, MUL, ADD)
                            else:
                                ins = cp(new, fresh)
                            if last:
                                ins.then_inc(cnt.up(dve_released), 1)
                            else:
                                ins.then_inc(cnt.up(dve_done), 1)
                dve.wait_ge(cnt.sem, cnt.value)

            def gla_gated(hd):
                invert(("gss", hd), GLA_DEV)
                for eh in range(2):
                    o = A(GLA_O + eh)[:, 0, :]
                    stt(o, o, pr("gla_norm", eh), A(GLA_DEV)[:, 0, :], MUL, MUL).then_inc(cnt.up(dve_done), 1)
                dve.wait_ge(cnt.sem, cnt.value)
                for eh in range(2):
                    m = 2 * hd + eh
                    tt(A(gla_mix(m))[:, 0, :], A(GLA_O + eh)[:, 0, :], A(16 + m)[:, 0, :], MUL).then_inc(cnt.up(gla_mix_ready if eh else dve_done), 1)
                dve.wait_ge(cnt.sem, cnt.value)
                cp(stat[:, 0, 0:1], stat[:, 1, 0:1]).then_inc(cnt.up(gla_o_used), 1)

            def gla_lows(hd):
                for m in (2 * hd, 2 * hd + 1):
                    low(gla_mix(m), A(gla_mix(m))[:, 0, :], 16 + m)

            for n in range(4):
                prepare(f"odd_v{n}")
                if n % 2 == 0:
                    gla_inputs(n // 2)
                    gla_cum(n // 2)
                else:
                    gla_decayed(n // 2)
            for m in range(3):
                prepare(f"odd_r{m}")
            gla_states(0)
            gla_inputs(2)
            gla_states(1)
            gla_cum(2)
            gla_decayed(2)
            dve.wait_ge(psum_ready, finished(("go", 0, 1)))
            gla_inputs(3)
            gla_gated(0)
            gla_states(2)
            gla_cum(3)
            gla_decayed(3)
            gla_gated(1)
            gla_lows(0)
            gla_states(3)
            gla_gated(2)
            gla_lows(1)
            prepare("odd_out0")
            gla_lows(2)
            gla_gated(3)
            gla_lows(3)
            post_norm("odd_post", "odd_post", output_ready, lambda m: f"odd_out{m // 2}", 8)

        @block.gpsimd
        def _(pool):
            cnt = Count()
            pool.wait_ge(con_loaded, 16)
            for l in range(DEPTH):
                pool.wait_ge(krope_ready, cnt.next(krope_ready))
                pool.wait_ge(psum_ready, finished(("rv", l, 1)))
                src = A(30)[64:96]
                pool.tensor_copy(A(31, 8)[64:96], src.broadcast_to((32, 8, T))).then_inc(cnt.up(krope_spread), 1)
                pool.wait_ge(cnt.sem, cnt.value)
                v, first, gate = A(14, 2), A(8, 2), A(0, 2)
                pool.wait_ge(shifted_ready, cnt.next(shifted_ready))
                if l:
                    pool.tensor_tensor(first, first, v, ALU.subtract).then_inc(cnt.up(pool_done), 1)
                    pool.wait_ge(*taken(("vgate", l, 1)))
                    pool.wait_ge(cnt.sem, cnt.value)
                    pool.tensor_tensor(first, first, gate, ALU.mult).then_inc(cnt.up(pool_done), 1)
                    pool.wait_ge(cnt.sem, cnt.value)
                    pool.tensor_tensor(v, v, first, ALU.add).then_inc(cnt.up(values_ready), 1)
                else:
                    pool.tensor_copy(first, v).then_inc(cnt.up(values_ready), 1)
                pool.wait_ge(cnt.sem, cnt.value)
                pool.wait_ge(decays_ready, cnt.next(decays_ready, 4))
                pool.wait_ge(bonus_product_ready, cnt.next(bonus_product_ready))
                pool.tensor_tensor(A(12, 2), A(12, 2), A(35, 2), ALU.mult).then_inc(cnt.up(k_decayed), 1)
                pool.wait_ge(r_decayed, cnt.next(r_decayed))
                pool.wait_ge(cnt.sem, cnt.value)
                chunked = lambda t: A(t, 2).rearrange("p a (c t) -> p (a c) t", t=RW_CHUNK)
                end = decay_end[:, :, :].rearrange("p a c -> p (a c)")[:, :, None].broadcast_to((P, 2 * NC, RW_CHUNK))
                pool.tensor_tensor(chunked(27), chunked(12), end, ALU.mult).then_inc(cnt.up(k_carried), 1)
                pool.wait_ge(cnt.sem, cnt.value)
                for hp in range(2):
                    pool.wait_ge(*taken(("L", l, hp, 1)))
                    for n, b in enumerate(LEVELS):
                        if n:
                            pool.wait_ge(psum_ready, finished(("T1", l, hp, n - 1, 1)))
                        mask = cst(f"lower_off{b}")[:, None, :].broadcast_to((P, 2 * NT, P))
                        pool.tensor_tensor(A(19, 2).rearrange("p e (j t) -> p (e j) t", t=P),
                                                  A(17, 2).rearrange("p e (j t) -> p (e j) t", t=P), mask,
                                                  ALU.mult).then_inc(cnt.up(lower_off_ready), 1)

        @block.sync
        def _(sp):
            cnt = Count()
            sp.dma_start(h[:, 0:2, :], x_in[:, 0:2, :]).then_inc(x_loaded[0], 16)
            sp.dma_start(par[:, :], par_in).then_inc(par_loaded, 16)
            for n in range(1, 4):
                sp.dma_start(h[:, 2 * n:2 * n + 2, :], x_in[:, 2 * n:2 * n + 2, :]).then_inc(x_loaded[n], 16)
            sp.dma_start(con[:, 0:FIRST_CON], con_in[:, 0:FIRST_CON]).then_inc(ones_loaded, 16)
            at = 0
            for n, (name, cols) in enumerate(plan):
                if n >= SLOTS:
                    before = plan[n - SLOTS][0]
                    if is_split(before):
                        sp.wait_ge(slab_split, split_index[before] + 1)
                    else:
                        sp.wait_ge(psum_ready, slab_group[n - SLOTS] + 1)
                src = slabs_in[at:at + P * cols].rearrange("(p n) -> p n", p=P)
                sp.dma_start(ring[:, n % SLOTS, 0:cols], src).then_inc(slab_loaded[n % SLOTS], 16)
                at += P * cols
                if n == 1:
                    sp.dma_start(A(0)[:, 0, :].bitcast(I32), pos_in).then_inc(pos_loaded, 16)
                if n == 2:
                    sp.dma_start(con[:, FIRST_CON:], con_in[:, FIRST_CON:]).then_inc(con_loaded, 16)
                    sp.dma_start(small[:, :], small_in).then_inc(small_loaded, 16)
                if name == "even_xb_gc0":
                    sp.wait_ge(psum_ready, finished(("down", DEPTH - 1, DT - 1, 1)))
                    sp.dma_start(A(0, 2), gates_in[:, 0:2]).then_inc(first_gates_loaded, 16)
                if name == "even_xb_gc1":
                    sp.dma_start(A(2, DT - 2), gates_in[:, 2:]).then_inc(gates_loaded, 16)
            for m in range(0, DT, 2):
                sp.wait_ge(output_ready, cnt.next(output_ready, 2))
                sp.dma_start(out[:, m:m + 2, :], h[:, m:m + 2, :]).then_inc(stored, 16)
            sp.wait_ge(stored, 16 * (DT // 2))


def kernel(**inputs):
    import concourse.bacc as bacc
    from concourse.bass_utils import run_bass_kernel_spmd

    x = {k: np.asarray(v) for k, v in inputs.items()}
    arrays = {
        "x_in": np.ascontiguousarray(x["x"][0].T.reshape(DT, P, T).transpose(1, 0, 2)),
        "pos_in": np.ascontiguousarray(np.broadcast_to(x["positions"].reshape(1, T), (P, T))),
        "slabs_in": pack_slabs(x),
        "par_in": pack_params(x),
        "small_in": pack_small(x),
        "gates_in": pack_gates(x),
        "con_in": constants(),
    }
    nc = bacc.Bacc("TRN2", target_bir_lowering=False, num_devices=1)
    args = [nc.dram_tensor(k, a.shape, mybir.dt.from_np(a.dtype), kind="ExternalInput").ap() for k, a in arrays.items()]
    out = nc.dram_tensor("out", (P, DT, T), F32, kind="ExternalOutput").ap()
    two_blocks(nc, *args, out)
    r = run_bass_kernel_spmd(nc, [arrays], core_ids=[0])
    y = r.results[0]["out"]
    return y.transpose(1, 0, 2).reshape(1, D, T).transpose(0, 2, 1)
```
